# Optimizing a Trainium2 kernel written in Bass

```python
import jax
import jax.numpy as jnp
from jax import lax
import numpy as np

D_MODEL = 1024
BATCH = 1
SEQ = 512
DEPTH = 2

A_HEAD_DIM = 64
A_WIDTH = D_MODEL // 2
A_HEADS = A_WIDTH // A_HEAD_DIM
MOBA_BLOCK = 256
MOBA_TOPK = 3
MOBA_Q_CHUNK = 32
B_WIDTH = D_MODEL // 2
B_HEADS = 4
B_HEAD_DIM = B_WIDTH // B_HEADS
B_QKV_BLOCK = 4
B_CONV = 4
MLSTM_CHUNK = 64
C_WIDTH = D_MODEL
C_GROUPS = 8
C_CHUNK = 128
IN_WIDTH = 4 * A_WIDTH + 2 * B_WIDTH
MIX_WIDTH = A_WIDTH + B_WIDTH
N_EVEN = (DEPTH + 1) // 2
N_ODD = DEPTH // 2
NEG = -1e30

kernel_name = "hybrid_moba_mlstm_gmlp_block"

def _rms_norm(x, g, eps=1e-6):
    xf = x.astype(jnp.float32)
    y = xf * lax.rsqrt(jnp.mean(xf * xf, axis=-1, keepdims=True) + eps)
    return (y * g.astype(jnp.float32)).astype(x.dtype)

def _layer_norm(x, eps=1e-5):
    xf = x.astype(jnp.float32)
    mu = jnp.mean(xf, axis=-1, keepdims=True)
    var = jnp.mean(jnp.square(xf - mu), axis=-1, keepdims=True)
    return (xf - mu) * lax.rsqrt(var + eps)

def _heads(t, n):
    b, s, _ = t.shape
    return t.reshape(b, s, n, -1).transpose(0, 2, 1, 3)

def _merge(t):
    b, h, s, d = t.shape
    return t.transpose(0, 2, 1, 3).reshape(b, s, h * d)

def _moba(q, k, v):
    b, h, s, dh = q.shape
    nb = -(-s // MOBA_BLOCK)
    pad = nb * MOBA_BLOCK - s
    kp = jnp.pad(k, ((0, 0), (0, 0), (0, pad), (0, 0)))
    vp = jnp.pad(v, ((0, 0), (0, 0), (0, pad), (0, 0)))
    kb = kp.reshape(b, h, nb, MOBA_BLOCK, dh)
    vb = vp.reshape(b, h, nb, MOBA_BLOCK, dh)
    kmean = jnp.mean(kb.astype(jnp.float32), axis=3)
    qblk = jnp.arange(s) // MOBA_BLOCK
    score = jnp.einsum('bhsd,bhnd->bhsn', q.astype(jnp.float32), kmean)
    past = jnp.arange(nb)[None, :] < qblk[:, None]
    score = jnp.where(past, score, NEG)
    topk = min(MOBA_TOPK, nb)
    _, idx = lax.top_k(score, topk)
    valid = idx < qblk[:, None]
    nq = s // MOBA_Q_CHUNK

    def chunks(t):
        return jnp.moveaxis(t.reshape(b, h, nq, MOBA_Q_CHUNK, *t.shape[3:]), 2, 0)

    gather = jax.vmap(jax.vmap(lambda blocks, ix: blocks[ix]))
    scale = dh ** -0.5

    def step(args):
        qc, ic, vmask, cid = args
        q0 = cid * MOBA_Q_CHUNK
        j = q0 // MOBA_BLOCK
        qpos = q0 + jnp.arange(MOBA_Q_CHUNK)
        k_sel = gather(kb, ic)
        v_sel = gather(vb, ic)
        k_own = lax.dynamic_slice_in_dim(kp, j * MOBA_BLOCK, MOBA_BLOCK, axis=2)
        v_own = lax.dynamic_slice_in_dim(vp, j * MOBA_BLOCK, MOBA_BLOCK, axis=2)
        l_sel = jnp.einsum('bhqd,bhqtkd->bhqtk', qc, k_sel).astype(jnp.float32) * scale
        l_sel = jnp.where(vmask[..., None], l_sel, NEG).reshape(b, h, MOBA_Q_CHUNK, topk * MOBA_BLOCK)
        kpos = j * MOBA_BLOCK + jnp.arange(MOBA_BLOCK)
        l_own = jnp.einsum('bhqd,bhkd->bhqk', qc, k_own).astype(jnp.float32) * scale
        l_own = jnp.where(kpos[None, :] <= qpos[:, None], l_own, NEG)
        p = jax.nn.softmax(jnp.concatenate([l_sel, l_own], axis=-1), axis=-1).astype(v.dtype)
        p_sel = p[..., :topk * MOBA_BLOCK].reshape(b, h, MOBA_Q_CHUNK, topk, MOBA_BLOCK)
        p_own = p[..., topk * MOBA_BLOCK:]
        return (jnp.einsum('bhqtk,bhqtkd->bhqd', p_sel, v_sel)
                + jnp.einsum('bhqk,bhkd->bhqd', p_own, v_own))

    out = lax.map(step, (chunks(q), chunks(idx), chunks(valid), jnp.arange(nq)))
    return jnp.moveaxis(out, 0, 2).reshape(b, h, s, dh)

def _mlstm(q, k, v, ig, fg):
    dtype = q.dtype
    b, h, s, dh = q.shape
    L = MLSTM_CHUNK
    nc = s // L
    q = q.astype(jnp.float32)
    k = k.astype(jnp.float32) * (dh ** -0.5)
    v = v.astype(jnp.float32)
    ig = ig.astype(jnp.float32)
    lf = jax.nn.log_sigmoid(fg.astype(jnp.float32))

    def chunks(t):
        return jnp.moveaxis(t.reshape(b, h, nc, L, *t.shape[3:]), 2, 0)

    tri = jnp.tril(jnp.ones((L, L), dtype=bool))

    def step(carry, xs):
        C, n, m = carry
        qc, kc, vc, ic, lc = xs
        cum = jnp.cumsum(lc, axis=-1)
        tot = cum[..., -1]
        dmat = jnp.where(tri, cum[..., :, None] - cum[..., None, :] + ic[..., None, :], NEG)
        g = cum + m[..., None]
        m_t = jnp.maximum(g, jnp.max(dmat, axis=-1))
        w_intra = jnp.einsum('bhtd,bhsd->bhts', qc, kc) * jnp.exp(dmat - m_t[..., None])
        w_inter = jnp.exp(g - m_t)
        num = (w_inter[..., None] * jnp.einsum('bhvk,bhtk->bhtv', C, qc)
               + jnp.einsum('bhts,bhsv->bhtv', w_intra, vc))
        den = w_inter * jnp.einsum('bhk,bhtk->bht', n, qc) + jnp.sum(w_intra, axis=-1)
        hc = num / jnp.maximum(jnp.abs(den), jnp.exp(-m_t))[..., None]
        w_state = tot[..., None] - cum + ic
        m_new = jnp.maximum(tot + m, jnp.max(w_state, axis=-1))
        decay = jnp.exp(tot + m - m_new)
        ws = jnp.exp(w_state - m_new[..., None])
        C = decay[..., None, None] * C + jnp.einsum('bhs,bhsv,bhsk->bhvk', ws, vc, kc)
        n = decay[..., None] * n + jnp.einsum('bhs,bhsk->bhk', ws, kc)
        return (C, n, m_new), hc

    init = (jnp.zeros((b, h, dh, dh), jnp.float32), jnp.zeros((b, h, dh), jnp.float32),
            jnp.zeros((b, h), jnp.float32))
    _, hs = lax.scan(step, init, (chunks(q), chunks(k), chunks(v), chunks(ig), chunks(lf)))
    return jnp.moveaxis(hs, 0, 2).reshape(b, h, s, dh).astype(dtype)

def _causal_conv(x, w, bias):
    ch = x.shape[-1]
    y = lax.conv_general_dilated(x, w[:, None, :].astype(x.dtype), window_strides=(1,),
                                 padding=[(B_CONV - 1, 0)], dimension_numbers=('NWC', 'WIO', 'NWC'),
                                 feature_group_count=ch)
    return y + bias

def _headwise(x, w):
    b, s, d = x.shape
    nblk, blk, _ = w.shape
    return jnp.einsum('bsgi,gio->bsgo', x.reshape(b, s, nblk, blk), w).reshape(b, s, d)

def _even_mixer(h, w_in, w_out, q_g, k_g, conv_w, conv_b, wq, wk, wv, w_gates, b_gates, out_g, skip):
    proj = h @ w_in
    aq, ak, av, az, bx, bz = jnp.split(
        proj, [A_WIDTH, 2 * A_WIDTH, 3 * A_WIDTH, 4 * A_WIDTH, 4 * A_WIDTH + B_WIDTH], axis=-1)
    q = _rms_norm(_heads(aq, A_HEADS), q_g)
    k = _rms_norm(_heads(ak, A_HEADS), k_g)
    ya = _merge(_moba(q, k, _heads(av, A_HEADS))) * jax.nn.silu(az)
    xc = jax.nn.silu(_causal_conv(bx, conv_w, conv_b))
    bq = _headwise(xc, wq)
    bk = _headwise(xc, wk)
    bv = _headwise(bx, wv)
    gates = jnp.concatenate([bq, bk, bv], axis=-1) @ w_gates + b_gates
    ig = gates[..., :B_HEADS].transpose(0, 2, 1)
    fg = gates[..., B_HEADS:].transpose(0, 2, 1)
    hb = _mlstm(_heads(bq, B_HEADS), _heads(bk, B_HEADS), _heads(bv, B_HEADS), ig, fg)
    hb = _merge(_layer_norm(hb).astype(h.dtype)) * out_g
    yb = (hb + skip * xc) * jax.nn.silu(bz)
    return jnp.concatenate([ya, yb], axis=-1) @ w_out

def _odd_mixer(h, w_in, w_out, ln_g, ln_b, ws, bs):
    b, s, _ = h.shape
    u, v, z = jnp.split(h @ w_in, [C_WIDTH, 2 * C_WIDTH], axis=-1)
    u = jax.nn.gelu(u)
    v = (_layer_norm(jax.nn.gelu(v)) * ln_g + ln_b).astype(h.dtype)
    nch = s // C_CHUNK
    vg = v.reshape(b, nch, C_CHUNK, C_GROUPS, C_WIDTH // C_GROUPS)
    wm = jnp.where(jnp.tril(jnp.ones((C_CHUNK, C_CHUNK), dtype=bool)), ws, 0.0)
    sg = jnp.einsum('gts,bnsgc->bntgc', wm, vg) + bs.T[:, :, None]
    y = u * sg.reshape(b, s, C_WIDTH) * jax.nn.silu(z)
    return y @ w_out

def setup_inputs(seed: int = 0) -> dict:
    key = jax.random.key(seed)
    ks = jax.random.split(key, 24)

    def nrm(k, shape, sc):
        return jax.random.normal(k, shape, jnp.float32) * sc

    nblk = B_WIDTH // B_QKV_BLOCK
    i_bias = nrm(ks[15], (N_EVEN, B_HEADS), 0.1)
    f_bias = jnp.linspace(3.0, 6.0, B_HEADS, dtype=jnp.float32)[None, :] + nrm(ks[16], (N_EVEN, B_HEADS), 0.1)
    return {
        "x": nrm(ks[0], (BATCH, SEQ, D_MODEL), 1.0),
        "c": nrm(ks[1], (BATCH, D_MODEL), 1.0),
        "ln_g": 1.0 + nrm(ks[2], (DEPTH, D_MODEL), 0.1),
        "ada_w": nrm(ks[3], (DEPTH, D_MODEL, 3 * D_MODEL), 0.5 * D_MODEL ** -0.5),
        "ada_b": nrm(ks[4], (DEPTH, 3 * D_MODEL), 0.02),
        "w_in": nrm(ks[5], (DEPTH, D_MODEL, IN_WIDTH), D_MODEL ** -0.5),
        "w_out": nrm(ks[6], (DEPTH, MIX_WIDTH, D_MODEL), MIX_WIDTH ** -0.5),
        "a_q_g": 1.0 + nrm(ks[7], (N_EVEN, A_HEAD_DIM), 0.1),
        "a_k_g": 1.0 + nrm(ks[8], (N_EVEN, A_HEAD_DIM), 0.1),
        "b_conv_w": nrm(ks[9], (N_EVEN, B_CONV, B_WIDTH), B_CONV ** -0.5),
        "b_conv_b": nrm(ks[10], (N_EVEN, B_WIDTH), 0.02),
        "b_wq": nrm(ks[11], (N_EVEN, nblk, B_QKV_BLOCK, B_QKV_BLOCK), B_QKV_BLOCK ** -0.5),
        "b_wk": nrm(ks[12], (N_EVEN, nblk, B_QKV_BLOCK, B_QKV_BLOCK), B_QKV_BLOCK ** -0.5),
        "b_wv": nrm(ks[13], (N_EVEN, nblk, B_QKV_BLOCK, B_QKV_BLOCK), B_QKV_BLOCK ** -0.5),
        "b_w_gates": nrm(ks[14], (N_EVEN, 3 * B_WIDTH, 2 * B_HEADS), (3 * B_WIDTH) ** -0.5),
        "b_b_gates": jnp.concatenate([i_bias, f_bias], axis=-1),
        "b_out_g": 1.0 + nrm(ks[17], (N_EVEN, B_WIDTH), 0.1),
        "b_skip": 1.0 + nrm(ks[18], (N_EVEN, B_WIDTH), 0.1),
        "c_ln_g": 1.0 + nrm(ks[19], (N_ODD, C_WIDTH), 0.1),
        "c_ln_b": nrm(ks[20], (N_ODD, C_WIDTH), 0.02),
        "c_ws": nrm(ks[21], (N_ODD, C_GROUPS, C_CHUNK, C_CHUNK), C_CHUNK ** -0.5),
        "c_bs": 1.0 + nrm(ks[22], (N_ODD, C_GROUPS, C_CHUNK), 0.1),
    }

def reference(x, c, ln_g, ada_w, ada_b, w_in, w_out, a_q_g, a_k_g, b_conv_w, b_conv_b, b_wq, b_wk,
              b_wv, b_w_gates, b_b_gates, b_out_g, b_skip, c_ln_g, c_ln_b, c_ws, c_bs):
    cs = jax.nn.silu(c)
    for layer in range(DEPTH):
        mod = cs @ ada_w[layer] + ada_b[layer]
        shift, scale, gate = jnp.split(mod, 3, axis=-1)
        h = _rms_norm(x, ln_g[layer]) * (1.0 + scale[:, None, :]) + shift[:, None, :]
        if layer % 2 == 0:
            e = layer // 2
            y = _even_mixer(h, w_in[layer], w_out[layer], a_q_g[e], a_k_g[e], b_conv_w[e], b_conv_b[e],
                            b_wq[e], b_wk[e], b_wv[e], b_w_gates[e], b_b_gates[e], b_out_g[e], b_skip[e])
        else:
            o = layer // 2
            y = _odd_mixer(h, w_in[layer], w_out[layer], c_ln_g[o], c_ln_b[o], c_ws[o], c_bs[o])
        x = x + gate[:, None, :] * y
    return x


_drawn_inputs = setup_inputs


def setup_inputs(seed=0):
    import zlib

    import numpy as np

    out = dict(_drawn_inputs(seed))
    spreads = {}
    factors = {'a_q_g': 8.0,
     'a_k_g': 8.0,
     'b_conv_b': 8.0,
     'b_out_g': 3.857,
     'b_skip': 6.013,
     'c_ln_g': 5.084,
     'c_ln_b': 39.653,
     'c_bs': 3.663}
    for name, (base, spread) in spreads.items():
        noise = np.random.default_rng([zlib.crc32(name.encode()), seed]).standard_normal(out[name].shape)
        drawn = base * np.exp(spread * noise) if base else spread * noise
        out[name] = jnp.asarray(drawn.astype(out[name].dtype))
    for name, factor in factors.items():
        out[name] = (out[name] * factor).astype(out[name].dtype)
    return out
```

```python
from contextlib import ExitStack

import concourse.bass as bass
from concourse import mybir

F32 = mybir.dt.float32
F32R = mybir.dt.float32r
BF16 = mybir.dt.bfloat16
ALU = mybir.AluOpType
ACT = mybir.ActivationFunctionType
AX_X = mybir.AxisListType.X

P = 128
D = 1024
T = 512
KT = D // P
NT = T // P
CH = 512
KH = 4
AH = 8
DA = 64
MH = 4
VP = 130
NEG = -1e30
RAW = 3
SPLIT = 2
LNEXP = "natural_log_exp_and_others"

CHUNKS = [
    ("in", 0, 4, (0, 1), "feature", "bx"), ("in", 0, 3, (0, 1), "feature", "az"),
    ("in", 0, 5, (0, 1), "feature", "bz"), ("in", 0, 0, (0, 1), "token", "aq"),
    ("in", 0, 1, (0, 1), "token", "ak"), ("in", 0, 2, (0, 1), "token", "av"),
    ("out", 0, 0, (1, 0), "token", "y0"), ("out", 0, 1, (1, 0), "token", "y0"),
    ("in", 1, 2, (0, 1), "token", "cv"), ("in", 1, 3, (0, 1), "token", "cv"),
    ("in", 1, 0, (0, 1), "feature", "cu"), ("in", 1, 1, (0, 1), "feature", "cu"),
    ("in", 1, 4, (0, 1), "feature", "cz"), ("in", 1, 5, (0, 1), "feature", "cz"),
    ("out", 1, 0, (0, 1), "token", "y1"), ("out", 1, 1, (0, 1), "token", "y1"),
]
HALVES = [(c, kh) for c in range(len(CHUNKS)) for kh in CHUNKS[c][3]]
NHALF = len(HALVES)
ADA_FIRST = [(0, 2), (0, 3), (0, 0), (0, 1)]
ADA_LATER = [(0, 4), (0, 5), (1, 2), (1, 3), (1, 0), (1, 1), (1, 4), (1, 5)]
ADA = ADA_FIRST + ADA_LATER
GATE_ITEMS = [n for n, (_, cc) in enumerate(ADA) if cc >= 4]
MOD_ITEMS = [n for n, (_, cc) in enumerate(ADA) if cc < 4]
ADA_SLOT = {n: (2 * (n - 4), 1) for n in range(4, 12)} | {10: (13, 0), 11: (14, 1)}
ADA_USE_SLOT = {n: (s, g + 1) for n, (s, g) in ADA_SLOT.items()} | {10: (16, 2), 11: (17, 2)}


def plan_stream():
    stream = [("ada", n) for n in range(2 * len(ADA_FIRST))]
    ada = 2 * len(ADA_FIRST)
    for w in range(NHALF):
        stream.append(("w", w))
        if w % 2 == 1 and ada < 2 * len(ADA):
            stream += [("ada", ada), ("ada", ada + 1)]
            ada += 2
    return stream


STREAM = plan_stream()
PLACE = {item: n for n, item in enumerate(STREAM)}

ROWS = {}
for _name, _rows in (("ada_b", 48), ("ln_g", 16), ("c", 8), ("conv_w", 16), ("conv_b", 4), ("out_g", 4),
                     ("skip", 4), ("c_ln_g", 8), ("q_g", 1), ("k_g", 1)):
    ROWS[_name] = (sum(r for _, r in ROWS.values()), _rows)
NROWS = sum(r for _, r in ROWS.values())

UNITS = [(2 * p + e, i, e) for p in range(AH // 2) for i in range(NT) for e in range(2)]
NU = len(UNITS)
S_ORDER = (0, 1, 3, 2)
PAD = 256


def PT_ON_ACT(u):
    return UNITS[u][1] == 3


LAG = 2
ATT_SLOTS = {}
_u = 0
for _slot, _n in [((11, g), 2) for g in range(4)] + [((12, -1), 4), ((12, 0), 6), ((12, 1), 6), ((12, 2), 6)]:
    ATT_SLOTS[_slot] = list(range(_u, min(_u + _n, NU + LAG)))
    _u += _n
YA_SPLIT = {8 * p + 11: p for p in range(3)} | {NU + LAG: 3}
Y_ORDER = (4, 5, 6, 7, 0, 1, 2, 3)
ATT_SLOTS[(12, 2)] = list(range(ATT_SLOTS[(12, 2)][0], NU + LAG + 1))


def build(nc, x, c, ln_g, ada_w, ada_b, w_in, w_out, a_q_g, a_k_g, b_conv_w, b_conv_b, b_wq, b_wk, b_wv,
          b_w_gates, b_b_gates, b_out_g, b_skip, c_ln_g, c_ln_b, c_ws, c_bs, out):
    with ExitStack() as ctx:
        def sb(name, shape, dt=F32):
            return ctx.enter_context(nc.sbuf_tensor(name, shape, dt))

        def sem(name):
            return ctx.enter_context(nc.semaphore(name))

        acc = [ctx.enter_context(nc.psum_tensor(f"acc{g}", [P, 512], F32)) for g in range(4)]
        work = [ctx.enter_context(nc.psum_tensor(f"work{g}", [P, 512], F32)) for g in range(4)]

        raw = sb("raw", [P, RAW, KH, CH])
        w_hi = sb("w_hi", [P, SPLIT, KH, CH], F32R)
        w_lo = sb("w_lo", [P, SPLIT, KH, CH], F32R)
        act_hi = sb("act_hi", [P, KT, T], F32R)
        act_lo = sb("act_lo", [P, KT, T], F32R)
        act = sb("act", [P, KT, T])
        xres = sb("xres", [P, NT, D])
        mid = sb("mid", [P, 4160])
        xc = sb("xc", [P, MH, T])
        conv = sb("conv", [P, MH, T])
        vals = sb("vals", [P, NT * MH * VP])
        num = sb("num", [P, NT * MH, VP])
        wts = sb("wts", [P, 1280])
        probs = sb("probs", [P, 3, T])
        gate_bc = sb("gate_bc", [P, D])
        ada_row = sb("ada_row", [P, 2, CH])
        ident = sb("ident", [P, P])
        ident_bf = sb("ident_bf", [P, P], BF16)
        causal_bf = sb("causal_bf", [P, P], BF16)
        upper = sb("upper", [P, P])
        ones = sb("ones", [P, P])
        head_sel = sb("head_sel", [P, MH, P])
        gate_sel = sb("gate_sel", [P, 8])
        cols = sb("cols", [P, NROWS])
        c_pad = sb("c_pad", [P, KT, 32])
        mod = sb("mod", [P, 2, 16])
        gain = sb("gain", [P, 2, 8])
        bg_bc = sb("bg_bc", [P, 8])
        wm = sb("wm", [P, 8, P])
        sg_add = sb("sg_add", [P, 8, P])
        neg_m = sb("neg_m", [P, T])
        rms = sb("rms", [P, 4, 8])
        gt = sb("gt", [P, 12, 16])
        pre = sb("pre", [P, NT, 4])
        st6 = sb("st6", [P, 16, 6])
        mv2 = sb("mv2", [P, 16, 2])
        qs = sb("qs", [P, 5, 64])
        mx = sb("mx", [P, 2, NU])
        rs = sb("rs", [P, 2, NU])
        wbd = mid[:, 2064:2064 + 1536].rearrange("p (m h c) -> p m h c", m=3, h=4)
        bx = mid[:, 0:4 * 515].rearrange("p (h t) -> p h t", h=4)
        k_raw = mid[:, 0:2048].rearrange("p (t n) -> p t n", t=NT)
        q_raw = mid[:, 2064:2064 + 2048].rearrange("p (t n) -> p t n", t=NT)
        probs_t = mid[:, 0:4096].rearrange("p (e j q) -> p e j q", e=2, j=NT)
        vg = mid[:, 0:4096].rearrange("p (t n) -> p t n", t=NT)
        mq = xres[:, 0:2, :].rearrange("p a (b t) -> p (a b) t", b=2)
        mk = xres[:, 2:4, :].rearrange("p a (b t) -> p (a b) t", b=2)
        qt = xres[:, :, :].rearrange("p a (b t) -> p (a b) t", b=2)
        kt = conv
        mvals = vals[:, :].rearrange("p (t h v) -> p t h v", t=NT, h=MH)
        avals = vals[:, 0:2048].rearrange("p (t n) -> p t n", t=NT)
        wvt = wts[:, 0:512].rearrange("p (h c) -> p h c", h=4)
        ws_raw = num[:, 0:8, 0:P]
        lnb_bc = vals[:, 0:1024]
        bs_bc = gate_bc[:, :].rearrange("p (g t) -> p g t", g=8)
        expw = probs[:, :, :].rearrange("p a b -> p (a b)")
        xn = xc[:, :, :].rearrange("p (a b) t -> p a (b t)", a=2)
        gates_t = conv[:, 3, :]
        run = conv[0:4, 0:3, :].rearrange("p a t -> p (a t)").rearrange("p (b n) -> p b n", b=2)
        rows = probs[:, 2, 0:P]
        block_diag = wts[:, 512:640].rearrange("p (b o) -> p b o", o=4)
        wqkv = wts[:, 640:688].rearrange("p (m h o) -> p m h o", m=3, h=4)
        wg_pad = num[:, :, :].rearrange("p a b -> p (a b)")[:, 1040:1424].rearrange("p (b r) -> p b r", r=32)
        tmp = conv
        OFF = [0, 512, 896, 1152]

        def col(name, n, k=1):
            r = ROWS[name][0] + n
            return cols[:, r:r + k]

        raw_in = [sem(f"raw_in{s}") for s in range(RAW)]
        ada_used = sem("ada_used")
        w_hi_ready, w_lo_ready = sem("w_hi_ready"), sem("w_lo_ready")
        even_half_done, acc_ready = sem("even_half_done"), sem("acc_ready")
        acc_freed_act, acc_freed_dve = sem("acc_freed_act"), sem("acc_freed_dve")
        rows_in, x_in, small_in, ws_in, wg_in = (sem("rows_in"), [sem(f"x_in{t}") for t in range(NT)],
                                                 sem("small_in"), sem("ws_in"), sem("wg_in"))
        consts, pool_step, dve_step, act_step = sem("consts"), sem("pool_step"), sem("dve_step"), sem("act_step")
        wg_zero, pool_prep = sem("wg_zero"), sem("pool_prep")
        rows_t, cols_ready, c_ready = sem("rows_t"), sem("cols_ready"), sem("c_ready")
        ss_ready, ln_ready, xn_ready = sem("ss_ready"), sem("ln_ready"), sem("xn_ready")
        var_ready = sem("var_ready")
        xt_psum, xt_evac = sem("xt_psum"), sem("xt_evac")
        wm_psum, wm_evac, sg_psum0, sg_ready = sem("wm_psum"), sem("wm_evac"), sem("sg_psum0"), sem("sg_ready")
        ada_evac, modc_psum, mod_ready = sem("ada_evac"), sem("modc_psum"), sem("mod_ready")
        gate_b_in, gate_psum, gate_ready = sem("gate_b_in"), sem("gate_psum"), sem("gate_ready")
        h_exact, h_hi, h_ready = sem("h_exact"), sem("h_hi"), sem("h_ready")
        conv_step, xc_ready = sem("conv_step"), sem("xc_ready")
        wvt_psum, wvt_ready, eff_psum, eff_ready = (sem("wvt_psum"), sem("wvt_ready"), sem("eff_psum"),
                                                    sem("eff_ready"))
        mv_psum, mv_evac, mqk_psum, mqk_evac = sem("mv_psum"), sem("mv_evac"), sem("mqk_psum"), sem("mqk_evac")
        skip_done = sem("skip_done")
        g_psum, g_evac, gt_psum, gt_abs, gt_ln, lf_ready = (sem("g_psum"), sem("g_evac"), sem("gt_psum"),
                                                            sem("gt_abs"), sem("gt_ln"), sem("lf_ready"))
        cum_psum, a_ready, at_psum, m_rows, mc_psum, mc_ready, guard_ready = (
            sem("cum_psum"), sem("a_ready"), sem("at_psum"), sem("m_rows"), sem("mc_psum"), sem("mc_ready"),
            sem("guard_ready"))
        mb_psum, mexp, st_psum, wt_mult, wt_ready, pv_psum, num_evac = (
            sem("mb_psum"), sem("mexp"), sem("st_psum"), sem("wt_mult"), sem("wt_ready"), sem("pv_psum"),
            sem("num_evac"))
        hb_ready, hbt_psum, yb_part = sem("hb_ready"), sem("hbt_psum"), sem("yb_part")
        q_evac, k_evac, qk_ss, qk_ln, k_norm = (sem("q_evac"), sem("k_evac"), sem("qk_ss"),
                                                        sem("qk_ln"), sem("k_norm"))
        sq_used = sem("sq_used")
        qt_zero, qt_psum, kt_psum, qt_ready, kt_ready = (sem("qt_zero"), sem("qt_psum"), sem("kt_psum"),
                                                         sem("qt_ready"), sem("kt_ready"))
        s_psum, bias_ready, exp_ready, p_ready, pt_psum, pt_dve, pt_act, o_psum = (
            sem("s_psum"), sem("bias_ready"), sem("exp_ready"), sem("p_ready"), sem("pt_psum"), sem("pt_dve"),
            sem("pt_act"), sem("o_psum"))
        mvar_ready, mln_ready = sem("mvar_ready"), sem("mln_ready")
        y_exact, y_hi, y_ready = sem("y_exact"), sem("y_hi"), sem("y_ready")
        x1_ready, h1_psum, h1_exact, h1_hi, h1_ready = (sem("x1_ready"), sem("h1_psum"), sem("h1_exact"),
                                                        sem("h1_hi"), sem("h1_ready"))
        ss1_ready, var1_ready, ln1_ready, xn1_ready = (sem("ss1_ready"), sem("var1_ready"), sem("ln1_ready"),
                                                       sem("xn1_ready"))
        cv_ready, cvar_ready, cln_ready, vn_ready = (sem("cv_ready"), sem("cvar_ready"), sem("cln_ready"),
                                                     sem("vn_ready"))
        u_ready, sg_psum, us_ready, zs_ready, zs_used = (sem("u_ready"), sem("sg_psum"), sem("us_ready"),
                                                         sem("zs_ready"), sem("zs_used"))
        z1_exact, z1_hi, z1_ready = sem("z1_exact"), sem("z1_hi"), sem("z1_ready")
        out_ready, stored = sem("out_ready"), sem("stored")

        w_views = {"in": [w_in[l].rearrange("(k p) n -> p k n", p=P) for l in range(2)],
                   "out": [w_out[l].rearrange("(k p) n -> p k n", p=P) for l in range(2)]}
        ada_views = [ada_w[l].rearrange("(k p) n -> p k n", p=P) for l in range(2)]
        x_view = x[0].rearrange("(t p) d -> p t d", p=P)
        out_view = out[0].rearrange("(t p) d -> p t d", p=P)

        def landed(eng, item):
            n = PLACE[item]
            eng.wait_ge(raw_in[n % RAW], 16 * (n // RAW + 1))
            return n % RAW

        def half_done(eng, w):
            if w % 2:
                eng.wait_ge(acc_ready, 4 * (w // 2) + 4)
            else:
                eng.wait_ge(even_half_done, w // 2 + 1)

        DVE_CHUNKS = [n for n, ch in enumerate(CHUNKS) if ch[5] in ("y0", "y1")]

        def acc_free(eng, chunk, g):
            before = sum(n < chunk for n in DVE_CHUNKS)
            if chunk in DVE_CHUNKS:
                eng.wait_ge(acc_freed_dve, 4 * before + g + 1)
            else:
                eng.wait_ge(acc_freed_act, 4 * (chunk - before) + g + 1)

        def what(w):
            return CHUNKS[HALVES[w][0]][5]

        block = ctx.enter_context(nc.Block())

        @block.sync
        def _(sp):
            for n, (kind, m) in enumerate(STREAM):
                if n >= RAW:
                    before = STREAM[n - RAW]
                    if before[0] == "ada":
                        sp.wait_ge(ada_used, before[1] + 1)
                    else:
                        sp.wait_ge(w_lo_ready, before[1] + 1)
                if kind == "ada":
                    layer, cc = ADA[m // 2]
                    src = ada_views[layer][:, KH * (m % 2):KH * (m % 2) + KH, CH * cc:CH * cc + CH]
                else:
                    chunk, kh = HALVES[m]
                    mat, layer, cc = CHUNKS[chunk][:3]
                    src = w_views[mat][layer][:, KH * kh:KH * kh + KH, CH * cc:CH * cc + CH]
                    if m == 15:
                        sp.wait_ge(s_psum, NU)
                        for t in range(NT):
                            sp.dma_start(xres[:, t, :], x_view[:, t, :]).then_inc(x_in[t], 16)
                sp.dma_start(raw[:, n % RAW, :, :], src).then_inc(raw_in[n % RAW], 16)
            for cc in range(2):
                for t in range(NT):
                    sp.wait_ge(out_ready, 4 * cc + t + 1)
                    sp.dma_start(out_view[:, t, CH * cc:CH * cc + CH],
                                 xres[:, t, CH * cc:CH * cc + CH]).then_inc(stored, 16)
            sp.wait_ge(stored, 16 * 8)

        @block.gpsimd
        def _(pool):
            count = [0]

            def link(ins):
                count[0] += 1
                ins.then_inc(pool_step, 1)
                pool.wait_ge(pool_step, count[0])

            link(pool.memset(wg_pad, 0.0))
            pool.dma_start(wg_pad[:, :, 0:8], b_w_gates[0].rearrange("(b p) r -> p b r", p=P)).then_inc(wg_in, 16)
            pool.dma_start(ws_raw, c_ws[0].rearrange("g t s -> t g s")).then_inc(ws_in, 16)
            pool.dma_start(lnb_bc, c_ln_b[0:1, :].to_broadcast((P, D))).then_inc(small_in, 16)
            pool.dma_start(gate_bc[:, :], c_bs[0:1].rearrange("a g t -> a (g t)").to_broadcast((P, D))).then_inc(small_in, 16)
            pool.dma_start(bg_bc[:, :], b_b_gates[0:1, :].to_broadcast((P, 8))).then_inc(small_in, 16)
            for m, w in enumerate((b_wq, b_wk, b_wv)):
                pool.dma_start(wqkv[:, m, :, :],
                               w[0].rearrange("(h b) i o -> (b i) h o", h=4)).then_inc(small_in, 16)
            link(pool.memset(ident[:], 0.0))
            pool.affine_select(out=ident[:], in_=ident[:], compare_op=ALU.not_equal, fill=1.0, base=0,
                               pattern=[[-1, P]], channel_multiplier=1).then_inc(consts, 1)
            link(pool.memset(c_pad[:], 0.0))
            pool.memset(ones[:], 1.0).then_inc(consts, 1)
            link(pool.memset(ident_bf[:], 0.0))
            pool.affine_select(out=ident_bf[:], in_=ident_bf[:], compare_op=ALU.not_equal, fill=1.0, base=0,
                               pattern=[[-1, P]], channel_multiplier=1).then_inc(consts, 1)
            link(pool.memset(causal_bf[:], 0.0))
            pool.affine_select(out=causal_bf[:], in_=causal_bf[:], compare_op=ALU.is_ge, fill=NEG, base=0,
                               pattern=[[-1, P]], channel_multiplier=1).then_inc(consts, 1)
            link(pool.memset(upper[:], 1.0))
            pool.affine_select(out=upper[:], in_=upper[:], compare_op=ALU.is_ge, fill=0.0, base=0,
                               pattern=[[1, P]], channel_multiplier=-1).then_inc(consts, 1)
            pool.wait_ge(ws_in, 16)
            pool.affine_select(out=ws_raw, in_=ws_raw, compare_op=ALU.is_ge, fill=0.0, base=0,
                               pattern=[[0, 8], [-1, P]], channel_multiplier=1).then_inc(pool_prep, 1)
            link(pool.memset(block_diag, 1.0))
            link(pool.affine_select(out=block_diag, in_=block_diag, compare_op=ALU.is_ge, fill=0.0, base=0,
                                    pattern=[[-4, 32], [0, 4]], channel_multiplier=1))
            link(pool.affine_select(out=block_diag, in_=block_diag, compare_op=ALU.is_ge, fill=0.0, base=3,
                                    pattern=[[4, 32], [0, 4]], channel_multiplier=-1))
            pool.wait_ge(small_in, 16 * 6)
            for m in (2, 0, 1):
                for h in range(4):
                    last = pool.tensor_tensor(
                        wbd[:, m, h, :].rearrange("p (b o) -> p b o", o=4),
                        wqkv[:, m, h:h + 1, :].to_broadcast((P, 32, 4)), block_diag, ALU.mult)
                last.then_inc(pool_prep, 1)
            for h in range(MH):
                last = pool.memset(bx[:, h, 0:3], 0.0)
            last.then_inc(pool_prep, 1)
            link(pool.memset(head_sel[:], 0.0))
            pool.affine_select(out=head_sel[:], in_=head_sel[:], compare_op=ALU.not_equal, fill=1.0, base=0,
                               pattern=[[-1, MH], [0, P]], channel_multiplier=1).then_inc(pool_prep, 1)
            link(pool.memset(gate_sel[:], 0.0))
            for g in range(4):
                link(pool.affine_select(out=gate_sel[:], in_=gate_sel[:], compare_op=ALU.not_equal, fill=1.0,
                                        base=-32 * g, pattern=[[-1, 8]], channel_multiplier=1))
            pool.wait_ge(sg_psum0, 8)
            pool.memset(mvals[:, :, :, P:P + 1], 1.0).then_inc(pool_prep, 1)
            pool.memset(neg_m[:], 0.0).then_inc(pool_prep, 1)

            def gate_bias(n):
                layer, cc = ADA[n]
                pool.wait_ge(ada_evac, n + 1)
                if n > GATE_ITEMS[0]:
                    pool.wait_ge(gate_b_in, 16 * GATE_ITEMS.index(n))
                pool.dma_start(ada_row[1:2, n % 2, :], ada_b[layer:layer + 1, CH * cc:CH * cc + CH]).then_inc(gate_b_in, 16)

            gate_bias(4)
            gate_bias(5)
            pool.wait_ge(xc_ready, MH)
            pool.memset(run[:, :, 0:PAD], 0.0).then_inc(pool_prep, 1)

            for h in range(MH):
                for n, s in enumerate(S_ORDER):
                    pool.wait_ge(wt_mult, NT * h + n + 1)
                    blk = wts[:, OFF[s]:OFF[s] + P]
                    pool.affine_select(out=blk, in_=blk, compare_op=ALU.is_ge, fill=0.0, base=0,
                                       pattern=[[1, P]], channel_multiplier=-1).then_inc(wt_ready, 1)
            pool.wait_ge(st_psum, 4 * MH)
            pool.wait_ge(wt_ready, NT * MH)
            for e in range(2):
                if e:
                    pool.wait_ge(qt_zero, 1)
                pool.memset(xres[64 - 64 * e:P - 64 * e, :, CH * e:CH * e + CH], 0.0).then_inc(qt_zero, 1)
            gate_bias(10)
            gate_bias(11)

        @block.tensor
        def _(pe):
            def group(w, g):
                chunk, kh = HALVES[w]
                layout, name = CHUNKS[chunk][4:6]
                first = kh == CHUNKS[chunk][3][0]
                if first and chunk:
                    acc_free(pe, chunk - 1, g)
                s = w % SPLIT
                for i in range(KH):
                    k = KH * kh + i
                    if name in ("bx",) and g == 0:
                        pe.wait_ge(h_ready, k + 1)
                    if name == "y0" and chunk == 6 and g == 0:
                        pe.wait_ge(y_ready, (k - KH if kh else k + KH) + 1)
                    if name == "cv" and chunk == 8 and i == 0 and kh == 0:
                        pe.wait_ge(h1_ready, g + 1)
                    if name == "y1" and chunk == 14 and g == 0:
                        pe.wait_ge(z1_ready, k + 1)
                    parts = [(w_hi, act_hi), (w_hi, act_lo), (w_lo, act_hi)]
                    if layout == "token":
                        parts = [(w_hi, act_hi), (w_lo, act_hi), (w_hi, act_lo)]
                    for n, (wp, ap) in enumerate(parts):
                        if layout == "feature":
                            lhsT, rhs = wp[:, s, i, P * g:P * g + P], ap[:, k, :]
                        else:
                            lhsT, rhs = ap[:, k, P * g:P * g + P], wp[:, s, i, :]
                        last = pe.matmul(acc[g][:, :], lhsT, rhs, start=first and i == 0 and n == 0,
                                         stop=not first and i == KH - 1 and n == 2)
                if not first:
                    last.then_inc(acc_ready, 1)
                elif g == 3:
                    last.then_inc(even_half_done, 1)

            def ada_pair(n, bank):
                for kh in range(2):
                    s = landed(pe, ("ada", 2 * n + kh))
                    for j in range(4):
                        last = pe.matmul(bank[32 * j:32 * j + 32, :], c_pad[:, KH * kh + j, :], raw[:, s, j, :],
                                         start=kh == 0, stop=kh == 1, tile_position=(0, 32 * j))
                        if j == 3 and kh == 0:
                            last.then_inc(ada_used, 1)
                last.then_inc(ada_used, 1)

            def mod_cols(n, bank):
                pe.wait_ge(ada_evac, n + 1)
                for q in range(4):
                    last = pe.matmul(bank[:, q:q + 1], ada_row[:, n % 2, P * q:P * q + P], ones[:, 0:1],
                                     start=True, stop=True)
                last.then_inc(modc_psum, 1)

            def gate_row(n, bank):
                pe.wait_ge(ada_evac, n + 1)
                pe.wait_ge(gate_b_in, 16 * (GATE_ITEMS.index(n) + 1))
                pe.matmul(bank[:, :], ones[:, :], ada_row[:, n % 2, :], start=True, stop=True).then_inc(gate_psum, 1)

            pe.wait_ge(rows_in, 16 * 12)
            pe.wait_ge(consts, 2)
            pe.transpose(work[0][:, 0:NROWS], rows[0:NROWS, :], ident[0:NROWS, 0:NROWS]).then_inc(rows_t, 1)
            for t in range(NT):
                pe.wait_ge(xn_ready, t + 1)
                for hf in range(2):
                    n = 2 * t + hf
                    if n >= 4:
                        pe.wait_ge(xt_evac, n - 3)
                    for q in range(4):
                        k = 4 * hf + q
                        last = pe.transpose(acc[n % 4][:, P * q:P * q + P], xres[:, t, P * k:P * k + P], ident[:, :])
                    last.then_inc(xt_psum, 1)
            pe.wait_ge(pool_prep, 1)
            pe.wait_ge(cols_ready, 1)
            for hf in range(2):
                for q in range(4):
                    last = pe.transpose(work[hf][:, P * q:P * q + P], ws_raw[:, 4 * hf + q, :], ident[:, :])
                last.then_inc(wm_psum, 1)
            pe.wait_ge(small_in, 16 * 6)
            for g in range(8):
                pe.wait_ge(wm_evac, g // 4 + 1)
                pe.matmul(work[g // 4][:, P * (g % 4):P * (g % 4) + P], lnb_bc[:, P * g:P * g + P], wm[:, g, :],
                          start=True, stop=True).then_inc(sg_psum0, 1)

            pe.wait_ge(c_ready, 1)
            for n in range(4):
                if n >= 1:
                    pe.wait_ge(mod_ready, n)
                ada_pair(n, work[3])
                mod_cols(n, work[3])
            def wv_transposes():
                pe.wait_ge(consts, 5)
                pe.wait_ge(pool_prep, 2)
                pe.wait_ge(sg_ready, 2)
                for h in range(4):
                    last = pe.transpose(work[0][:, P * h:P * h + P], wbd[:, 2, h, :], ident[:, :])
                last.then_inc(wvt_psum, 1)

            def gate_eff():
                pe.wait_ge(wvt_ready, 1)
                pe.wait_ge(wg_in, 16)
                for h in range(4):
                    last = pe.matmul(work[1][:, 8 * h:8 * h + 8], wvt[:, h, :], wg_pad[:, 8 + h, 0:8],
                                     start=True, stop=True)
                last.then_inc(eff_psum, 1)

            def m_values(t):
                if t == 0:
                    pe.wait_ge(acc_freed_act, MH)
                    pe.wait_ge(eff_ready, 1)
                if t == 3:
                    pe.wait_ge(mv_evac, 1)
                for h in range(MH):
                    last = pe.matmul(work[t % 3][:, P * h:P * h + P], bx[:, h, 3 + P * t:3 + P * t + P],
                                     wbd[:, 2, h, :], start=True, stop=True)
                last.then_inc(mv_psum, 1)

            def m_qk(n):
                pe.wait_ge(mv_evac, 4)
                pe.wait_ge(xc_ready, n % 4 + 1)
                pe.wait_ge(pool_prep, 4)
                if n >= 3:
                    pe.wait_ge(mqk_evac, n - 2)
                pe.matmul(work[n % 3][:, :], wbd[:, n // 4, n % 4, :], xc[:, n % 4, :],
                          start=True, stop=True).then_inc(mqk_psum, 1)

            def gates():
                pe.wait_ge(mqk_evac, 8)
                for part in range(3):
                    for h in range(MH):
                        rhs = (mq[:, h, :], mk[:, h, :], bx[:, h, 3:3 + T])[part]
                        last = pe.matmul(work[0][32 * h:32 * h + 32, :], wg_pad[:, 4 * part + h, :], rhs,
                                         start=part == 0, stop=part == 2, tile_position=(0, 32 * h))
                last.then_inc(g_psum, 1)

            def gates_tokens():
                pe.wait_ge(g_evac, 1)
                pe.wait_ge(pool_prep, 8)
                for t in range(NT):
                    last = pe.matmul(work[1][:, 8 * t:8 * t + 8], gates_t[:, P * t:P * t + P], gate_sel[:, :],
                                     start=True, stop=True)
                last.then_inc(gt_psum, 1)

            def cumulate():
                pe.wait_ge(lf_ready, 1)
                pe.matmul(work[2][:, 0:16], upper[:, :], gt[:, 4, :], start=True, stop=False)
                pe.matmul(work[2][:, 0:16], ones[:, :], pre[:, :, :].rearrange("p t h -> p (t h)"), start=False,
                          stop=True).then_inc(cum_psum, 1)

            def a_rows():
                pe.wait_ge(a_ready, 1)
                for t in range(NT):
                    last = pe.transpose(work[0][0:4, P * t:P * t + P], gt[:, 6, 4 * t:4 * t + 4], ident[:, :])
                last.then_inc(at_psum, 1)

            def m_cols():
                pe.wait_ge(m_rows, 1)
                for t in range(NT):
                    last = pe.transpose(work[1][:, 4 * t:4 * t + 4], neg_m[0:4, P * t:P * t + P], ident[0:4, 0:4])
                last.then_inc(mc_psum, 1)

            def m_scores(h):
                if h == 0:
                    pe.wait_ge(mc_ready, 1)
                else:
                    pe.wait_ge(wt_mult, NT * h)
                    pe.wait_ge(num_evac, 2 * h)
                pe.matmul(work[0][:, :], head_sel[:, h, :], neg_m[:, :], start=True, stop=True).then_inc(mb_psum, 1)
                for s, bank, at in ((0, 1, 0), (1, 2, 0), (3, 2, 384)):
                    n = T - P * s
                    pe.matmul(work[bank][:, at:at + n], mk[:, h, P * s:P * s + P], mq[:, h, P * s:T],
                              start=True, stop=True).then_inc(st_psum, 1)

            def m_scores2(h):
                pe.wait_ge(mexp, NT * (h + 1))
                pe.matmul(work[0][:, 0:256], mk[:, h, 256:384], mq[:, h, 256:T], start=True,
                          stop=True).then_inc(st_psum, 1)

            def m_values_out(h):
                pe.wait_ge(wt_ready, NT * (h + 1))
                for t in range(NT):
                    bank = work[1 + t // 2]
                    at = 256 * (t % 2)
                    for s in range(t + 1):
                        o = OFF[s] + P * (t - s)
                        last = pe.matmul(bank[:, at:at + P + 1], wts[:, o:o + P], mvals[:, s, h, 0:P + 1],
                                         start=s == 0, stop=s == t)
                    if t % 2:
                        last.then_inc(pv_psum, 1)

            def hb_transposes(h):
                if h == 0:
                    pe.wait_ge(hb_ready, 1)
                    pe.wait_ge(mod_ready, len(MOD_ITEMS))
                else:
                    pe.wait_ge(yb_part, h)
                for t in range(NT):
                    last = pe.transpose(work[3][:, P * t:P * t + P], num[:, 4 * t + h, 0:P], ident[:, :])
                last.then_inc(hbt_psum, 1)

            def qk_transposes(n):
                if n == 0:
                    pe.wait_ge(q_evac, 4)
                    pe.wait_ge(num_evac, 2 * MH)
                if n == 4:
                    pe.wait_ge(k_norm, 4)
                if 2 <= n < 6:
                    pe.wait_ge(qt_ready, n - 1)
                if n >= 6:
                    pe.wait_ge(kt_ready, n - 5)
                src = q_raw if n < 4 else k_raw
                p = n % 4
                for t in range(NT):
                    last = pe.transpose(work[n % 2][:, P * t:P * t + P], src[:, t, P * p:P * p + P], ident[:, :])
                last.then_inc(qt_psum if n < 4 else kt_psum, 1)

            def a_scores(u):
                h, i, e = UNITS[u]
                if u < 2:
                    pe.wait_ge(qt_ready, 4)
                    pe.wait_ge(kt_ready, 4)
                    pe.wait_ge(qt_zero, 2)
                else:
                    pe.wait_ge(exp_ready, u - 1)
                n = P * (i + 1)
                bank = work[u % 2]
                pe.matmul(bank[:, 0:n], qt[:, h, P * i:P * i + P], kt[:, h // 2, 0:n], start=True, stop=False)
                pe.matmul(bank[:, n - P:n], ident_bf[:, :], causal_bf[:, :], start=False,
                          stop=True).then_inc(s_psum, 1)

            def p_transposes(u):
                h, i, e = UNITS[u]
                pe.wait_ge(p_ready, u + 1)
                if u:
                    pt_done(pe, u - 1)
                for j in range(i + 1):
                    last = pe.transpose(work[2][:, P * j:P * j + P], probs[:, u % 3, P * j:P * j + P], ident[:, :])
                last.then_inc(pt_psum, 1)

            def a_values(p):
                pt_done(pe, 8 * p + 7)
                pt_done(pe, 8 * p + 6)
                if p == 0:
                    pe.wait_ge(acc_freed_act, 24)
                    pe.wait_ge(yb_part, 4)
                else:
                    pe.wait_ge(y_exact, 4 + p)
                for j in range(NT):
                    for e in range(2):
                        h = 2 * p + e
                        last = pe.matmul(work[3][64 * e:64 * e + 64, P * j:T], avals[:, j, DA * h:DA * h + DA],
                                         probs_t[:, e, j, P * j:T], start=j == 0, stop=j == NT - 1)
                last.then_inc(o_psum, 1)

            def pt_done(eng, u):
                n = sum(PT_ON_ACT(v) for v in range(u + 1))
                if PT_ON_ACT(u):
                    eng.wait_ge(pt_act, n)
                else:
                    eng.wait_ge(pt_dve, u + 1 - n)

            def attention(u):
                if u < NU:
                    a_scores(u)
                if u >= LAG and (u - LAG) % 8 == 0 and u - LAG > 0:
                    a_values((u - LAG) // 8 - 1)
                if LAG <= u < NU + LAG:
                    p_transposes(u - LAG)

            def h1_transposes(t):
                pe.wait_ge(xn1_ready, t + 1)
                if t:
                    pe.wait_ge(h1_exact, 8 * t)
                for k in range(KT):
                    last = pe.transpose(work[k // 4][:, P * (k % 4):P * (k % 4) + P], xn[:, t % 2, P * k:P * k + P],
                                        ident[:, :])
                last.then_inc(h1_psum, 1)

            def spatial(g):
                pe.wait_ge(vn_ready, 4)
                if g >= 3:
                    pe.wait_ge(us_ready, g - 2)
                for t in range(NT):
                    last = pe.matmul(work[g % 3][:, P * t:P * t + P], vg[:, t, P * g:P * g + P], wm[:, g, :],
                                     start=True, stop=True)
                last.then_inc(sg_psum, 1)

            extra = {(0, 0): [wv_transposes], (0, 3): [gate_eff]}

            def at(slot, job):
                extra.setdefault(slot, []).append(job)

            for t in range(NT):
                at((2, t), lambda t=t: m_values(t))
            for n in range(8):
                at((3, n // 2), lambda n=n: m_qk(n))
            at((4, 0), gates)
            at((4, 1), gates_tokens)
            at((6, 1), cumulate)
            at((6, 2), a_rows)
            at((6, 3), m_cols)
            for h in range(MH):
                for n, job in enumerate((m_scores, m_scores2, m_values_out)):
                    slot = 28 + 3 * h + n
                    at((slot // 4, slot % 4), lambda h=h, job=job: job(h))
            for p in range(4):
                at((10, p), lambda p=p: qk_transposes(2 * p))
                at((10, p), lambda p=p: qk_transposes(2 * p + 1))
                at((11, p), lambda p=p: hb_transposes(p))
            for slot, us in ATT_SLOTS.items():
                for u in us:
                    at(slot, lambda u=u: attention(u))
            for t, slot in enumerate(((15, 2), (15, 3), (16, 0), (16, 1))):
                at(slot, lambda t=t: h1_transposes(t))
            for g in range(8):
                at((22 + g // 4, g % 4) if g < 4 else (24, g % 4), lambda g=g: spatial(g))
            bank3_free = {4: (mod_ready, 4), 5: (gate_ready, 1), 6: (gate_ready, 2), 7: (mod_ready, 5),
                          8: (mod_ready, 6), 9: (mod_ready, 7), 10: (y_exact, 8), 11: (ada_evac, 11)}

            def ada_later(n):
                pe.wait_ge(*bank3_free[n])
                ada_pair(n, work[3])

            def ada_use(n):
                if n in MOD_ITEMS:
                    mod_cols(n, work[3])
                else:
                    if n >= 10:
                        pe.wait_ge(*((ada_evac, 12) if n == 10 else (gate_ready, 3)))
                    gate_row(n, work[3])

            for n in range(4, 12):
                at(ADA_SLOT[n], lambda n=n: ada_later(n))
                at(ADA_USE_SLOT[n], lambda n=n: ada_use(n))
            for w in range(NHALF):
                for job in extra.get((w, -1), []):
                    job()
                pe.wait_ge(w_lo_ready, w + 1)
                for g in range(4):
                    group(w, g)
                    for job in extra.get((w, g), []):
                        job()

        @block.scalar
        def _(act_e):
            count = [0]

            def link(ins):
                count[0] += 1
                ins.then_inc(act_step, 1)
                act_e.wait_ge(act_step, count[0])

            def copy(dst, src):
                return nc.scalar.activation(dst, src, ACT.Copy)

            def rsqrt(y, v, ready, n, done):
                act_e.wait_ge(ready, n)
                link(nc.scalar.activation(y, v, ACT.Ln))
                nc.scalar.activation(y, y, ACT.Exp, scale=-0.5).then_inc(done, 1)

            def split_hi(w):
                s = landed(act_e, ("w", w))
                if w >= SPLIT:
                    half_done(act_e, w - SPLIT)
                copy(w_hi[:, w % SPLIT, :, :], raw[:, s, :, :]).then_inc(w_hi_ready, 1)

            def ada_out(n):
                act_e.wait_ge(ada_used, 2 * n + 2)
                copy(ada_row[:, n % 2, :], work[3][:, :]).then_inc(ada_evac, 1)

            flat = [("ada_b", ada_b), ("ln_g", ln_g), ("c", c)]
            for name, a in flat:
                r, n = ROWS[name]
                act_e.dma_start(rows[r:r + n, :], a.rearrange("l (j f) -> (l j) f", f=P)).then_inc(rows_in, 16)
            for name, a in (("conv_w", b_conv_w[0]), ("conv_b", b_conv_b), ("out_g", b_out_g), ("skip", b_skip),
                            ("c_ln_g", c_ln_g)):
                r, n = ROWS[name]
                act_e.dma_start(rows[r:r + n, :], a.rearrange("l (j f) -> (l j) f", f=P)).then_inc(rows_in, 16)
            for name, a in (("q_g", a_q_g), ("k_g", a_k_g)):
                r = ROWS[name][0]
                for e in range(2):
                    act_e.dma_start(rows[r:r + 1, DA * e:DA * e + DA], a).then_inc(rows_in, 16)
            for t in range(NT):
                act_e.dma_start(xres[:, t, :], x_view[:, t, :]).then_inc(x_in[t], 16)
            nc.scalar.preload_act_table_set("silu_and_others")
            for t in range(NT):
                act_e.wait_ge(x_in[t], 16)
                nc.scalar.activation(act[:, 2 * t:2 * t + 2, :].rearrange("p a b -> p (a b)"), xres[:, t, :], ACT.Square,
                                     accum_out=rms[:, 0, t:t + 1]).then_inc(ss_ready, 1)
            act_e.wait_ge(cols_ready, 1)
            act_e.wait_ge(consts, 2)
            nc.scalar.activation(c_pad[:, :, 0], col("c", 0, 8), ACT.Silu).then_inc(c_ready, 1)
            nc.scalar.preload_act_table_set(LNEXP)
            rsqrt(rms[:, 2, 0:4], rms[:, 1, 0:4], var_ready, 1, ln_ready)
            for n in range(8):
                act_e.wait_ge(xt_psum, n + 1)
                t, hf = n // 2, n % 2
                copy(act[:, 4 * hf:4 * hf + 4, P * t:P * t + P],
                     acc[n % 4][:, :].rearrange("p (k q) -> p k q", k=4)).then_inc(xt_evac, 1)
            for hf in range(2):
                act_e.wait_ge(wm_psum, hf + 1)
                copy(wm[:, 4 * hf:4 * hf + 4, :], work[hf][:, :].rearrange("p (k q) -> p k q", k=4)).then_inc(wm_evac, 1)
            for n in range(4):
                ada_out(n)
            split_hi(0)
            for k in range(KT):
                act_e.wait_ge(h_exact, k + 1)
                copy(act_hi[:, k, :], act[:, k, :]).then_inc(h_hi, 1)

            todo = {}

            def at(slot, job):
                todo.setdefault(slot, []).append(job)

            def acc_wait(w, g):
                act_e.wait_ge(acc_ready, 4 * (w // 2) + g + 1)

            def bx_out(g):
                acc_wait(1, g)
                copy(bx[:, g, 3:3 + T], acc[g][:, :]).then_inc(acc_freed_act, 1)

            def gate_act(w, g, k):
                acc_wait(w, g)
                nc.scalar.activation(act[:, k, :], acc[g][:, :], ACT.Silu).then_inc(acc_freed_act, 1)

            def mv_out(t):
                act_e.wait_ge(mv_psum, t + 1)
                if t == 0:
                    act_e.wait_ge(pool_prep, 7)
                copy(mvals[:, t, :, 0:P], work[t % 3][:, :].rearrange("p (h v) -> p h v", h=MH)).then_inc(mv_evac, 1)

            def xc_out(h):
                act_e.wait_ge(conv_step, 12 + h + 1)
                nc.scalar.activation(xc[:, h, :], conv[:, h, :], ACT.Silu).then_inc(xc_ready, 1)

            def mqk_out(n):
                act_e.wait_ge(mqk_psum, n + 1)
                copy((mq if n < 4 else mk)[:, n % 4, :], work[n % 3][:, :]).then_inc(mqk_evac, 1)

            def gates_out():
                act_e.wait_ge(g_psum, 1)
                copy(gates_t[:, :], work[0][:, :]).then_inc(g_evac, 1)

            def gates_log():
                nc.scalar.preload_act_table_set(LNEXP)
                act_e.wait_ge(gt_abs, 1)
                link(nc.scalar.activation(gt[:, 3, :], gt[:, 2, :], ACT.Exp, scale=-1.0))
                nc.scalar.activation(gt[:, 3, :], gt[:, 3, :], ACT.Ln, bias=1.0).then_inc(gt_ln, 1)

            def guard():
                act_e.wait_ge(mc_ready, 1)
                nc.scalar.activation(gt[:, 9, :], gt[:, 7, :], ACT.Exp).then_inc(guard_ready, 1)

            def m_exps(h):
                act_e.wait_ge(mb_psum, h + 1)
                for s in S_ORDER:
                    n = T - P * s
                    nc.scalar.activation(expw[:, OFF[s]:OFF[s] + n], work[0][:, P * s:T], ACT.Exp,
                                         bias=gt[:, 6, 4 * s + h:4 * s + h + 1]).then_inc(mexp, 1)

            def num_out(h):
                for a in range(2):
                    act_e.wait_ge(pv_psum, 2 * h + a + 1)
                    dst = num[:, :, :].rearrange("p (t h) v -> p t h v", t=NT)[:, 2 * a:2 * a + 2, h, 0:P + 1]
                    src = work[1 + a][:, :].rearrange("p (t v) -> p t v", t=2)[:, :, 0:P + 1]
                    copy(dst, src).then_inc(num_evac, 1)

            def qk_out(w, g, dst, evac):
                n = g + (4 if dst is k_raw else 0)
                acc_wait(w, g)
                copy(dst[:, g, :], acc[g][:, :]).then_inc(evac, 1)
                if n >= 2:
                    act_e.wait_ge(sq_used, n - 1)
                nc.scalar.activation(conv[:, n % 2, :], acc[g][:, :], ACT.Square).then_inc(acc_freed_act, 1)

            def v_out(g):
                acc_wait(11, g)
                copy(avals[:, g, :], acc[g][:, :]).then_inc(acc_freed_act, 1)

            def qt_out(p):
                act_e.wait_ge(qt_psum, p + 1)
                for e in range(2):
                    r = slice(64 * e, 64 * e + 64)
                    last = nc.scalar.activation(qt[r, 2 * p + e, :], work[p % 2][r, :], ACT.Copy,
                                                scale=col("q_g", 0)[r])
                last.then_inc(qt_ready, 1)

            def attention(u):
                if u < NU:
                    h, i, e = UNITS[u]
                    n = P * (i + 1)
                    act_e.wait_ge(bias_ready, u + 1)
                    if u >= 3:
                        act_e.wait_ge(pt_psum, u - 2)
                    q = 8 * i + h
                    nc.scalar.activation(probs[:, u % 3, 0:n], work[u % 2][:, 0:n], ACT.Exp, bias=mx[:, 1, u:u + 1],
                                         scale=qs[:, 4, q:q + 1], accum_out=rs[:, 0, u:u + 1]).then_inc(exp_ready, 1)
                v = u - LAG
                if 0 <= v < NU and PT_ON_ACT(v):
                    h, i, e = UNITS[v]
                    act_e.wait_ge(pt_psum, v + 1)
                    copy(probs_t[:, e, 0:i + 1, P * i:P * i + P],
                         work[2][:, 0:P * (i + 1)].rearrange("p (j q) -> p j q", j=i + 1)).then_inc(pt_act, 1)
                if u in YA_SPLIT:
                    y_hi_part(4 + YA_SPLIT[u])

            def y_hi_part(n):
                k = Y_ORDER[n]
                half_done(act_e, 11)
                act_e.wait_ge(y_exact, n + 1)
                copy(act_hi[:, k, :], act[:, k, :]).then_inc(y_hi, 1)

            def x1_square(t):
                act_e.wait_ge(x1_ready, t + 1)
                nc.scalar.activation(probs[:, :, :].rearrange("p a b -> p (a b)")[:, 0:D], xres[:, t, :], ACT.Square,
                                     accum_out=rms[:, 0, 4 + t:5 + t]).then_inc(ss1_ready, 1)
                rsqrt(rms[:, 2, 4 + t:5 + t], rms[:, 1, 4 + t:5 + t], var1_ready, t + 1, ln1_ready)

            def h1_hi_part(t):
                act_e.wait_ge(h1_exact, KT * (t + 1))
                copy(act_hi[:, :, P * t:P * t + P], act[:, :, P * t:P * t + P]).then_inc(h1_hi, 1)

            def gelu_v(w, g):
                cc = (w - 17) // 2
                acc_wait(w, g)
                nc.scalar.activation(vg[:, g, CH * cc:CH * cc + CH], acc[g][:, :],
                                     ACT.Gelu_apprx_tanh).then_inc(acc_freed_act, 1)

            def cv_rsqrt():
                nc.scalar.preload_act_table_set(LNEXP)
                rsqrt(rms[:, 2, 0:4], rms[:, 1, 0:4], cvar_ready, 1, cln_ready)
                nc.scalar.preload_act_table_set("gelu_apprx_tanh_and_others")

            def gelu_u(w, g):
                acc_wait(w, g)
                k = g + 4 * ((w - 21) // 2)
                nc.scalar.activation(act[:, k, :], acc[g][:, :], ACT.Gelu_apprx_tanh).then_inc(acc_freed_act, 1)

            def silu_z(w, g):
                n = g + 4 * ((w - 25) // 2)
                acc_wait(w, g)
                if n >= 4:
                    act_e.wait_ge(z1_exact, n - 3)
                nc.scalar.activation(tmp[:, n % 4, :], acc[g][:, :], ACT.Silu).then_inc(acc_freed_act, 1)

            def z1_hi_part(k):
                half_done(act_e, 27)
                act_e.wait_ge(z1_exact, k + 1)
                copy(act_hi[:, k, :], act[:, k, :]).then_inc(z1_hi, 1)

            for g in range(4):
                at((1, g), lambda g=g: bx_out(g))
                at((2, g), lambda g=g: mv_out(g))
                at((3, g), lambda g=g: gate_act(3, g, g))
                at((5, g), lambda g=g: gate_act(5, g, 4 + g))
                at((7, g), lambda g=g: qk_out(7, g, q_raw, q_evac))
                at((9, g), lambda g=g: qk_out(9, g, k_raw, k_evac))
                at((11, g), lambda g=g: v_out(g))
                at((17, g), lambda g=g: gelu_v(17, g))
                at((19, g), lambda g=g: gelu_v(19, g))
                at((21, g), lambda g=g: gelu_u(21, g))
                at((23, g), lambda g=g: gelu_u(23, g))
                at((25, g), lambda g=g: silu_z(25, g))
                at((27, g), lambda g=g: silu_z(27, g))
            at((1, 3), lambda: nc.scalar.preload_act_table_set("silu_and_others"))
            for h in range(MH):
                at((2, 3), lambda h=h: xc_out(h))
            for n in range(8):
                at((3, n // 2), lambda n=n: mqk_out(n))
            at((4, 0), gates_out)
            at((6, 0), gates_log)
            at((6, 3), guard)
            for h in range(MH):
                s0, s2 = 28 + 3 * h, 28 + 3 * h + 2
                at((s0 // 4, s0 % 4), lambda h=h: m_exps(h))
                at((s2 // 4, s2 % 4), lambda h=h: num_out(h))
            at((10, 0), lambda: rsqrt(qs[:, 2, :], qs[:, 1, :], qk_ss, 1, qk_ln))
            for p in range(4):
                at((10, p // 2), lambda p=p: qt_out(p))
            at((10, 1), lambda: rsqrt(gt[:, 9, :], gt[:, 8, :], mvar_ready, 1, mln_ready))
            for slot, us in ATT_SLOTS.items():
                if slot == (12, -1):
                    for n in range(4):
                        at((11, 3), lambda n=n: y_hi_part(n))
                for u in us:
                    at(slot, lambda u=u: attention(u))
            at((15, 0), lambda: x1_square(0))
            at((15, 1), lambda: x1_square(1))
            at((15, 2), lambda: x1_square(2))
            at((15, 2), lambda: h1_hi_part(0))
            at((15, 3), lambda: h1_hi_part(1))
            at((15, 3), lambda: x1_square(3))
            at((16, 0), lambda: h1_hi_part(2))
            at((16, 1), lambda: h1_hi_part(3))
            at((16, 1), lambda: nc.scalar.preload_act_table_set("gelu_apprx_tanh_and_others"))
            at((20, 0), cv_rsqrt)
            at((24, 0), lambda: nc.scalar.preload_act_table_set("silu_and_others"))
            for n in range(4, 12):
                at(ADA_SLOT[n], lambda n=n: ada_out(n))
            for k in range(KT):
                at((27, 3), lambda k=k: z1_hi_part(k))
            for w in range(NHALF):
                if w == 12:
                    for job in todo.get((w, -1), []):
                        job()
                if w + 1 < NHALF:
                    split_hi(w + 1)
                for g in range(4):
                    for job in todo.get((w, g), []):
                        job()

        @block.vector
        def _(dve):
            v_e = nc.vector
            count = [0]

            def link(ins):
                count[0] += 1
                ins.then_inc(dve_step, 1)
                dve.wait_ge(dve_step, count[0])

            def refine(y, v, t):
                link(v_e.tensor_tensor(t, y, y, ALU.mult))
                link(v_e.tensor_tensor(t, t, v, ALU.mult))
                link(v_e.tensor_scalar(t, t, -0.5, 1.5, ALU.mult, ALU.add))
                link(v_e.tensor_tensor(y, y, t, ALU.mult))

            def minus(dst, whole, hi):
                return v_e.tensor_tensor(dst, whole, hi.bitcast(F32), ALU.subtract)

            def split_lo(w):
                dve.wait_ge(w_hi_ready, w + 1)
                s = landed(dve, ("w", w))
                minus(w_lo[:, w % SPLIT, :, :], raw[:, s, :, :], w_hi[:, w % SPLIT, :, :]).then_inc(w_lo_ready, 1)

            def mod_out(n):
                layer, cc = ADA[n]
                dve.wait_ge(modc_psum, MOD_ITEMS.index(n) + 1)
                dst = mod[:, layer, 4 * cc:4 * cc + 4]
                ins = v_e.tensor_tensor(dst, work[3][:, 0:4], col("ada_b", 24 * layer + 4 * cc, 4), ALU.add)
                if cc >= 2:
                    link(ins)
                    ins = v_e.scalar_tensor_tensor(out=gain[:, layer, 4 * cc - 8:4 * cc - 4], in0=dst, scalar=1.0,
                                                   in1=col("ln_g", 8 * layer + 4 * cc - 8, 4), op0=ALU.add,
                                                   op1=ALU.mult)
                ins.then_inc(mod_ready, 1)

            def gate_out(n):
                cc = ADA[n][1]
                dve.wait_ge(gate_psum, GATE_ITEMS.index(n) + 1)
                v_e.tensor_copy(gate_bc[:, CH * (cc - 4):CH * (cc - 3)], work[3][:, :]).then_inc(gate_ready, 1)

            dve.wait_ge(rows_t, 1)
            v_e.tensor_copy(cols[:, :], work[0][:, 0:NROWS]).then_inc(cols_ready, 1)
            dve.wait_ge(ss_ready, NT)
            v_e.tensor_scalar(rms[:, 1, 0:4], rms[:, 0, 0:4], 1.0 / D, 1e-6, ALU.mult, ALU.add).then_inc(var_ready, 1)
            dve.wait_ge(ln_ready, 1)
            refine(rms[:, 2, 0:4], rms[:, 1, 0:4], rms[:, 3, 0:4])
            for t in range(NT):
                v_e.tensor_scalar(xres[:, t, :], xres[:, t, :], rms[:, 2, t:t + 1], None, ALU.mult).then_inc(xn_ready, 1)
            dve.wait_ge(small_in, 16 * 6)
            for a in range(2):
                dve.wait_ge(sg_psum0, 4 * a + 4)
                v_e.tensor_tensor(sg_add[:, 4 * a:4 * a + 4, :], work[a][:, :].rearrange("p (g t) -> p g t", g=4),
                                  bs_bc[:, 4 * a:4 * a + 4, :], ALU.add).then_inc(sg_ready, 1)
            for n in range(4):
                mod_out(n)
            dve.wait_ge(mod_ready, 4)
            dve.wait_ge(xt_evac, 8)

            def h_part(k):
                v_e.tensor_scalar(act[:, k, :], act[:, k, :], gain[:, 0, k:k + 1], mod[:, 0, k:k + 1], ALU.mult,
                                  ALU.add).then_inc(h_exact, 1)

            def h_lo_part(k):
                dve.wait_ge(h_hi, k + 1)
                minus(act_lo[:, k, :], act[:, k, :], act_hi[:, k, :]).then_inc(h_ready, 1)

            h_part(0)
            h_part(1)
            split_lo(0)
            for k in range(KT):
                if k + 2 < KT:
                    h_part(k + 2)
                h_lo_part(k)

            todo = {}

            def at(slot, job):
                todo.setdefault(slot, []).append(job)

            def wvt_out():
                dve.wait_ge(wvt_psum, 1)
                v_e.tensor_copy(wvt, work[0][:, :].rearrange("p (h c) -> p h c", h=4)).then_inc(wvt_ready, 1)

            def eff_out():
                dve.wait_ge(eff_psum, 1)
                v_e.tensor_copy(wg_pad[:, 8:12, 0:8],
                                work[1][:, 0:32].rearrange("p (h r) -> p h r", h=4)).then_inc(eff_ready, 1)

            def conv_tap(j, h):
                w = col("conv_w", 4 * j + h)
                if j == 0:
                    dve.wait_ge(acc_freed_act, h + 1)
                    dve.wait_ge(pool_prep, 5)
                    ins = v_e.tensor_scalar(conv[:, h, :], bx[:, h, 0:T], w, col("conv_b", h), ALU.mult, ALU.add)
                else:
                    dve.wait_ge(conv_step, 4 * (j - 1) + h + 1)
                    ins = v_e.scalar_tensor_tensor(out=conv[:, h, :], in0=bx[:, h, j:j + T], scalar=w,
                                                   in1=conv[:, h, :], op0=ALU.mult, op1=ALU.add)
                ins.then_inc(conv_step, 1)

            def skip_part():
                dve.wait_ge(mqk_psum, 8)
                for h in range(MH):
                    last = v_e.tensor_scalar(xc[:, h, :], xc[:, h, :], col("skip", h), None, ALU.mult)
                last.then_inc(skip_done, 1)

            def gates_add():
                dve.wait_ge(gt_psum, 1)
                for m in range(2):
                    ins = v_e.tensor_tensor(
                        gt[:, m, :].rearrange("p (t h) -> p t h", t=NT),
                        work[1][:, 0:32].rearrange("p (t r) -> p t r", t=NT)[:, :, 4 * m:4 * m + 4],
                        bg_bc[:, 4 * m:4 * m + 4].unsqueeze(1).to_broadcast((P, NT, 4)), ALU.add)
                link(ins)
                v_e.scalar_tensor_tensor(out=gt[:, 2, :], in0=gt[:, 1, :], scalar=-1.0, in1=gt[:, 1, :],
                                         op0=ALU.mult, op1=ALU.max).then_inc(gt_abs, 1)

            def log_forget():
                dve.wait_ge(gt_ln, 1)
                link(v_e.scalar_tensor_tensor(out=gt[:, 4, :], in0=gt[:, 1, :], scalar=0.0, in1=gt[:, 3, :],
                                              op0=ALU.min, op1=ALU.subtract))
                v_e.memset(pre[:, 0, :], 0.0)
                link(v_e.tensor_copy(pre[:, 1, :], gt[:, 4, 0:4]))
                link(v_e.tensor_tensor(pre[:, 2, :], pre[:, 1, :], gt[:, 4, 4:8], ALU.add))
                v_e.tensor_tensor(pre[:, 3, :], pre[:, 2, :], gt[:, 4, 8:12], ALU.add).then_inc(lf_ready, 1)

            def a_cols():
                dve.wait_ge(cum_psum, 1)
                v_e.tensor_copy(gt[:, 5, :], work[2][:, 0:16])
                v_e.tensor_tensor(gt[:, 6, :], gt[:, 0, :], work[2][:, 0:16], ALU.subtract).then_inc(a_ready, 1)

            def running_max():
                dve.wait_ge(at_psum, 1)
                dve.wait_ge(pool_prep, 9)
                link(v_e.tensor_scalar(run[:, 0, PAD:PAD + T], work[0][0:4, :], 0.0, None, ALU.max))
                b, d = 0, 1
                while d < T:
                    link(v_e.tensor_tensor(run[:, 1 - b, PAD:PAD + T], run[:, b, PAD:PAD + T],
                                           run[:, b, PAD - d:PAD + T - d], ALU.max))
                    b, d = 1 - b, 2 * d
                v_e.tensor_scalar(neg_m[0:4, :], run[:, b, PAD:PAD + T], -1.0, None, ALU.mult).then_inc(m_rows, 1)

            def m_exponent():
                dve.wait_ge(mc_psum, 1)
                v_e.tensor_tensor(gt[:, 7, :], work[1][:, 0:16], gt[:, 5, :], ALU.subtract).then_inc(mc_ready, 1)

            def weights(h, part):
                if part == 0 and h:
                    dve.wait_ge(pv_psum, 2 * h)
                for n, s in enumerate(S_ORDER):
                    if (n == 3) != (part == 1):
                        continue
                    dve.wait_ge(st_psum, NT * h + (1, 3, 3, 4)[n])
                    dve.wait_ge(mexp, NT * h + n + 1)
                    bank, at_ = {0: (1, 0), 1: (2, 0), 3: (2, 384), 2: (0, 0)}[s]
                    m = T - P * s
                    v_e.scalar_tensor_tensor(out=wts[:, OFF[s]:OFF[s] + m], in0=work[bank][:, at_:at_ + m],
                                             scalar=float(P) ** -0.5, in1=expw[:, OFF[s]:OFF[s] + m], op0=ALU.mult,
                                             op1=ALU.mult).then_inc(wt_mult, 1)

            def head_stats(h):
                dve.wait_ge(num_evac, 2 * h + 2)
                for t in range(NT):
                    ins = v_e.bn_stats(st6[:, 4 * t + h, :], num[:, 4 * t + h, 0:P])
                link(ins)
                for t in range(NT):
                    ins = v_e.bn_aggr(mv2[:, 4 * t + h, :], st6[:, 4 * t + h, :])
                if h == MH - 1:
                    link(ins)

            def square_sums(n):
                dve.wait_ge(acc_freed_act, 12 + n + 1)
                v_e.tensor_reduce(qs[:, 0, 8 * n:8 * n + 8], conv[:, n % 2, :].rearrange("p (h d) -> p h d", h=AH),
                                  AX_X, ALU.add).then_inc(sq_used, 1)

            def norms():
                dve.wait_ge(sq_used, 8)
                v_e.tensor_scalar(qs[:, 1, :], qs[:, 0, :], 1.0 / DA, 1e-6, ALU.mult, ALU.add).then_inc(qk_ss, 1)
                dve.wait_ge(guard_ready, 1)
                link(v_e.scalar_tensor_tensor(out=gt[:, 8, :], in0=num[:, :, P], scalar=-1.0, in1=num[:, :, P],
                                              op0=ALU.mult, op1=ALU.max))
                link(v_e.tensor_tensor(gt[:, 8, :], gt[:, 8, :], gt[:, 9, :], ALU.max))
                link(v_e.reciprocal(gt[:, 10, :], gt[:, 8, :]))
                link(v_e.tensor_tensor(gt[:, 11, :], gt[:, 10, :], gt[:, 10, :], ALU.mult))
                link(v_e.tensor_tensor(gt[:, 11, :], gt[:, 11, :], mv2[:, :, 1], ALU.mult))
                v_e.tensor_scalar(gt[:, 8, :], gt[:, 11, :], 1e-5, None, ALU.add).then_inc(mvar_ready, 1)
                dve.wait_ge(qk_ln, 1)
                refine(qs[:, 2, :], qs[:, 1, :], qs[:, 3, :])
                link(v_e.tensor_scalar(qs[:, 4, :], qs[:, 2, :], float(DA) ** -0.5, None, ALU.mult))
                for t in range(NT):
                    v = k_raw[:, t, :].rearrange("p (h d) -> p h d", h=AH)
                    v_e.tensor_tensor(v, v, qs[:, 2, 32 + 8 * t:40 + 8 * t].unsqueeze(2).to_broadcast((P, AH, DA)),
                                      ALU.mult).then_inc(k_norm, 1)

            def hb_part():
                dve.wait_ge(mln_ready, 1)
                refine(gt[:, 9, :], gt[:, 8, :], gt[:, 11, :])
                link(v_e.tensor_tensor(gt[:, 10, :], gt[:, 10, :], gt[:, 9, :], ALU.mult))
                for n in range(16):
                    last = v_e.tensor_scalar(num[:, n, 0:P], num[:, n, 0:P], mv2[:, n, 0:1], gt[:, 10, n:n + 1],
                                             ALU.subtract, ALU.mult)
                last.then_inc(hb_ready, 1)

            def kt_out(p):
                dve.wait_ge(kt_psum, p + 1)
                v_e.tensor_scalar(kt[:, p, :], work[p % 2][:, :], col("k_g", 0), None, ALU.mult).then_inc(kt_ready, 1)

            def yb_out(h):
                dve.wait_ge(hbt_psum, h + 1)
                if h == 0:
                    dve.wait_ge(skip_done, 1)
                v_e.scalar_tensor_tensor(out=xc[:, h, :], in0=work[3][:, :], scalar=col("out_g", h), in1=xc[:, h, :],
                                         op0=ALU.mult, op1=ALU.add).then_inc(yb_part, 1)
                dve.wait_ge(yb_part, h + 1)
                dve.wait_ge(acc_freed_act, 12)
                v_e.tensor_tensor(act[:, 4 + h, :], act[:, 4 + h, :], xc[:, h, :], ALU.mult).then_inc(y_exact, 1)

            def attention(u):
                if u < NU:
                    h, i, e = UNITS[u]
                    n = P * (i + 1)
                    q = 8 * i + h
                    dve.wait_ge(s_psum, u + 1)
                    link(v_e.reduce_max(mx[:, 0, u:u + 1], work[u % 2][:, 0:n], AX_X))
                    v_e.scalar_tensor_tensor(out=mx[:, 1, u:u + 1], in0=mx[:, 0, u:u + 1], scalar=-1.0,
                                             in1=qs[:, 4, q:q + 1], op0=ALU.mult, op1=ALU.mult).then_inc(bias_ready, 1)
                v = u - 1
                if 0 <= v < NU:
                    n = P * (UNITS[v][1] + 1)
                    dve.wait_ge(exp_ready, v + 1)
                    link(v_e.reciprocal(rs[:, 1, v:v + 1], rs[:, 0, v:v + 1]))
                    v_e.tensor_scalar(probs[:, v % 3, 0:n], probs[:, v % 3, 0:n], rs[:, 1, v:v + 1], None,
                                      ALU.mult).then_inc(p_ready, 1)
                v = u - LAG
                if v >= 8 and v % 8 == 0:
                    ya_out(v // 8 - 1)
                if 0 <= v < NU and not PT_ON_ACT(v):
                    h, i, e = UNITS[v]
                    dve.wait_ge(pt_psum, v + 1)
                    v_e.tensor_copy(probs_t[:, e, 0:i + 1, P * i:P * i + P],
                                    work[2][:, 0:P * (i + 1)].rearrange("p (j q) -> p j q", j=i + 1)).then_inc(pt_dve, 1)
                if u in YA_SPLIT:
                    y_lo_part(4 + YA_SPLIT[u])

            def ya_out(p):
                dve.wait_ge(o_psum, p + 1)
                v_e.tensor_tensor(act[:, p, :], work[3][:, :], act[:, p, :], ALU.mult).then_inc(y_exact, 1)

            def y_lo_part(n):
                k = Y_ORDER[n]
                dve.wait_ge(y_hi, n + 1)
                minus(act_lo[:, k, :], act[:, k, :], act_hi[:, k, :]).then_inc(y_ready, 1)

            def residual(w, g, done):
                cc = CHUNKS[HALVES[w][0]][2]
                dve.wait_ge(acc_ready, 4 * (w // 2) + g + 1)
                v_e.tensor_tensor(tmp[:, g, :], acc[g][:, :], gate_bc[:, CH * cc:CH * cc + CH],
                                  ALU.mult).then_inc(acc_freed_dve, 1)
                dve.wait_ge(acc_freed_dve, 4 * sum(n < HALVES[w][0] for n in DVE_CHUNKS) + g + 1)
                if w == 13:
                    dve.wait_ge(x_in[g], 32)
                ins = v_e.tensor_tensor(xres[:, g, CH * cc:CH * cc + CH], xres[:, g, CH * cc:CH * cc + CH],
                                        tmp[:, g, :], ALU.add)
                if done is not None:
                    ins.then_inc(done, 1)

            def x1_norm(t):
                c4 = slice(4 + t, 5 + t)
                dve.wait_ge(ss1_ready, t + 1)
                v_e.tensor_scalar(rms[:, 1, c4], rms[:, 0, c4], 1.0 / D, 1e-6, ALU.mult,
                                  ALU.add).then_inc(var1_ready, 1)
                dve.wait_ge(ln1_ready, t + 1)
                refine(rms[:, 2, c4], rms[:, 1, c4], rms[:, 3, c4])
                if t >= 2:
                    dve.wait_ge(h1_psum, t - 1)
                v_e.tensor_scalar(xn[:, t % 2, :], xres[:, t, :], rms[:, 2, c4], None, ALU.mult).then_inc(xn1_ready, 1)

            def h1_part(t):
                dve.wait_ge(h1_psum, t + 1)
                dve.wait_ge(mod_ready, 8)
                for k in range(KT):
                    v_e.tensor_scalar(act[:, k, P * t:P * t + P], work[k // 4][:, P * (k % 4):P * (k % 4) + P],
                                      gain[:, 1, k:k + 1], mod[:, 1, k:k + 1], ALU.mult, ALU.add).then_inc(h1_exact, 1)

            def h1_lo_part(t):
                dve.wait_ge(h1_hi, t + 1)
                cs = slice(P * t, P * t + P)
                minus(act_lo[:, :, cs], act[:, :, cs], act_hi[:, :, cs]).then_inc(h1_ready, 1)

            def cv_stats(w, g):
                cc = (w - 17) // 2
                dve.wait_ge(acc_freed_act, 24 + 4 * cc + g + 1)
                ins = v_e.bn_stats(st6[:, 2 * g + cc, :], vg[:, g, CH * cc:CH * cc + CH])
                if cc:
                    link(ins)
                    ins = v_e.bn_aggr(mv2[:, g, :], st6[:, 2 * g:2 * g + 2, :].rearrange("p a b -> p (a b)"))
                    link(ins)

            def cv_norm():
                v_e.tensor_scalar(rms[:, 1, 0:4], mv2[:, 0:4, 1], 1e-5, None, ALU.add).then_inc(cvar_ready, 1)
                dve.wait_ge(cln_ready, 1)
                refine(rms[:, 2, 0:4], rms[:, 1, 0:4], rms[:, 3, 0:4])
                for t in range(NT):
                    v_e.tensor_scalar(vg[:, t, :], vg[:, t, :], mv2[:, t, 0:1], rms[:, 2, t:t + 1], ALU.subtract,
                                      ALU.mult).then_inc(vn_ready, 1)

            def spatial_out(g):
                dve.wait_ge(sg_psum, g + 1)
                t3 = probs[:, g % 3, :].rearrange("p (t q) -> p t q", t=NT)
                link(v_e.scalar_tensor_tensor(out=t3, in0=work[g % 3][:, :].rearrange("p (t q) -> p t q", t=NT),
                                              scalar=col("c_ln_g", g),
                                              in1=sg_add[:, g:g + 1, :].to_broadcast((P, NT, P)), op0=ALU.mult,
                                              op1=ALU.add))
                dve.wait_ge(acc_freed_act, 32 + g + 1)
                v_e.tensor_tensor(act[:, g, :], act[:, g, :], probs[:, g % 3, :], ALU.mult).then_inc(us_ready, 1)

            def z_out(n):
                dve.wait_ge(acc_freed_act, 40 + n + 1)
                dve.wait_ge(us_ready, n + 1)
                v_e.tensor_tensor(act[:, n, :], act[:, n, :], tmp[:, n % 4, :], ALU.mult).then_inc(z1_exact, 1)

            def z1_lo_part(k):
                dve.wait_ge(z1_hi, k + 1)
                minus(act_lo[:, k, :], act[:, k, :], act_hi[:, k, :]).then_inc(z1_ready, 1)

            at((0, 0), wvt_out)
            at((0, 3), eff_out)
            for g in range(4):
                at((1, g), lambda g=g: conv_tap(0, g))
                at((7, g), lambda g=g: square_sums(g))
                at((9, g), lambda g=g: square_sums(4 + g))
                at((11, g), lambda g=g: yb_out(g))
                at((13, g), lambda g=g: residual(13, g, None))
                at((17, g), lambda g=g: cv_stats(17, g))
                at((19, g), lambda g=g: cv_stats(19, g))
                at((22, g), lambda g=g: spatial_out(g))
                at((24, g), lambda g=g: spatial_out(4 + g))
                at((25, g), lambda g=g: z_out(g))
                at((27, g), lambda g=g: z_out(4 + g))
                at((29, g), lambda g=g: residual(29, g, out_ready))
                at((31, g), lambda g=g: residual(31, g, out_ready))
            for j in range(1, 4):
                for h in range(MH):
                    at((1, 3), lambda j=j, h=h: conv_tap(j, h))
            at((4, 0), skip_part)
            at((4, 1), gates_add)
            at((6, 0), log_forget)
            at((6, 1), a_cols)
            at((6, 2), running_max)
            at((6, 3), m_exponent)
            for h in range(MH):
                s0 = 28 + 3 * h
                at((s0 // 4, s0 % 4), lambda h=h: weights(h, 0))
                at(((s0 + 1) // 4, (s0 + 1) % 4), lambda h=h: weights(h, 1))
                at(((s0 + 2) // 4, (s0 + 2) % 4), lambda h=h: head_stats(h))
            at((10, 0), norms)
            at((10, 1), hb_part)
            for p in range(4):
                at((10, 2 + p // 2), lambda p=p: kt_out(p))
            for slot, us in ATT_SLOTS.items():
                if slot == (12, -1):
                    for n in range(4):
                        at((11, 3), lambda n=n: y_lo_part(n))
                for u in us:
                    at(slot, lambda u=u: attention(u))
            for t in range(3):
                at((15, t), lambda t=t: residual(15, t, x1_ready))
                at((15, t), lambda t=t: x1_norm(t))
            at((15, 2), lambda: h1_part(0))
            at((15, 2), lambda: h1_lo_part(0))
            at((15, 3), lambda: residual(15, 3, x1_ready))
            at((15, 3), lambda: h1_part(1))
            at((15, 3), lambda: x1_norm(3))
            at((15, 3), lambda: h1_lo_part(1))
            for t in (2, 3):
                at((16, t - 2), lambda t=t: h1_part(t))
                at((16, t - 2), lambda t=t: h1_lo_part(t))
            at((20, 0), cv_norm)
            for n in range(4, 12):
                at(ADA_USE_SLOT[n], lambda n=n: (mod_out(n) if n in MOD_ITEMS else gate_out(n)))
            for k in range(KT):
                at((27, 3), lambda k=k: z1_lo_part(k))
            for w in range(NHALF):
                if w == 12:
                    for job in todo.get((w, -1), []):
                        job()
                if w + 1 < NHALF:
                    split_lo(w + 1)
                for g in range(4):
                    for job in todo.get((w, g), []):
                        job()


_INS = ["x", "c", "ln_g", "ada_w", "ada_b", "w_in", "w_out", "a_q_g", "a_k_g", "b_conv_w", "b_conv_b", "b_wq", "b_wk",
        "b_wv", "b_w_gates", "b_b_gates", "b_out_g", "b_skip", "c_ln_g", "c_ln_b", "c_ws", "c_bs"]


def kernel(**inputs):
    import numpy as _np
    import concourse.bacc as _bacc
    from concourse import mybir as _mybir
    from concourse.bass_utils import run_bass_kernel_spmd as _run

    nc = _bacc.Bacc("TRN2", target_bir_lowering=False, num_devices=1)
    arrays, args = {}, []
    for name in _INS:
        a = _np.ascontiguousarray(inputs[name])
        arrays[f"in_{name}_dram"] = a
        args.append(nc.dram_tensor(f"in_{name}_dram", a.shape, _mybir.dt.from_np(a.dtype), kind="ExternalInput").ap())
    args.append(nc.dram_tensor("out_0_dram", (1, T, D), _mybir.dt.float32, kind="ExternalOutput").ap())
    build(nc, *args)
    r = _run(nc, [arrays], core_ids=[0])
    return r.results[0]["out_0_dram"]
```

```python
from contextlib import ExitStack

import concourse.bass as bass
from concourse import mybir

F32 = mybir.dt.float32
F32R = mybir.dt.float32r
BF16 = mybir.dt.bfloat16
ALU = mybir.AluOpType
ACT = mybir.ActivationFunctionType
AX_X = mybir.AxisListType.X

P = 128
D = 1024
T = 512
KT = D // P
NT = T // P
CH = 512
KH = 4
AH = 8
DA = 64
MH = 4
VP = 130
NEG = -1e30
RAW = 3
SPLIT = 2
L1 = 16
PARTS = 2
LNEXP = "natural_log_exp_and_others"

CHUNKS = [
    ("in", 0, 4, (0, 1), "feature", "bx"), ("in", 0, 5, (0, 1), "feature", "bz"),
    ("in", 0, 0, (0, 1), "token", "aq"), ("in", 0, 1, (0, 1), "token", "ak"),
    ("in", 0, 2, (0, 1), "token", "av"), ("in", 0, 3, (1, 0), "feature", "az"),
    ("out", 0, 0, (1, 0), "token", "y0"), ("out", 0, 1, (1, 0), "token", "y0"),
    ("in", 1, 2, (0, 1), "token", "cv"), ("in", 1, 3, (0, 1), "token", "cv"),
    ("in", 1, 0, (0, 1), "feature", "cu"), ("in", 1, 1, (0, 1), "feature", "cu"),
    ("in", 1, 4, (0, 1), "feature", "cz"), ("in", 1, 5, (0, 1), "feature", "cz"),
    ("out", 1, 0, (0, 1), "token", "y1"), ("out", 1, 1, (0, 1), "token", "y1"),
]
BX, BZ, AQ, AK, AV, AZ, Y0, CV, CU, CZ = 0, 1, 2, 3, 4, 5, 6, 8, 10, 12
HALVES = [(c, kh) for c in range(len(CHUNKS)) for kh in CHUNKS[c][3]]
NHALF = len(HALVES)
ADA_FIRST = [(0, 2), (0, 3), (0, 0), (0, 1)]
ADA_LATER = [(0, 4), (0, 5), (1, 2), (1, 3), (1, 0), (1, 1), (1, 4), (1, 5)]
ADA = ADA_FIRST + ADA_LATER
GATE_ITEMS = [n for n, (_, cc) in enumerate(ADA) if cc >= 4]
MOD_ITEMS = [n for n, (_, cc) in enumerate(ADA) if cc < 4]
ADA_LANDS = {4: 2, 5: 3, 6: 4, 7: 6, 8: 10, 9: 11, 10: 14, 11: 16}
ADA_MUL = (0, 1)
ADA_USE_SLOT = {4: (2, 2), 5: (4, 2), 6: (5, 3), 7: (7, 1), 8: (13, 0), 9: (13, 1), 10: (17, 1), 11: (19, 0)}




PLACES = {
    "spatial weights": (0, 0), "ln_b sums": (0, 2), "wv transposes": (0, 3), "gate fold": (1, 0),
    "mLSTM values": ((2, 0), (2, 1), (2, 2), (2, 3)),
    "mLSTM q, k": ((3, 0), (3, 0), (3, 1), (3, 2), (3, 2), (3, 2), (3, 3), (3, 3)),
    "skip": (3, 3), "gates": (4, 0), "gate columns": (4, 1), "gate logs": (4, 1), "running sums": (4, 2),
    "running max": (5, 0), "max columns": (5, 3),
    "q, k norms": (7, 3), "mLSTM norms": (8, 3), "mLSTM normalised": (9, 0),
    "q, k transposes": ((8, 3), (8, 3), (8, 3), (8, 3), (9, 0), (9, 0), (9, 0), (9, 0)),
    "mLSTM outputs": ((9, 3), (9, 3), (9, 3), (10, 0)),
    "spatial": ((21, 3), (22, 1), (22, 1), (22, 2), (23, 2), (23, 3), (24, 1), (24, 2)),
}


def plan_stream():
    stream = [("ada", n) for n in range(2 * len(ADA_FIRST))]
    stream.insert(4, ("w", 0))
    for w in range(1, NHALF):
        stream.append(("w", w))
        for n, after in ADA_LANDS.items():
            if after == w:
                stream += [("ada", 2 * n), ("ada", 2 * n + 1)]
    return stream


STREAM = plan_stream()
PLACE = {item: n for n, item in enumerate(STREAM)}

ROWS = {}
for _name, _rows in (("ada_b", 48), ("ln_g", 16), ("conv_w", 16), ("conv_b", 4), ("out_g", 4),
                     ("skip", 4), ("c_ln_g", 8), ("q_g", 1), ("k_g", 1)):
    ROWS[_name] = (sum(r for _, r in ROWS.values()), _rows)
NROWS = sum(r for _, r in ROWS.values())

UNITS = [(2 * p + e, i, e) for p in range(AH // 2) for i in range(NT) for e in range(2)]
NU = len(UNITS)
S_ORDER = (0, 1, 3, 2)
PAD = 256


def PT_ON_ACT(u):
    return UNITS[u][1] == 3


LAG = 2
ATT_SLOTS = {}
_u = 0
for _slot, _n in zip([(9, 1), (9, 2), (9, 3)] + [(w, g) for w in (10, 11, 12) for g in range(4)][:11],
                     (2, 2, 2, 3, 3, 2, 3, 2, 2, 2, 3, 3, 3, 3)):
    ATT_SLOTS[_slot] = list(range(_u, _u + _n))
    _u += _n
assert _u == NU + LAG + 1
O_FIRST = 2
HEAD_SLOT = 24
YA_SPLIT = {8 * p + 9 + LAG: p for p in range(2, 3)} | {NU + LAG: 3}
Y_ORDER = (4, 5, 6, 7, 0, 1, 2, 3)


def build(nc, x, c, ln_g, ada_w, ada_b, w_in, w_out, a_q_g, a_k_g, b_conv_w, b_conv_b, b_wq, b_wk, b_wv,
          b_w_gates, b_b_gates, b_out_g, b_skip, c_ln_g, c_ln_b, c_ws, c_bs, out):
    with ExitStack() as ctx:
        def sb(name, shape, dt=F32):
            return ctx.enter_context(nc.sbuf_tensor(name, shape, dt))

        def sem(name):
            return ctx.enter_context(nc.semaphore(name))

        acc = [ctx.enter_context(nc.psum_tensor(f"acc{g}", [P, 512], F32)) for g in range(4)]
        work = [ctx.enter_context(nc.psum_tensor(f"work{g}", [P, 512], F32)) for g in range(4)]

        raw = sb("raw", [P, RAW, KH, CH])
        w_hi = sb("w_hi", [P, SPLIT, KH, CH], F32R)
        w_lo = sb("w_lo", [P, SPLIT, KH, CH], F32R)
        act_hi = sb("act_hi", [P, KT, T], F32R)
        act_lo = sb("act_lo", [P, KT, T], F32R)
        act = sb("act", [P, KT, T])
        xres = sb("xres", [P, NT, D])
        xc = sb("xc", [P, MH, T])
        conv = sb("conv", [P, MH, T])
        late = sb("late", [P, 2 * NT * MH * VP])
        wts = sb("wts", [P, 1280])
        probs = sb("probs", [P, 3, T])
        gate_bc = sb("gate_bc", [P, D])
        ada_row = sb("ada_row", [P, 2, CH])
        ident = sb("ident", [P, P])
        ident_bf = sb("ident_bf", [P, P], BF16)
        causal_bf = sb("causal_bf", [P, P], BF16)
        upper = sb("upper", [P, P])
        ones = sb("ones", [P, P])
        head_sel = sb("head_sel", [P, MH, P])
        gate_sel = sb("gate_sel", [P, 8])
        cols = sb("cols", [P, NROWS])
        c_pad = sb("c_pad", [P, KT, 32])
        mod = sb("mod", [P, 2, 16])
        gain = sb("gain", [P, 2, 8])
        bg_bc = sb("bg_bc", [P, 8])
        wm = sb("wm", [P, 8, P])
        sg_add = sb("sg_add", [P, 8, P])
        neg_m = sb("neg_m", [P, T])
        rms = sb("rms", [P, 4, 8])
        gt = sb("gt", [P, 12, 16])
        pre = sb("pre", [P, NT, 4])
        st6 = sb("st6", [P, 16, 6])
        mv2 = sb("mv2", [P, 16, 2])
        qs = sb("qs", [P, 5, 64])
        mx = sb("mx", [P, 2, NU])
        rs = sb("rs", [P, 2, NU])
        with nc.sbuf_tensor("mid", [P, 4160], F32) as mid:
            pass
        third = sb("third", [P, 2, KH, CH], F32R)
        vals = late[:, 0:NT * MH * VP]
        num = late[:, NT * MH * VP:].rearrange("p (n v) -> p n v", v=VP)
        vg = late[:, 0:4096].rearrange("p (t n) -> p t n", t=NT)
        wbd = mid[:, 2064:2064 + 1536].rearrange("p (m h c) -> p m h c", m=3, h=4)
        bx = mid[:, 0:4 * 515].rearrange("p (h t) -> p h t", h=4)
        k_raw = mid[:, 0:2048].rearrange("p (t n) -> p t n", t=NT)
        q_raw = mid[:, 2064:2064 + 2048].rearrange("p (t n) -> p t n", t=NT)
        probs_t = mid[:, 0:4096].rearrange("p (e j q) -> p e j q", e=2, j=NT)
        mq = xres[:, 0:2, :].rearrange("p a (b t) -> p (a b) t", b=2)
        mk = xres[:, 2:4, :].rearrange("p a (b t) -> p (a b) t", b=2)
        qt = xres[:, :, :].rearrange("p a (b t) -> p (a b) t", b=2)
        kt = conv
        mvals = vals[:, :].rearrange("p (t h v) -> p t h v", t=NT, h=MH)
        avals = vals[:, 0:2048].rearrange("p (t n) -> p t n", t=NT)
        wvt = wts[:, 0:512].rearrange("p (h c) -> p h c", h=4)
        ws_raw = num[:, 0:8, 0:P]
        lnb_bc = vals[:, 0:1024]
        bs_bc = gate_bc[:, :].rearrange("p (g t) -> p g t", g=8)
        expw = probs[:, :, :].rearrange("p a b -> p (a b)")
        xn = xc[:, :, :].rearrange("p (a b) t -> p a (b t)", a=2)
        gates_t = conv[:, 3, :]
        run = probs[0:4, :, :].rearrange("p a t -> p (a t)").rearrange("p (b n) -> p b n", b=2)
        rows = probs[:, 2, 0:P]
        c_row = conv[0:KT, 0, 0:P]
        block_diag = wts[:, 512:640].rearrange("p (b o) -> p b o", o=4)
        wqkv = wts[:, 640:688].rearrange("p (m h o) -> p m h o", m=3, h=4)
        wg_pad = num[:, :, :].rearrange("p a b -> p (a b)")[:, 1040:1424].rearrange("p (b r) -> p b r", r=32)
        tmp = conv
        OFF = [0, 512, 896, 1152]

        def col(name, n, k=1):
            r = ROWS[name][0] + n
            return cols[:, r:r + k]

        raw_in = [sem(f"raw_in{s}") for s in range(RAW)]
        ada_mult, ada_used = sem("ada_mult"), sem("ada_used")
        w_hi_ready, w_lo_ready = sem("w_hi_ready"), sem("w_lo_ready")
        even_half_done, acc_ready = sem("even_half_done"), sem("acc_ready")
        acc_freed_act, acc_freed_dve = sem("acc_freed_act"), sem("acc_freed_dve")
        rows_in, x_in, small_in, ws_in, wg_in = (sem("rows_in"), [sem(f"x_in{t}") for t in range(NT)],
                                                 sem("small_in"), sem("ws_in"), sem("wg_in"))
        consts, pool_step, dve_step, act_step = sem("consts"), sem("pool_step"), sem("dve_step"), sem("act_step")
        pool_prep = sem("pool_prep")
        rows_in_pool = sem("rows_in_pool")
        rows_t, cols_ready = sem("rows_t"), sem("cols_ready")
        c_in, c_psum, c_ready = sem("c_in"), sem("c_psum"), sem("c_ready")
        ss_ready, ln_ready, xn_ready = sem("ss_ready"), sem("ln_ready"), sem("xn_ready")
        var_ready = sem("var_ready")
        xt_psum, xt_evac = sem("xt_psum"), sem("xt_evac")
        wm_psum, wm_evac, sg_psum0, sg_ready = sem("wm_psum"), sem("wm_evac"), sem("sg_psum0"), sem("sg_ready")
        ada_evac, modc_psum, mod_ready = sem("ada_evac"), sem("modc_psum"), sem("mod_ready")
        gate_b_in, gate_psum, gate_ready = sem("gate_b_in"), sem("gate_psum"), sem("gate_ready")
        h_exact, h_hi, h_ready = sem("h_exact"), sem("h_hi"), sem("h_ready")
        conv_step, xc_ready = sem("conv_step"), sem("xc_ready")
        wvt_psum, wvt_ready, eff_psum, eff_ready = (sem("wvt_psum"), sem("wvt_ready"), sem("eff_psum"),
                                                    sem("eff_ready"))
        mv_psum, mv_evac, mqk_psum, mqk_evac = sem("mv_psum"), sem("mv_evac"), sem("mqk_psum"), sem("mqk_evac")
        skip_done = sem("skip_done")
        g_psum, g_evac, gt_psum, gt_abs, gt_ln, lf_ready = (sem("g_psum"), sem("g_evac"), sem("gt_psum"),
                                                            sem("gt_abs"), sem("gt_ln"), sem("lf_ready"))
        cum_psum, a_ready, at_psum, m_rows, mc_psum, mc_ready, guard_ready = (
            sem("cum_psum"), sem("a_ready"), sem("at_psum"), sem("m_rows"), sem("mc_psum"), sem("mc_ready"),
            sem("guard_ready"))
        mb_psum, mexp, st_psum, wt_mult, wt_ready, pv_psum, num_evac = (
            sem("mb_psum"), sem("mexp"), sem("st_psum"), sem("wt_mult"), sem("wt_ready"), sem("pv_psum"),
            sem("num_evac"))
        hb_ready, hbt_psum, yb_part = sem("hb_ready"), sem("hbt_psum"), sem("yb_part")
        q_evac, k_evac, qk_ss, qk_ln, k_norm = (sem("q_evac"), sem("k_evac"), sem("qk_ss"),
                                                        sem("qk_ln"), sem("k_norm"))
        sq_used = sem("sq_used")
        qt_zero, qt_psum, kt_psum, qt_ready, kt_ready = (sem("qt_zero"), sem("qt_psum"), sem("kt_psum"),
                                                         sem("qt_ready"), sem("kt_ready"))
        s_psum, bias_ready, exp_ready, p_ready, pt_psum, pt_dve, pt_act, o_psum = (
            sem("s_psum"), sem("bias_ready"), sem("exp_ready"), sem("p_ready"), sem("pt_psum"), sem("pt_dve"),
            sem("pt_act"), sem("o_psum"))
        mvar_ready, mln_ready = sem("mvar_ready"), sem("mln_ready")
        az_exp, az_den, az_rec, o_evac = sem("az_exp"), sem("az_den"), sem("az_rec"), sem("o_evac")
        y_exact, y_hi, y_ready = sem("y_exact"), sem("y_hi"), sem("y_ready")
        h1_exact_act = sem("h1_exact_act")
        x1_ready, h1_psum, h1_exact, h1_hi, h1_ready = (sem("x1_ready"), sem("h1_psum"), sem("h1_exact"),
                                                        sem("h1_hi"), sem("h1_ready"))
        ss1_ready, var1_ready, ln1_ready, xn1_ready = (sem("ss1_ready"), sem("var1_ready"), sem("ln1_ready"),
                                                       sem("xn1_ready"))
        cvar_ready, cln_ready, vn_ready = (sem("cvar_ready"), sem("cln_ready"),
                                                     sem("vn_ready"))
        sg_psum, us_ready = (sem("sg_psum"), sem("us_ready"))
        z1_exact, z1_hi, z1_ready = sem("z1_exact"), sem("z1_hi"), sem("z1_ready")
        out_ready, stored = sem("out_ready"), sem("stored")

        w_views = {"in": [w_in[l].rearrange("(k p) n -> p k n", p=P) for l in range(2)],
                   "out": [w_out[l].rearrange("(k p) n -> p k n", p=P) for l in range(2)]}
        ada_views = [ada_w[l].rearrange("(k p) n -> p k n", p=P) for l in range(2)]
        x_view = x[0].rearrange("(t p) d -> p t d", p=P)
        out_view = out[0].rearrange("(t p) d -> p t d", p=P)

        def landed(eng, item):
            n = PLACE[item]
            eng.wait_ge(raw_in[n % RAW], 16 * (n // RAW + 1))
            return n % RAW

        def half_done(eng, w):
            if w % 2:
                eng.wait_ge(acc_ready, 4 * (w // 2) + 4)
            else:
                eng.wait_ge(even_half_done, w // 2 + 1)

        def split_slot(w):
            s = w % SPLIT if w < L1 else (w + 1) % 3
            if s == SPLIT:
                return third[:, 0, :, :], third[:, 1, :, :]
            return w_hi[:, s, :, :], w_lo[:, s, :, :]

        def split_free(eng, w):
            if w == L1:
                eng.wait_ge(o_psum, 4)
            elif w == L1 + 1:
                half_done(eng, w - 3)
            elif w >= SPLIT:
                half_done(eng, w - (SPLIT if w < L1 else SPLIT + 1))

        DVE_CHUNKS = [n for n, ch in enumerate(CHUNKS) if ch[5] in ("az", "y0", "y1")]

        def acc_free(eng, chunk, g):
            before = sum(n < chunk for n in DVE_CHUNKS)
            if chunk in DVE_CHUNKS:
                eng.wait_ge(acc_freed_dve, 4 * before + g + 1)
            else:
                eng.wait_ge(acc_freed_act, 4 * (chunk - before) + g + 1)

        def what(w):
            return CHUNKS[HALVES[w][0]][5]

        block = ctx.enter_context(nc.Block())

        @block.sync
        def _(sp):
            for t in range(NT):
                sp.dma_start(xres[:, t, :], x_view[:, t, :]).then_inc(x_in[t], 16)
            for n, (kind, m) in enumerate(STREAM):
                if n >= RAW:
                    before = STREAM[n - RAW]
                    if before[0] == "ada":
                        sp.wait_ge(ada_used, before[1] + 1)
                    else:
                        sp.wait_ge(w_lo_ready, PARTS * (before[1] + 1))
                if kind == "ada":
                    layer, cc = ADA[m // 2]
                    src = ada_views[layer][:, KH * (m % 2):KH * (m % 2) + KH, CH * cc:CH * cc + CH]
                else:
                    chunk, kh = HALVES[m]
                    mat, layer, cc = CHUNKS[chunk][:3]
                    src = w_views[mat][layer][:, KH * kh:KH * kh + KH, CH * cc:CH * cc + CH]
                sp.dma_start(raw[:, n % RAW, :, :], src).then_inc(raw_in[n % RAW], 16)
            for cc in range(2):
                for t in range(NT):
                    sp.wait_ge(out_ready, 4 * cc + t + 1)
                    sp.dma_start(out_view[:, t, CH * cc:CH * cc + CH],
                                 xres[:, t, CH * cc:CH * cc + CH]).then_inc(stored, 16)
            sp.wait_ge(stored, 16 * 8)

        @block.gpsimd
        def _(pool):
            count = [0]

            def link(ins):
                count[0] += 1
                ins.then_inc(pool_step, 1)
                pool.wait_ge(pool_step, count[0])

            link(pool.memset(ident[:], 0.0))
            pool.affine_select(out=ident[:], in_=ident[:], compare_op=ALU.not_equal, fill=1.0, base=0,
                               pattern=[[-1, P]], channel_multiplier=1).then_inc(consts, 1)
            link(pool.memset(c_pad[:], 0.0))
            pool.memset(ones[:], 1.0).then_inc(consts, 1)
            for name, a in (("conv_w", b_conv_w[0]), ("conv_b", b_conv_b), ("out_g", b_out_g), ("skip", b_skip),
                            ("c_ln_g", c_ln_g)):
                r, n = ROWS[name]
                pool.dma_start(rows[r:r + n, :], a.rearrange("l (j f) -> (l j) f", f=P)).then_inc(rows_in_pool, 16)
            for name, a in (("q_g", a_q_g), ("k_g", a_k_g)):
                r = ROWS[name][0]
                for e in range(2):
                    pool.dma_start(rows[r:r + 1, DA * e:DA * e + DA], a).then_inc(rows_in_pool, 16)
            link(pool.memset(ident_bf[:], 0.0))
            pool.affine_select(out=ident_bf[:], in_=ident_bf[:], compare_op=ALU.not_equal, fill=1.0, base=0,
                               pattern=[[-1, P]], channel_multiplier=1).then_inc(consts, 1)
            link(pool.memset(causal_bf[:], 0.0))
            pool.affine_select(out=causal_bf[:], in_=causal_bf[:], compare_op=ALU.is_ge, fill=NEG, base=0,
                               pattern=[[-1, P]], channel_multiplier=1).then_inc(consts, 1)
            link(pool.memset(upper[:], 1.0))
            pool.affine_select(out=upper[:], in_=upper[:], compare_op=ALU.is_ge, fill=0.0, base=0,
                               pattern=[[1, P]], channel_multiplier=-1).then_inc(consts, 1)
            link(pool.memset(wg_pad, 0.0))
            landed(pool, ("ada", 2 * len(ADA_FIRST) - 2))
            pool.dma_start(wg_pad[:, :, 0:8], b_w_gates[0].rearrange("(b p) r -> p b r", p=P)).then_inc(wg_in, 16)
            pool.dma_start(ws_raw, c_ws[0].rearrange("g t s -> t g s")).then_inc(ws_in, 16)
            pool.dma_start(lnb_bc, c_ln_b[0:1, :].to_broadcast((P, D))).then_inc(small_in, 16)
            pool.dma_start(gate_bc[:, :], c_bs[0:1].rearrange("a g t -> a (g t)").to_broadcast((P, D))).then_inc(small_in, 16)
            pool.dma_start(bg_bc[:, :], b_b_gates[0:1, :].to_broadcast((P, 8))).then_inc(small_in, 16)
            for m, w in enumerate((b_wq, b_wk, b_wv)):
                pool.dma_start(wqkv[:, m, :, :],
                               w[0].rearrange("(h b) i o -> (b i) h o", h=4)).then_inc(small_in, 16)
            pool.wait_ge(ws_in, 16)
            pool.affine_select(out=ws_raw, in_=ws_raw, compare_op=ALU.is_ge, fill=0.0, base=0,
                               pattern=[[0, 8], [-1, P]], channel_multiplier=1).then_inc(pool_prep, 1)
            link(pool.memset(block_diag, 1.0))
            link(pool.affine_select(out=block_diag, in_=block_diag, compare_op=ALU.is_ge, fill=0.0, base=0,
                                    pattern=[[-4, 32], [0, 4]], channel_multiplier=1))
            link(pool.affine_select(out=block_diag, in_=block_diag, compare_op=ALU.is_ge, fill=0.0, base=3,
                                    pattern=[[4, 32], [0, 4]], channel_multiplier=-1))
            pool.wait_ge(small_in, 16 * 6)
            for m in (2, 0, 1):
                for h in range(4):
                    last = pool.tensor_tensor(
                        wbd[:, m, h, :].rearrange("p (b o) -> p b o", o=4),
                        wqkv[:, m, h:h + 1, :].to_broadcast((P, 32, 4)), block_diag, ALU.mult)
                last.then_inc(pool_prep, 1)
            for h in range(MH):
                last = pool.memset(bx[:, h, 0:3], 0.0)
            last.then_inc(pool_prep, 1)
            link(pool.memset(head_sel[:], 0.0))
            pool.affine_select(out=head_sel[:], in_=head_sel[:], compare_op=ALU.not_equal, fill=1.0, base=0,
                               pattern=[[-1, MH], [0, P]], channel_multiplier=1).then_inc(pool_prep, 1)
            link(pool.memset(gate_sel[:], 0.0))
            for g in range(4):
                link(pool.affine_select(out=gate_sel[:], in_=gate_sel[:], compare_op=ALU.not_equal, fill=1.0,
                                        base=-32 * g, pattern=[[-1, 8]], channel_multiplier=1))
            pool.wait_ge(sg_psum0, 8)
            pool.memset(mvals[:, :, :, P:P + 1], 1.0).then_inc(pool_prep, 1)
            pool.memset(neg_m[:], 0.0).then_inc(pool_prep, 1)
            pool.wait_ge(cols_ready, 1)
            pool.memset(run[:, :, 0:PAD], 0.0).then_inc(pool_prep, 1)

            def gate_bias(layer):
                pool.dma_start(gate_bc[:, :], ada_b[layer:layer + 1, 2 * D:3 * D].to_broadcast((P, D))).then_inc(gate_b_in, 16)

            def ada_sum(n):
                row = ada_row[:, n % 2, :]
                m = n - 2
                if m in GATE_ITEMS:
                    pool.wait_ge(gate_psum, GATE_ITEMS.index(m) + 1)
                else:
                    pool.wait_ge(modc_psum, MOD_ITEMS.index(m) + 1)
                for kh in range(2):
                    s = landed(pool, ("ada", 2 * n + kh))
                    pool.wait_ge(ada_mult, 2 * (n - len(ADA_FIRST)) + kh + 1)
                    link(pool.tensor_tensor(raw[:, s, 0:2, :], raw[:, s, 0:2, :], raw[:, s, 2:4, :], ALU.add))
                    if kh:
                        link(pool.tensor_tensor(row, row, raw[:, s, 0, :], ALU.add))
                        pool.tensor_tensor(row, row, raw[:, s, 1, :], ALU.add).then_inc(ada_used, 1)
                    else:
                        pool.tensor_tensor(row, raw[:, s, 0, :], raw[:, s, 1, :], ALU.add).then_inc(ada_used, 1)
                        pool.wait_ge(ada_used, 2 * n + 1)

            pool.wait_ge(sg_ready, 2)
            gate_bias(0)
            ada_sum(4)

            ada_sum(5)
            ada_sum(6)
            ada_sum(7)

            for h in range(MH):
                for n, s in enumerate(S_ORDER):
                    pool.wait_ge(wt_mult, NT * h + n + 1)
                    blk = wts[:, OFF[s]:OFF[s] + P]
                    pool.affine_select(out=blk, in_=blk, compare_op=ALU.is_ge, fill=0.0, base=0,
                                       pattern=[[1, P]], channel_multiplier=-1).then_inc(wt_ready, 1)
            pool.wait_ge(st_psum, 4 * MH)
            pool.wait_ge(wt_ready, NT * MH)
            for e in range(2):
                if e:
                    pool.wait_ge(qt_zero, 1)
                pool.memset(xres[64 - 64 * e:P - 64 * e, :, CH * e:CH * e + CH], 0.0).then_inc(qt_zero, 1)
            ada_sum(8)
            ada_sum(9)
            ada_sum(10)
            acc_free(pool, Y0 + 1, 3)
            gate_bias(1)
            ada_sum(11)

        @block.tensor
        def _(pe):
            def group(w, g):
                chunk, kh = HALVES[w]
                layout, name = CHUNKS[chunk][4:6]
                first = kh == CHUNKS[chunk][3][0]
                if first and chunk:
                    acc_free(pe, chunk - 1, g)
                hi, lo = split_slot(w)
                for i in range(KH):
                    k = KH * kh + i
                    if g == 0 and i % 2 == 0:
                        pe.wait_ge(w_lo_ready, PARTS * w + i // 2 + 1)
                    if name in ("bx",) and g == 0:
                        pe.wait_ge(h_ready, k + 1)
                    if name == "y0" and chunk == 6 and g == 0:
                        pe.wait_ge(y_ready, (k - KH if kh else k + KH) + 1)
                    if name == "cv" and chunk == 8 and i == 0 and kh == 0:
                        pe.wait_ge(h1_ready, g + 1)
                    if name == "y1" and chunk == 14 and g == 0:
                        pe.wait_ge(z1_ready, k + 1)
                    parts = [(hi, act_hi), (hi, act_lo), (lo, act_hi)]
                    if layout == "token":
                        parts = [(hi, act_hi), (lo, act_hi), (hi, act_lo)]
                    for n, (wp, ap) in enumerate(parts):
                        if layout == "feature":
                            lhsT, rhs = wp[:, i, P * g:P * g + P], ap[:, k, :]
                        else:
                            lhsT, rhs = ap[:, k, P * g:P * g + P], wp[:, i, :]
                        last = pe.matmul(acc[g][:, :], lhsT, rhs, start=first and i == 0 and n == 0,
                                         stop=not first and i == KH - 1 and n == 2)
                if not first:
                    last.then_inc(acc_ready, 1)
                elif g == 3:
                    last.then_inc(even_half_done, 1)

            def ada_pair(n, bank):
                for kh in range(2):
                    s = landed(pe, ("ada", 2 * n + kh))
                    for j in range(4):
                        last = pe.matmul(bank[32 * j:32 * j + 32, :], c_pad[:, KH * kh + j, :], raw[:, s, j, :],
                                         start=kh == 0, stop=kh == 1, tile_position=(0, 32 * j))
                        if j == 3 and kh == 0:
                            last.then_inc(ada_used, 1)
                last.then_inc(ada_used, 1)

            def mod_cols(n, bank):
                pe.wait_ge(*((ada_evac, n + 1) if n < 4 else (ada_used, 2 * n + 2)))
                for q in range(4):
                    last = pe.matmul(bank[:, q:q + 1], ada_row[:, n % 2, P * q:P * q + P], ones[:, 0:1],
                                     start=True, stop=True)
                last.then_inc(modc_psum, 1)

            def gate_row(n, bank):
                pe.wait_ge(*((ada_evac, n + 1) if n < 4 else (ada_used, 2 * n + 2)))
                pe.matmul(bank[:, :], ones[:, :], ada_row[:, n % 2, :], start=True, stop=True).then_inc(gate_psum, 1)

            pe.wait_ge(consts, 2)
            pe.wait_ge(c_in, 16)
            pe.transpose(work[2][:, 0:KT], c_row, ident[0:KT, 0:KT]).then_inc(c_psum, 1)
            pe.wait_ge(c_ready, 1)
            ada_pair(0, work[2])
            for t in range(NT):
                if t == NT - 1:
                    ada_pair(1, work[3])
                pe.wait_ge(xn_ready, t + 1)
                for hf in range(2):
                    n = 2 * t + hf
                    if n >= 4:
                        pe.wait_ge(xt_evac, n - 3)
                    for q in range(4):
                        k = 4 * hf + q
                        last = pe.transpose(acc[n % 4][:, P * q:P * q + P], xres[:, t, P * k:P * k + P], ident[:, :])
                    last.then_inc(xt_psum, 1)
            pe.wait_ge(rows_in, 16 * 2)
            pe.wait_ge(rows_in_pool, 16 * 9)
            pe.transpose(work[0][:, 0:NROWS], rows[0:NROWS, :], ident[0:NROWS, 0:NROWS]).then_inc(rows_t, 1)
            for n in range(4):
                if n >= 2:
                    pe.wait_ge(mod_ready, n - 1)
                    ada_pair(n, work[2 + n % 2])
                mod_cols(n, work[2 + n % 2])

            def wm_transposes():
                pe.wait_ge(pool_prep, 1)
                pe.wait_ge(cols_ready, 1)
                for hf in range(2):
                    for q in range(4):
                        last = pe.transpose(work[hf][:, P * q:P * q + P], ws_raw[:, 4 * hf + q, :], ident[:, :])
                    last.then_inc(wm_psum, 1)

            def ln_b_sums():
                pe.wait_ge(small_in, 16 * 6)
                for g in range(8):
                    pe.wait_ge(wm_evac, g // 4 + 1)
                    pe.matmul(work[g // 4][:, P * (g % 4):P * (g % 4) + P], lnb_bc[:, P * g:P * g + P], wm[:, g, :],
                              start=True, stop=True).then_inc(sg_psum0, 1)

            def wv_transposes():
                pe.wait_ge(consts, 5)
                pe.wait_ge(pool_prep, 2)
                pe.wait_ge(sg_ready, 2)
                for h in range(4):
                    last = pe.transpose(work[0][:, P * h:P * h + P], wbd[:, 2, h, :], ident[:, :])
                last.then_inc(wvt_psum, 1)

            def gate_eff():
                pe.wait_ge(wvt_ready, 1)
                pe.wait_ge(wg_in, 16)
                for h in range(4):
                    last = pe.matmul(work[1][:, 8 * h:8 * h + 8], wvt[:, h, :], wg_pad[:, 8 + h, 0:8],
                                     start=True, stop=True)
                last.then_inc(eff_psum, 1)

            def m_values(t):
                if t == 0:
                    acc_free(pe, BX, 3)
                    pe.wait_ge(eff_ready, 1)
                if t == 3:
                    pe.wait_ge(mv_evac, 1)
                for h in range(MH):
                    last = pe.matmul(work[t % 3][:, P * h:P * h + P], bx[:, h, 3 + P * t:3 + P * t + P],
                                     wbd[:, 2, h, :], start=True, stop=True)
                last.then_inc(mv_psum, 1)

            def m_qk(n):
                pe.wait_ge(mv_evac, 4)
                pe.wait_ge(xc_ready, n % 4 + 1)
                pe.wait_ge(pool_prep, 4)
                if n >= 3:
                    pe.wait_ge(mqk_evac, n - 2)
                pe.matmul(work[n % 3][:, :], wbd[:, n // 4, n % 4, :], xc[:, n % 4, :],
                          start=True, stop=True).then_inc(mqk_psum, 1)

            def gates():
                pe.wait_ge(mqk_evac, 8)
                for part in range(3):
                    for h in range(MH):
                        rhs = (mq[:, h, :], mk[:, h, :], bx[:, h, 3:3 + T])[part]
                        last = pe.matmul(work[0][32 * h:32 * h + 32, :], wg_pad[:, 4 * part + h, :], rhs,
                                         start=part == 0, stop=part == 2, tile_position=(0, 32 * h))
                last.then_inc(g_psum, 1)

            def gates_tokens():
                pe.wait_ge(g_evac, 1)
                pe.wait_ge(pool_prep, 8)
                for t in range(NT):
                    last = pe.matmul(work[1][:, 8 * t:8 * t + 8], gates_t[:, P * t:P * t + P], gate_sel[:, :],
                                     start=True, stop=True)
                last.then_inc(gt_psum, 1)

            def cumulate():
                pe.wait_ge(lf_ready, 1)
                pe.matmul(work[2][:, 0:16], upper[:, :], gt[:, 4, :], start=True, stop=False)
                pe.matmul(work[2][:, 0:16], ones[:, :], pre[:, :, :].rearrange("p t h -> p (t h)"), start=False,
                          stop=True).then_inc(cum_psum, 1)

            def a_rows():
                pe.wait_ge(a_ready, 1)
                for t in range(NT):
                    last = pe.transpose(work[0][0:4, P * t:P * t + P], gt[:, 6, 4 * t:4 * t + 4], ident[:, :])
                last.then_inc(at_psum, 1)

            def m_cols():
                pe.wait_ge(m_rows, 1)
                for t in range(NT):
                    last = pe.transpose(work[1][:, 4 * t:4 * t + 4], neg_m[0:4, P * t:P * t + P], ident[0:4, 0:4])
                last.then_inc(mc_psum, 1)

            def m_scores(h):
                if h == 0:
                    pe.wait_ge(mc_ready, 1)
                else:
                    pe.wait_ge(wt_mult, NT * h)
                    pe.wait_ge(num_evac, 2 * h)
                pe.matmul(work[0][:, :], head_sel[:, h, :], neg_m[:, :], start=True, stop=True).then_inc(mb_psum, 1)
                for s, bank, at in ((0, 1, 0), (1, 2, 0), (3, 2, 384)):
                    n = T - P * s
                    pe.matmul(work[bank][:, at:at + n], mk[:, h, P * s:P * s + P], mq[:, h, P * s:T],
                              start=True, stop=True).then_inc(st_psum, 1)

            def m_scores2(h):
                pe.wait_ge(mexp, NT * (h + 1))
                pe.matmul(work[0][:, 0:256], mk[:, h, 256:384], mq[:, h, 256:T], start=True,
                          stop=True).then_inc(st_psum, 1)

            def m_values_out(h):
                pe.wait_ge(wt_ready, NT * (h + 1))
                for t in range(NT):
                    bank = work[1 + t // 2]
                    at = 256 * (t % 2)
                    for s in range(t + 1):
                        o = OFF[s] + P * (t - s)
                        last = pe.matmul(bank[:, at:at + P + 1], wts[:, o:o + P], mvals[:, s, h, 0:P + 1],
                                         start=s == 0, stop=s == t)
                    if t % 2:
                        last.then_inc(pv_psum, 1)

            def hb_transposes(h):
                if h == 0:
                    pe.wait_ge(hb_ready, 1)
                    pe.wait_ge(mod_ready, 6)
                else:
                    pe.wait_ge(yb_part, h)
                for t in range(NT):
                    last = pe.transpose(work[3][:, P * t:P * t + P], num[:, 4 * t + h, 0:P], ident[:, :])
                last.then_inc(hbt_psum, 1)

            def qk_transposes(n):
                if n == 0:
                    pe.wait_ge(q_evac, 4)
                    pe.wait_ge(num_evac, 2 * MH)
                if n == 4:
                    pe.wait_ge(k_norm, 4)
                if 2 <= n < 6:
                    pe.wait_ge(qt_ready, n - 1)
                if n >= 6:
                    pe.wait_ge(kt_ready, n - 5)
                src = q_raw if n < 4 else k_raw
                p = n % 4
                for t in range(NT):
                    last = pe.transpose(work[n % 2][:, P * t:P * t + P], src[:, t, P * p:P * p + P], ident[:, :])
                last.then_inc(qt_psum if n < 4 else kt_psum, 1)

            def a_scores(u):
                h, i, e = UNITS[u]
                if u < 2:
                    pe.wait_ge(qt_ready, 4)
                    pe.wait_ge(kt_ready, 4)
                    pe.wait_ge(qt_zero, 2)
                else:
                    pe.wait_ge(exp_ready, u - 1)
                n = P * (i + 1)
                bank = work[u % 2]
                pe.matmul(bank[:, 0:n], qt[:, h, P * i:P * i + P], kt[:, h // 2, 0:n], start=True, stop=False)
                pe.matmul(bank[:, n - P:n], ident_bf[:, :], causal_bf[:, :], start=False,
                          stop=True).then_inc(s_psum, 1)

            def p_transposes(u):
                h, i, e = UNITS[u]
                pe.wait_ge(p_ready, u + 1)
                if u:
                    pt_done(pe, u - 1)
                for j in range(i + 1):
                    last = pe.transpose(work[2][:, P * j:P * j + P], probs[:, u % 3, P * j:P * j + P], ident[:, :])
                last.then_inc(pt_psum, 1)

            def a_values(p):
                pt_done(pe, 8 * p + 7)
                pt_done(pe, 8 * p + 6)
                if p == 0:
                    acc_free(pe, AV, 3)
                    pe.wait_ge(yb_part, 4)
                else:
                    pe.wait_ge(o_evac, p)
                for j in range(NT):
                    for e in range(2):
                        h = 2 * p + e
                        last = pe.matmul(work[3][64 * e:64 * e + 64, P * j:T], avals[:, j, DA * h:DA * h + DA],
                                         probs_t[:, e, j, P * j:T], start=j == 0, stop=j == NT - 1)
                last.then_inc(o_psum, 1)

            def pt_done(eng, u):
                n = sum(PT_ON_ACT(v) for v in range(u + 1))
                if PT_ON_ACT(u):
                    eng.wait_ge(pt_act, n)
                else:
                    eng.wait_ge(pt_dve, u + 1 - n)

            def attention(u):
                if u < NU:
                    a_scores(u)
                if u >= LAG and (u - LAG) % 8 == 0 and u - LAG > 0:
                    a_values((u - LAG) // 8 - 1)
                if LAG <= u < NU + LAG:
                    p_transposes(u - LAG)

            def h1_transposes(t):
                pe.wait_ge(xn1_ready, t + 1)
                if t:
                    pe.wait_ge(h1_exact, 4 * t)
                    pe.wait_ge(h1_exact_act, 4 * t)
                for k in range(KT):
                    last = pe.transpose(work[k // 4][:, P * (k % 4):P * (k % 4) + P], xn[:, t % 2, P * k:P * k + P],
                                        ident[:, :])
                last.then_inc(h1_psum, 1)

            def spatial(g):
                pe.wait_ge(vn_ready, 4)
                if g >= 3:
                    pe.wait_ge(us_ready, g - 2)
                for t in range(NT):
                    last = pe.matmul(work[g % 3][:, P * t:P * t + P], vg[:, t, P * g:P * g + P], wm[:, g, :],
                                     start=True, stop=True)
                last.then_inc(sg_psum, 1)

            extra = {}

            def at(slot, job):
                extra.setdefault(slot, []).append(job)

            at(PLACES["spatial weights"], wm_transposes)
            at(PLACES["ln_b sums"], ln_b_sums)
            at(PLACES["wv transposes"], wv_transposes)
            at(PLACES["gate fold"], gate_eff)
            for t in range(NT):
                at(PLACES["mLSTM values"][t], lambda t=t: m_values(t))
            for n in range(8):
                at(PLACES["mLSTM q, k"][n], lambda n=n: m_qk(n))
            at(PLACES["gates"], gates)
            at(PLACES["gate columns"], gates_tokens)
            at(PLACES["running sums"], cumulate)
            at(PLACES["running max"], a_rows)
            at(PLACES["max columns"], m_cols)
            for h in range(MH):
                for n, job in enumerate((m_scores, m_scores2, m_values_out)):
                    slot = HEAD_SLOT + 3 * h + n
                    at((slot // 4, slot % 4), lambda h=h, job=job: job(h))
            for n in range(8):
                at(PLACES["q, k transposes"][n], lambda n=n: qk_transposes(n))
            for p, slot in enumerate(PLACES["mLSTM outputs"]):
                at(slot, lambda p=p: hb_transposes(p))
            for slot, us in ATT_SLOTS.items():
                for u in us:
                    at(slot, lambda u=u: attention(u))
            for t, slot in enumerate(((15, 1), (15, 2), (15, 3), (16, 1))):
                at(slot, lambda t=t: h1_transposes(t))
            for g in range(8):
                at(PLACES["spatial"][g], lambda g=g: spatial(g))
            bank3_free = {4: (mod_ready, 4), 5: (gate_ready, 1), 6: (gate_ready, 2), 7: (mod_ready, 5),
                          8: (o_evac, 4), 9: (mod_ready, 7), 10: (mod_ready, 8), 11: (gate_ready, 3)}

            def ada_use(n):
                pe.wait_ge(*bank3_free[n])
                (mod_cols if n in MOD_ITEMS else gate_row)(n, work[3])

            for n in range(4, 12):
                at(ADA_USE_SLOT[n], lambda n=n: ada_use(n))
            for w in range(NHALF):
                if w == L1 - 2:
                    continue
                for g in range(4):
                    if w == L1 - 1:
                        group(w - 1, g)
                        for job in extra.get((w - 1, g), []):
                            job()
                    group(w, g)
                    for job in extra.get((w, g), []):
                        job()

        @block.scalar
        def _(act_e):
            count = [0]

            def link(ins):
                count[0] += 1
                ins.then_inc(act_step, 1)
                act_e.wait_ge(act_step, count[0])

            def copy(dst, src):
                return nc.scalar.activation(dst, src, ACT.Copy)

            def rsqrt(y, v, ready, n, done):
                act_e.wait_ge(ready, n)
                link(nc.scalar.activation(y, v, ACT.Ln))
                nc.scalar.activation(y, y, ACT.Exp, scale=-0.5).then_inc(done, 1)

            def split_hi(w):
                s = landed(act_e, ("w", w))
                split_free(act_e, w)
                for a in range(PARTS):
                    copy(split_slot(w)[0][:, 2 * a:2 * a + 2, :], raw[:, s, 2 * a:2 * a + 2, :]).then_inc(w_hi_ready, 1)

            def ada_out(n):
                act_e.wait_ge(ada_used, 2 * n + 2)
                copy(ada_row[:, n % 2, :], work[2 + n % 2][:, :]).then_inc(ada_evac, 1)

            def ada_mul(n, kh):
                s = landed(act_e, ("ada", 2 * n + kh))
                for j in range(KH):
                    k = KH * kh + j
                    ins = nc.scalar.activation(raw[:, s, j, :], raw[:, s, j, :], ACT.Copy, scale=c_pad[:, k, 0:1])
                ins.then_inc(ada_mult, 1)

            act_e.dma_start(c_row, c.rearrange("l (j f) -> (l j) f", f=P)).then_inc(c_in, 16)
            flat = [("ada_b", ada_b), ("ln_g", ln_g)]
            for name, a in flat:
                r, n = ROWS[name]
                act_e.dma_start(rows[r:r + n, :], a.rearrange("l (j f) -> (l j) f", f=P)).then_inc(rows_in, 16)
            nc.scalar.preload_act_table_set("silu_and_others")
            act_e.wait_ge(c_psum, 1)
            nc.scalar.activation(c_pad[:, :, 0], work[2][:, 0:KT], ACT.Silu).then_inc(c_ready, 1)
            for t in range(NT):
                act_e.wait_ge(x_in[t], 16)
                nc.scalar.activation(act[:, 2 * t:2 * t + 2, :].rearrange("p a b -> p (a b)"), xres[:, t, :], ACT.Square,
                                     accum_out=rms[:, 0, t:t + 1]).then_inc(ss_ready, 1)
            nc.scalar.preload_act_table_set(LNEXP)
            rsqrt(rms[:, 2, 0:4], rms[:, 1, 0:4], var_ready, 1, ln_ready)
            ada_out(0)
            for n in range(8):
                act_e.wait_ge(xt_psum, n + 1)
                t, hf = n // 2, n % 2
                copy(act[:, 4 * hf:4 * hf + 4, P * t:P * t + P],
                     acc[n % 4][:, :].rearrange("p (k q) -> p k q", k=4)).then_inc(xt_evac, 1)
            ada_out(1)
            split_hi(0)
            ada_out(2)
            ada_out(3)
            for k in range(KT):
                act_e.wait_ge(h_exact, k + 1)
                copy(act_hi[:, k, :], act[:, k, :]).then_inc(h_hi, 1)

            todo = {}

            def at(slot, job):
                todo.setdefault(slot, []).append(job)

            def acc_wait(w, g):
                act_e.wait_ge(acc_ready, 4 * (w // 2) + g + 1)

            def wm_out():
                for hf in range(2):
                    act_e.wait_ge(wm_psum, hf + 1)
                    copy(wm[:, 4 * hf:4 * hf + 4, :],
                         work[hf][:, :].rearrange("p (k q) -> p k q", k=4)).then_inc(wm_evac, 1)

            def bx_out(g):
                acc_wait(1, g)
                copy(bx[:, g, 3:3 + T], acc[g][:, :]).then_inc(acc_freed_act, 1)

            def gate_act(w, g, k):
                acc_wait(w, g)
                nc.scalar.activation(act[:, k, :], acc[g][:, :], ACT.Silu).then_inc(acc_freed_act, 1)

            def mv_out(t):
                act_e.wait_ge(mv_psum, t + 1)
                if t == 0:
                    act_e.wait_ge(pool_prep, 7)
                copy(mvals[:, t, :, 0:P], work[t % 3][:, :].rearrange("p (h v) -> p h v", h=MH)).then_inc(mv_evac, 1)

            def xc_out(h):
                act_e.wait_ge(conv_step, 4 * h + 4)
                nc.scalar.activation(xc[:, h, :], conv[:, h, :], ACT.Silu).then_inc(xc_ready, 1)

            def mqk_out(n):
                act_e.wait_ge(mqk_psum, n + 1)
                copy((mq if n < 4 else mk)[:, n % 4, :], work[n % 3][:, :]).then_inc(mqk_evac, 1)

            def gates_out():
                act_e.wait_ge(g_psum, 1)
                copy(gates_t[:, :], work[0][:, :]).then_inc(g_evac, 1)

            def gates_log():
                nc.scalar.preload_act_table_set(LNEXP)
                act_e.wait_ge(gt_abs, 1)
                link(nc.scalar.activation(gt[:, 3, :], gt[:, 2, :], ACT.Exp, scale=-1.0))
                nc.scalar.activation(gt[:, 3, :], gt[:, 3, :], ACT.Ln, bias=1.0).then_inc(gt_ln, 1)

            def guard():
                act_e.wait_ge(mc_ready, 1)
                nc.scalar.activation(gt[:, 9, :], gt[:, 7, :], ACT.Exp).then_inc(guard_ready, 1)

            def m_exps(h):
                act_e.wait_ge(mb_psum, h + 1)
                for s in S_ORDER:
                    n = T - P * s
                    nc.scalar.activation(expw[:, OFF[s]:OFF[s] + n], work[0][:, P * s:T], ACT.Exp,
                                         bias=gt[:, 6, 4 * s + h:4 * s + h + 1]).then_inc(mexp, 1)

            def num_out(h):
                for a in range(2):
                    act_e.wait_ge(pv_psum, 2 * h + a + 1)
                    dst = num[:, :, :].rearrange("p (t h) v -> p t h v", t=NT)[:, 2 * a:2 * a + 2, h, 0:P + 1]
                    src = work[1 + a][:, :].rearrange("p (t v) -> p t v", t=2)[:, :, 0:P + 1]
                    copy(dst, src).then_inc(num_evac, 1)

            def qk_out(w, g, dst, evac):
                n = g + (4 if dst is k_raw else 0)
                acc_wait(w, g)
                copy(dst[:, g, :], acc[g][:, :]).then_inc(evac, 1)
                if n >= 2:
                    act_e.wait_ge(sq_used, n - 1)
                nc.scalar.activation(conv[:, n % 2, :], acc[g][:, :], ACT.Square).then_inc(acc_freed_act, 1)

            def v_out(g):
                acc_wait(9, g)
                copy(avals[:, g, :], acc[g][:, :]).then_inc(acc_freed_act, 1)

            def az_exp_out(g):
                acc_wait(11, g)
                if g >= 2:
                    acc_free(act_e, AZ, g - 2)
                nc.scalar.activation(wts[:, 512 * (g % 2):512 * (g % 2) + 512], acc[g][:, :], ACT.Exp,
                                     scale=-1.0).then_inc(az_exp, 1)

            def az_rec_out(g):
                act_e.wait_ge(az_den, g + 1)
                e = wts[:, 512 * (g % 2):512 * (g % 2) + 512]
                link(nc.scalar.activation(e, e, ACT.Ln))
                nc.scalar.activation(e, e, ACT.Exp, scale=-1.0).then_inc(az_rec, 1)

            def x_again():
                act_e.wait_ge(s_psum, NU)
                for t in range(NT):
                    act_e.dma_start(xres[:, t, :], x_view[:, t, :]).then_inc(x_in[t], 16)

            def qt_out(p):
                act_e.wait_ge(qt_psum, p + 1)
                for e in range(2):
                    r = slice(64 * e, 64 * e + 64)
                    last = nc.scalar.activation(qt[r, 2 * p + e, :], work[p % 2][r, :], ACT.Copy,
                                                scale=col("q_g", 0)[r])
                last.then_inc(qt_ready, 1)

            def attention(u):
                if u < NU:
                    h, i, e = UNITS[u]
                    n = P * (i + 1)
                    act_e.wait_ge(bias_ready, u + 1)
                    if u >= 3:
                        act_e.wait_ge(pt_psum, u - 2)
                    q = 8 * i + h
                    nc.scalar.activation(probs[:, u % 3, 0:n], work[u % 2][:, 0:n], ACT.Exp, bias=mx[:, 1, u:u + 1],
                                         scale=qs[:, 4, q:q + 1], accum_out=rs[:, 0, u:u + 1]).then_inc(exp_ready, 1)
                v = u - LAG
                if 0 <= v < NU and PT_ON_ACT(v):
                    h, i, e = UNITS[v]
                    act_e.wait_ge(pt_psum, v + 1)
                    copy(probs_t[:, e, 0:i + 1, P * i:P * i + P],
                         work[2][:, 0:P * (i + 1)].rearrange("p (j q) -> p j q", j=i + 1)).then_inc(pt_act, 1)
                if u in YA_SPLIT:
                    y_hi_part(4 + YA_SPLIT[u])

            def y_hi_part(n):
                k = Y_ORDER[n]
                half_done(act_e, 10 if k >= KH else 11)
                if n < 4:
                    act_e.wait_ge(y_exact, n + 1)
                elif n - 4 < O_FIRST:
                    acc_free(act_e, AZ, n - 4)
                else:
                    act_e.wait_ge(o_evac, n - 3)
                copy(act_hi[:, k, :], act[:, k, :]).then_inc(y_hi, 1)

            def x1_square(t):
                act_e.wait_ge(x1_ready, t + 1)
                nc.scalar.activation(probs[:, :, :].rearrange("p a b -> p (a b)")[:, 0:D], xres[:, t, :], ACT.Square,
                                     accum_out=rms[:, 0, 4 + t:5 + t]).then_inc(ss1_ready, 1)
                rsqrt(rms[:, 2, 4 + t:5 + t], rms[:, 1, 4 + t:5 + t], var1_ready, t + 1, ln1_ready)

            def h1_act_part(t):
                act_e.wait_ge(h1_psum, t + 1)
                act_e.wait_ge(mod_ready, 8)
                for k in range(KH, KT):
                    nc.scalar.activation(act[:, k, P * t:P * t + P], work[1][:, P * (k - KH):P * (k - KH) + P],
                                         ACT.Identity, bias=mod[:, 1, k:k + 1],
                                         scale=gain[:, 1, k:k + 1]).then_inc(h1_exact_act, 1)

            def h1_hi_part(t):
                act_e.wait_ge(h1_exact, 4 * (t + 1))
                act_e.wait_ge(h1_exact_act, 4 * (t + 1))
                copy(act_hi[:, :, P * t:P * t + P], act[:, :, P * t:P * t + P]).then_inc(h1_hi, 1)

            def gelu_v(w, g):
                cc = (w - 17) // 2
                acc_wait(w, g)
                nc.scalar.activation(vg[:, g, CH * cc:CH * cc + CH], acc[g][:, :],
                                     ACT.Gelu_apprx_tanh).then_inc(acc_freed_act, 1)

            def cv_rsqrt():
                nc.scalar.preload_act_table_set(LNEXP)
                rsqrt(rms[:, 2, 0:4], rms[:, 1, 0:4], cvar_ready, 1, cln_ready)
                nc.scalar.preload_act_table_set("gelu_apprx_tanh_and_others")

            def gelu_u(w, g):
                acc_wait(w, g)
                k = g + 4 * ((w - 21) // 2)
                nc.scalar.activation(act[:, k, :], acc[g][:, :], ACT.Gelu_apprx_tanh).then_inc(acc_freed_act, 1)

            def silu_z(w, g):
                n = g + 4 * ((w - 25) // 2)
                acc_wait(w, g)
                if n >= 4:
                    act_e.wait_ge(z1_exact, n - 3)
                nc.scalar.activation(tmp[:, n % 4, :], acc[g][:, :], ACT.Silu).then_inc(acc_freed_act, 1)

            def z1_hi_part(k):
                half_done(act_e, 26 if k < KH else 27)
                act_e.wait_ge(z1_exact, k + 1)
                copy(act_hi[:, k, :], act[:, k, :]).then_inc(z1_hi, 1)

            at(PLACES["spatial weights"], wm_out)
            for g in range(4):
                at((1, g), lambda g=g: bx_out(g))
                at(PLACES["mLSTM values"][g], lambda g=g: mv_out(g))
                at((3, g), lambda g=g: gate_act(3, g, 4 + g))
                at((5, g), lambda g=g: qk_out(5, g, q_raw, q_evac))
                at((7, g), lambda g=g: qk_out(7, g, k_raw, k_evac))
                at((9, g), lambda g=g: v_out(g))
                at((17, g), lambda g=g: gelu_v(17, g))
                at((19, g), lambda g=g: gelu_v(19, g))
                at((21, g), lambda g=g: gelu_u(21, g))
                at((23, g), lambda g=g: gelu_u(23, g))
                at((25, g), lambda g=g: silu_z(25, g))
                at((27, g), lambda g=g: silu_z(27, g))
            at((1, 3), lambda: nc.scalar.preload_act_table_set("silu_and_others"))
            for h in range(MH):
                at((2, 0), lambda h=h: xc_out(h))
            for n in range(8):
                at(PLACES["mLSTM q, k"][n], lambda n=n: mqk_out(n))
            at(PLACES["gates"], gates_out)
            at(PLACES["gate logs"], gates_log)
            at(PLACES["max columns"], guard)
            for h in range(MH):
                s0, s2 = HEAD_SLOT + 3 * h, HEAD_SLOT + 3 * h + 2
                at((s0 // 4, s0 % 4), lambda h=h: m_exps(h))
                at((s2 // 4, s2 % 4), lambda h=h: num_out(h))
            at(PLACES["q, k norms"], lambda: rsqrt(qs[:, 2, :], qs[:, 1, :], qk_ss, 1, qk_ln))
            for p in range(4):
                at(PLACES["q, k transposes"][p], lambda p=p: qt_out(p))
            at(PLACES["mLSTM normalised"], lambda: rsqrt(gt[:, 9, :], gt[:, 8, :], mvar_ready, 1, mln_ready))
            for g in range(4):
                at((11, g), lambda g=g: az_exp_out(g))
            for slot, us in ATT_SLOTS.items():
                for u in us:
                    at(slot, lambda u=u: attention(u))
            for g in range(4):
                at((11, g), lambda g=g: az_rec_out(g))
            for n in range(4 + O_FIRST):
                at((11, n // 2) if n < 4 else (11, 3), lambda n=n: y_hi_part(n))
            at((12, 2), x_again)
            for t in range(NT):
                at((15, t), lambda t=t: x1_square(t))
                if t:
                    at((15, t), lambda t=t: h1_act_part(t - 1))
                    at((15, t), lambda t=t: h1_hi_part(t - 1))
            at((15, 3), lambda: h1_act_part(3))
            at((15, 3), lambda: h1_hi_part(3))
            at((15, 3), lambda: split_hi(L1 + 1))
            at((16, 1), lambda: nc.scalar.preload_act_table_set("gelu_apprx_tanh_and_others"))
            at((20, 0), cv_rsqrt)
            at((24, 0), lambda: nc.scalar.preload_act_table_set("silu_and_others"))
            for k in range(KT):
                at((27, -1) if k < KH else (27, 3), lambda k=k: z1_hi_part(k))
            for n, after in ADA_LANDS.items():
                for kh in range(2):
                    at((after - 1, ADA_MUL[kh]), lambda n=n, kh=kh: ada_mul(n, kh))
            for w in range(NHALF):
                if w + 1 < NHALF and w != L1:
                    split_hi(w + 1)
                for g in range(-1, 4):
                    for job in todo.get((w, g), []):
                        job()

        @block.vector
        def _(dve):
            v_e = nc.vector
            count = [0]

            def link(ins):
                count[0] += 1
                ins.then_inc(dve_step, 1)
                dve.wait_ge(dve_step, count[0])

            def refine(y, v, t):
                link(v_e.tensor_tensor(t, y, y, ALU.mult))
                link(v_e.tensor_tensor(t, t, v, ALU.mult))
                link(v_e.tensor_scalar(t, t, -0.5, 1.5, ALU.mult, ALU.add))
                link(v_e.tensor_tensor(y, y, t, ALU.mult))

            def minus(dst, whole, hi):
                return v_e.tensor_tensor(dst, whole, hi.bitcast(F32), ALU.subtract)

            def split_lo(w):
                s = landed(dve, ("w", w))
                for a in range(PARTS):
                    dve.wait_ge(w_hi_ready, PARTS * w + a + 1)
                    ks = slice(2 * a, 2 * a + 2)
                    hi, lo = split_slot(w)
                    minus(lo[:, ks, :], raw[:, s, ks, :], hi[:, ks, :]).then_inc(w_lo_ready, 1)

            def mod_out(n):
                layer, cc = ADA[n]
                dve.wait_ge(modc_psum, MOD_ITEMS.index(n) + 1)
                dst = mod[:, layer, 4 * cc:4 * cc + 4]
                ins = v_e.tensor_tensor(dst, work[2 + n % 2 if n < 4 else 3][:, 0:4], col("ada_b", 24 * layer + 4 * cc, 4), ALU.add)
                if cc >= 2:
                    link(ins)
                    ins = v_e.scalar_tensor_tensor(out=gain[:, layer, 4 * cc - 8:4 * cc - 4], in0=dst, scalar=1.0,
                                                   in1=col("ln_g", 8 * layer + 4 * cc - 8, 4), op0=ALU.add,
                                                   op1=ALU.mult)
                ins.then_inc(mod_ready, 1)

            def gate_out(n):
                cc = ADA[n][1]
                dve.wait_ge(gate_psum, GATE_ITEMS.index(n) + 1)
                dve.wait_ge(gate_b_in, 16 * (ADA[n][0] + 1))
                dst = gate_bc[:, CH * (cc - 4):CH * (cc - 3)]
                v_e.tensor_tensor(dst, work[3][:, :], dst, ALU.add).then_inc(gate_ready, 1)

            dve.wait_ge(ss_ready, NT)
            v_e.tensor_scalar(rms[:, 1, 0:4], rms[:, 0, 0:4], 1.0 / D, 1e-6, ALU.mult, ALU.add).then_inc(var_ready, 1)
            dve.wait_ge(ln_ready, 1)
            refine(rms[:, 2, 0:4], rms[:, 1, 0:4], rms[:, 3, 0:4])
            for t in range(NT):
                v_e.tensor_scalar(xres[:, t, :], xres[:, t, :], rms[:, 2, t:t + 1], None, ALU.mult).then_inc(xn_ready, 1)
            dve.wait_ge(rows_t, 1)
            v_e.tensor_copy(cols[:, :], work[0][:, 0:NROWS]).then_inc(cols_ready, 1)
            dve.wait_ge(cols_ready, 1)
            mod_out(0)
            for n in range(1, 4):
                if n == 2:
                    split_lo(0)
                mod_out(n)
            dve.wait_ge(mod_ready, 4)
            dve.wait_ge(xt_evac, 8)

            def h_part(k):
                v_e.tensor_scalar(act[:, k, :], act[:, k, :], gain[:, 0, k:k + 1], mod[:, 0, k:k + 1], ALU.mult,
                                  ALU.add).then_inc(h_exact, 1)

            def h_lo_part(k):
                dve.wait_ge(h_hi, k + 1)
                minus(act_lo[:, k, :], act[:, k, :], act_hi[:, k, :]).then_inc(h_ready, 1)

            h_part(0)
            h_part(1)
            for k in range(KT):
                if k + 2 < KT:
                    h_part(k + 2)
                h_lo_part(k)

            todo = {}

            def at(slot, job):
                todo.setdefault(slot, []).append(job)

            def wvt_out():
                dve.wait_ge(wvt_psum, 1)
                v_e.tensor_copy(wvt, work[0][:, :].rearrange("p (h c) -> p h c", h=4)).then_inc(wvt_ready, 1)

            def sg_out():
                dve.wait_ge(small_in, 16 * 6)
                for a in range(2):
                    dve.wait_ge(sg_psum0, 4 * a + 4)
                    v_e.tensor_tensor(sg_add[:, 4 * a:4 * a + 4, :], work[a][:, :].rearrange("p (g t) -> p g t", g=4),
                                      bs_bc[:, 4 * a:4 * a + 4, :], ALU.add).then_inc(sg_ready, 1)

            def eff_out():
                dve.wait_ge(eff_psum, 1)
                v_e.tensor_copy(wg_pad[:, 8:12, 0:8],
                                work[1][:, 0:32].rearrange("p (h r) -> p h r", h=4)).then_inc(eff_ready, 1)

            def conv_tap(j, h):
                w = col("conv_w", 4 * j + h)
                if j == 0:
                    acc_free(dve, BX, h)
                    dve.wait_ge(pool_prep, 5)
                    ins = v_e.tensor_scalar(conv[:, h, :], bx[:, h, 0:T], w, col("conv_b", h), ALU.mult, ALU.add)
                else:
                    dve.wait_ge(conv_step, 4 * h + j)
                    ins = v_e.scalar_tensor_tensor(out=conv[:, h, :], in0=bx[:, h, j:j + T], scalar=w,
                                                   in1=conv[:, h, :], op0=ALU.mult, op1=ALU.add)
                ins.then_inc(conv_step, 1)

            def skip_part():
                dve.wait_ge(mqk_psum, 8)
                for h in range(MH):
                    last = v_e.tensor_scalar(xc[:, h, :], xc[:, h, :], col("skip", h), None, ALU.mult)
                last.then_inc(skip_done, 1)

            def gates_add():
                dve.wait_ge(gt_psum, 1)
                for m in range(2):
                    ins = v_e.tensor_tensor(
                        gt[:, m, :].rearrange("p (t h) -> p t h", t=NT),
                        work[1][:, 0:32].rearrange("p (t r) -> p t r", t=NT)[:, :, 4 * m:4 * m + 4],
                        bg_bc[:, 4 * m:4 * m + 4].unsqueeze(1).to_broadcast((P, NT, 4)), ALU.add)
                link(ins)
                v_e.scalar_tensor_tensor(out=gt[:, 2, :], in0=gt[:, 1, :], scalar=-1.0, in1=gt[:, 1, :],
                                         op0=ALU.mult, op1=ALU.max).then_inc(gt_abs, 1)

            def log_forget():
                dve.wait_ge(gt_ln, 1)
                link(v_e.scalar_tensor_tensor(out=gt[:, 4, :], in0=gt[:, 1, :], scalar=0.0, in1=gt[:, 3, :],
                                              op0=ALU.min, op1=ALU.subtract))
                v_e.memset(pre[:, 0, :], 0.0)
                link(v_e.tensor_copy(pre[:, 1, :], gt[:, 4, 0:4]))
                link(v_e.tensor_tensor(pre[:, 2, :], pre[:, 1, :], gt[:, 4, 4:8], ALU.add))
                v_e.tensor_tensor(pre[:, 3, :], pre[:, 2, :], gt[:, 4, 8:12], ALU.add).then_inc(lf_ready, 1)

            def a_cols():
                dve.wait_ge(cum_psum, 1)
                v_e.tensor_copy(gt[:, 5, :], work[2][:, 0:16])
                v_e.tensor_tensor(gt[:, 6, :], gt[:, 0, :], work[2][:, 0:16], ALU.subtract).then_inc(a_ready, 1)

            def running_max():
                dve.wait_ge(at_psum, 1)
                dve.wait_ge(pool_prep, 9)
                link(v_e.tensor_scalar(run[:, 0, PAD:PAD + T], work[0][0:4, :], 0.0, None, ALU.max))
                b, d = 0, 1
                while d < T:
                    link(v_e.tensor_tensor(run[:, 1 - b, PAD:PAD + T], run[:, b, PAD:PAD + T],
                                           run[:, b, PAD - d:PAD + T - d], ALU.max))
                    b, d = 1 - b, 2 * d
                v_e.tensor_scalar(neg_m[0:4, :], run[:, b, PAD:PAD + T], -1.0, None, ALU.mult).then_inc(m_rows, 1)

            def m_exponent():
                dve.wait_ge(mc_psum, 1)
                v_e.tensor_tensor(gt[:, 7, :], work[1][:, 0:16], gt[:, 5, :], ALU.subtract).then_inc(mc_ready, 1)

            def weights(h, part):
                if part == 0 and h:
                    dve.wait_ge(pv_psum, 2 * h)
                for n, s in enumerate(S_ORDER):
                    if (n == 3) != (part == 1):
                        continue
                    dve.wait_ge(st_psum, NT * h + (1, 3, 3, 4)[n])
                    dve.wait_ge(mexp, NT * h + n + 1)
                    bank, at_ = {0: (1, 0), 1: (2, 0), 3: (2, 384), 2: (0, 0)}[s]
                    m = T - P * s
                    v_e.scalar_tensor_tensor(out=wts[:, OFF[s]:OFF[s] + m], in0=work[bank][:, at_:at_ + m],
                                             scalar=float(P) ** -0.5, in1=expw[:, OFF[s]:OFF[s] + m], op0=ALU.mult,
                                             op1=ALU.mult).then_inc(wt_mult, 1)

            def head_stats(h):
                dve.wait_ge(num_evac, 2 * h + 2)
                for t in range(NT):
                    ins = v_e.bn_stats(st6[:, 4 * t + h, :], num[:, 4 * t + h, 0:P])
                link(ins)
                for t in range(NT):
                    ins = v_e.bn_aggr(mv2[:, 4 * t + h, :], st6[:, 4 * t + h, :])
                if h == MH - 1:
                    link(ins)

            def square_sums(n):
                acc_free(dve, AQ + n // 4, n % 4)
                v_e.tensor_reduce(qs[:, 0, 8 * n:8 * n + 8], conv[:, n % 2, :].rearrange("p (h d) -> p h d", h=AH),
                                  AX_X, ALU.add).then_inc(sq_used, 1)

            def m_norms():
                dve.wait_ge(guard_ready, 1)
                link(v_e.scalar_tensor_tensor(out=gt[:, 8, :], in0=num[:, :, P], scalar=-1.0, in1=num[:, :, P],
                                              op0=ALU.mult, op1=ALU.max))
                link(v_e.tensor_tensor(gt[:, 8, :], gt[:, 8, :], gt[:, 9, :], ALU.max))
                link(v_e.reciprocal(gt[:, 10, :], gt[:, 8, :]))
                link(v_e.tensor_tensor(gt[:, 11, :], gt[:, 10, :], gt[:, 10, :], ALU.mult))
                link(v_e.tensor_tensor(gt[:, 11, :], gt[:, 11, :], mv2[:, :, 1], ALU.mult))
                v_e.tensor_scalar(gt[:, 8, :], gt[:, 11, :], 1e-5, None, ALU.add).then_inc(mvar_ready, 1)

            def qk_norms():
                dve.wait_ge(sq_used, 8)
                dve.wait_ge(k_evac, 4)
                v_e.tensor_scalar(qs[:, 1, :], qs[:, 0, :], 1.0 / DA, 1e-6, ALU.mult, ALU.add).then_inc(qk_ss, 1)
                dve.wait_ge(qk_ln, 1)
                refine(qs[:, 2, :], qs[:, 1, :], qs[:, 3, :])
                link(v_e.tensor_scalar(qs[:, 4, :], qs[:, 2, :], float(DA) ** -0.5, None, ALU.mult))
                for t in range(NT):
                    v = k_raw[:, t, :].rearrange("p (h d) -> p h d", h=AH)
                    v_e.tensor_tensor(v, v, qs[:, 2, 32 + 8 * t:40 + 8 * t].unsqueeze(2).to_broadcast((P, AH, DA)),
                                      ALU.mult).then_inc(k_norm, 1)

            def hb_part():
                dve.wait_ge(mln_ready, 1)
                refine(gt[:, 9, :], gt[:, 8, :], gt[:, 11, :])
                link(v_e.tensor_tensor(gt[:, 10, :], gt[:, 10, :], gt[:, 9, :], ALU.mult))
                for n in range(16):
                    last = v_e.tensor_scalar(num[:, n, 0:P], num[:, n, 0:P], mv2[:, n, 0:1], gt[:, 10, n:n + 1],
                                             ALU.subtract, ALU.mult)
                last.then_inc(hb_ready, 1)

            def kt_out(p):
                dve.wait_ge(kt_psum, p + 1)
                v_e.tensor_scalar(kt[:, p, :], work[p % 2][:, :], col("k_g", 0), None, ALU.mult).then_inc(kt_ready, 1)

            def yb_out(h):
                dve.wait_ge(hbt_psum, h + 1)
                if h == 0:
                    dve.wait_ge(skip_done, 1)
                v_e.scalar_tensor_tensor(out=xc[:, h, :], in0=work[3][:, :], scalar=col("out_g", h), in1=xc[:, h, :],
                                         op0=ALU.mult, op1=ALU.add).then_inc(yb_part, 1)
                dve.wait_ge(yb_part, h + 1)
                acc_free(dve, BZ, 3)
                v_e.tensor_tensor(act[:, 4 + h, :], act[:, 4 + h, :], xc[:, h, :], ALU.mult).then_inc(y_exact, 1)

            def attention(u):
                if u < NU:
                    h, i, e = UNITS[u]
                    n = P * (i + 1)
                    q = 8 * i + h
                    dve.wait_ge(s_psum, u + 1)
                    link(v_e.reduce_max(mx[:, 0, u:u + 1], work[u % 2][:, 0:n], AX_X))
                    v_e.scalar_tensor_tensor(out=mx[:, 1, u:u + 1], in0=mx[:, 0, u:u + 1], scalar=-1.0,
                                             in1=qs[:, 4, q:q + 1], op0=ALU.mult, op1=ALU.mult).then_inc(bias_ready, 1)
                v = u - 1
                if 0 <= v < NU:
                    n = P * (UNITS[v][1] + 1)
                    dve.wait_ge(exp_ready, v + 1)
                    link(v_e.reciprocal(rs[:, 1, v:v + 1], rs[:, 0, v:v + 1]))
                    v_e.tensor_scalar(probs[:, v % 3, 0:n], probs[:, v % 3, 0:n], rs[:, 1, v:v + 1], None,
                                      ALU.mult).then_inc(p_ready, 1)
                v = u - LAG
                if v >= 8 and v % 8 == 0:
                    ya_out(v // 8 - 1)
                if 0 <= v < NU and not PT_ON_ACT(v):
                    h, i, e = UNITS[v]
                    dve.wait_ge(pt_psum, v + 1)
                    v_e.tensor_copy(probs_t[:, e, 0:i + 1, P * i:P * i + P],
                                    work[2][:, 0:P * (i + 1)].rearrange("p (j q) -> p j q", j=i + 1)).then_inc(pt_dve, 1)
                if u in YA_SPLIT:
                    y_lo_part(4 + YA_SPLIT[u])

            def ya_out(p):
                dve.wait_ge(o_psum, p + 1)
                if p < O_FIRST:
                    v_e.tensor_copy(act[:, p, :], work[3][:, :]).then_inc(o_evac, 1)
                else:
                    acc_free(dve, AZ, p)
                    v_e.tensor_tensor(act[:, p, :], work[3][:, :], act[:, p, :], ALU.mult).then_inc(o_evac, 1)

            def az_add(p):
                dve.wait_ge(az_exp, p + 1)
                e = wts[:, 512 * (p % 2):512 * (p % 2) + 512]
                v_e.tensor_scalar(e, e, 3e38, 1.0, ALU.min, ALU.add).then_inc(az_den, 1)

            def az_out(p):
                dve.wait_ge(az_rec, p + 1)
                e = wts[:, 512 * (p % 2):512 * (p % 2) + 512]
                if p < O_FIRST:
                    dve.wait_ge(o_evac, p + 1)
                    link(v_e.tensor_tensor(act[:, p, :], act[:, p, :], e, ALU.mult))
                    e = act[:, p, :]
                v_e.tensor_tensor(act[:, p, :], acc[p][:, :], e, ALU.mult).then_inc(acc_freed_dve, 1)

            def y_lo_part(n):
                k = Y_ORDER[n]
                dve.wait_ge(y_hi, n + 1)
                minus(act_lo[:, k, :], act[:, k, :], act_hi[:, k, :]).then_inc(y_ready, 1)

            def residual(w, g, done):
                cc = CHUNKS[HALVES[w][0]][2]
                dve.wait_ge(acc_ready, 4 * (w // 2) + g + 1)
                v_e.tensor_tensor(tmp[:, g, :], acc[g][:, :], gate_bc[:, CH * cc:CH * cc + CH],
                                  ALU.mult).then_inc(acc_freed_dve, 1)
                dve.wait_ge(acc_freed_dve, 4 * sum(n < HALVES[w][0] for n in DVE_CHUNKS) + g + 1)
                if w == 13:
                    dve.wait_ge(x_in[g], 32)
                ins = v_e.tensor_tensor(xres[:, g, CH * cc:CH * cc + CH], xres[:, g, CH * cc:CH * cc + CH],
                                        tmp[:, g, :], ALU.add)
                if done is not None:
                    ins.then_inc(done, 1)

            def x1_norm(t):
                c4 = slice(4 + t, 5 + t)
                dve.wait_ge(ss1_ready, t + 1)
                v_e.tensor_scalar(rms[:, 1, c4], rms[:, 0, c4], 1.0 / D, 1e-6, ALU.mult,
                                  ALU.add).then_inc(var1_ready, 1)
                dve.wait_ge(ln1_ready, t + 1)
                refine(rms[:, 2, c4], rms[:, 1, c4], rms[:, 3, c4])
                if t >= 2:
                    dve.wait_ge(h1_psum, t - 1)
                v_e.tensor_scalar(xn[:, t % 2, :], xres[:, t, :], rms[:, 2, c4], None, ALU.mult).then_inc(xn1_ready, 1)

            def h1_part(t):
                dve.wait_ge(h1_psum, t + 1)
                dve.wait_ge(mod_ready, 8)
                for k in range(KH):
                    v_e.tensor_scalar(act[:, k, P * t:P * t + P], work[k // 4][:, P * (k % 4):P * (k % 4) + P],
                                      gain[:, 1, k:k + 1], mod[:, 1, k:k + 1], ALU.mult, ALU.add).then_inc(h1_exact, 1)

            def h1_lo_part(t):
                dve.wait_ge(h1_hi, t + 1)
                cs = slice(P * t, P * t + P)
                minus(act_lo[:, :, cs], act[:, :, cs], act_hi[:, :, cs]).then_inc(h1_ready, 1)

            def cv_stats(w, g):
                cc = (w - 17) // 2
                acc_free(dve, CV + cc, g)
                ins = v_e.bn_stats(st6[:, 2 * g + cc, :], vg[:, g, CH * cc:CH * cc + CH])
                if cc:
                    link(ins)
                    ins = v_e.bn_aggr(mv2[:, g, :], st6[:, 2 * g:2 * g + 2, :].rearrange("p a b -> p (a b)"))
                    link(ins)

            def cv_norm():
                v_e.tensor_scalar(rms[:, 1, 0:4], mv2[:, 0:4, 1], 1e-5, None, ALU.add).then_inc(cvar_ready, 1)
                dve.wait_ge(cln_ready, 1)
                refine(rms[:, 2, 0:4], rms[:, 1, 0:4], rms[:, 3, 0:4])
                for t in range(NT):
                    v_e.tensor_scalar(vg[:, t, :], vg[:, t, :], mv2[:, t, 0:1], rms[:, 2, t:t + 1], ALU.subtract,
                                      ALU.mult).then_inc(vn_ready, 1)

            def spatial_out(g):
                dve.wait_ge(sg_psum, g + 1)
                t3 = probs[:, g % 3, :].rearrange("p (t q) -> p t q", t=NT)
                link(v_e.scalar_tensor_tensor(out=t3, in0=work[g % 3][:, :].rearrange("p (t q) -> p t q", t=NT),
                                              scalar=col("c_ln_g", g),
                                              in1=sg_add[:, g:g + 1, :].to_broadcast((P, NT, P)), op0=ALU.mult,
                                              op1=ALU.add))
                acc_free(dve, CU + g // 4, g % 4)
                v_e.tensor_tensor(act[:, g, :], act[:, g, :], probs[:, g % 3, :], ALU.mult).then_inc(us_ready, 1)

            def z_out(n):
                acc_free(dve, CZ + n // 4, n % 4)
                dve.wait_ge(us_ready, n + 1)
                v_e.tensor_tensor(act[:, n, :], act[:, n, :], tmp[:, n % 4, :], ALU.mult).then_inc(z1_exact, 1)

            def z1_lo_part(k):
                dve.wait_ge(z1_hi, k + 1)
                minus(act_lo[:, k, :], act[:, k, :], act_hi[:, k, :]).then_inc(z1_ready, 1)

            at(PLACES["ln_b sums"], sg_out)
            at(PLACES["wv transposes"], wvt_out)
            at(PLACES["gate fold"], eff_out)
            for g in range(4):
                for j in range(4):
                    at((1, g), lambda g=g, j=j: conv_tap(j, g))
                at((5, g), lambda g=g: square_sums(g))
                at((7, g), lambda g=g: square_sums(4 + g))
                at((13, g), lambda g=g: residual(13, g, None))
                at((17, g), lambda g=g: cv_stats(17, g))
                at((19, g), lambda g=g: cv_stats(19, g))
                at((25, g), lambda g=g: z_out(g))
                at((27, g), lambda g=g: z_out(4 + g))
                at((29, g), lambda g=g: residual(29, g, out_ready))
                at((31, g), lambda g=g: residual(31, g, out_ready))
            for p, slot in enumerate(PLACES["mLSTM outputs"]):
                at(slot, lambda p=p: yb_out(p))
            for g in range(8):
                at(PLACES["spatial"][g], lambda g=g: spatial_out(g))
            at(PLACES["skip"], skip_part)
            at(PLACES["gate columns"], gates_add)
            at(PLACES["gate logs"], log_forget)
            at(PLACES["running sums"], a_cols)
            at(PLACES["running max"], running_max)
            at(PLACES["max columns"], m_exponent)
            for h in range(MH):
                s0 = HEAD_SLOT + 3 * h
                at((s0 // 4, s0 % 4), lambda h=h: weights(h, 0))
                at(((s0 + 1) // 4, (s0 + 1) % 4), lambda h=h: weights(h, 1))
                at(((s0 + 2) // 4, (s0 + 2) % 4), lambda h=h: head_stats(h))
            at(PLACES["q, k norms"], qk_norms)
            at(PLACES["mLSTM norms"], m_norms)
            for p in range(4):
                at(PLACES["q, k transposes"][4 + p], lambda p=p: kt_out(p))
            at(PLACES["mLSTM normalised"], hb_part)
            for g in range(4):
                at((11, g), lambda g=g: az_add(g))
            for slot, us in ATT_SLOTS.items():
                for u in us:
                    at(slot, lambda u=u: attention(u))
            for g in range(4):
                at((11, g), lambda g=g: az_out(g))
            for n in range(4 + O_FIRST):
                at((11, n // 2) if n < 4 else (11, 3), lambda n=n: y_lo_part(n))
            for t in range(NT):
                at((15, t), lambda t=t: residual(15, t, x1_ready))
                at((15, t), lambda t=t: x1_norm(t))
                if t:
                    at((15, t), lambda t=t: h1_part(t - 1))
                    at((15, t), lambda t=t: h1_lo_part(t - 1))
            at((15, 3), lambda: h1_part(3))
            at((15, 3), lambda: h1_lo_part(3))
            at((15, 3), lambda: split_lo(L1 + 1))
            at((20, 0), cv_norm)
            for n in range(4, 12):
                at(ADA_USE_SLOT[n], lambda n=n: (mod_out(n) if n in MOD_ITEMS else gate_out(n)))
            for k in range(KT):
                at((27, -1) if k < KH else (27, 3), lambda k=k: z1_lo_part(k))
            for w in range(NHALF):
                if w + 1 < NHALF and w != L1:
                    split_lo(w + 1)
                for g in range(-1, 4):
                    for job in todo.get((w, g), []):
                        job()


_INS = ["x", "c", "ln_g", "ada_w", "ada_b", "w_in", "w_out", "a_q_g", "a_k_g", "b_conv_w", "b_conv_b", "b_wq", "b_wk",
        "b_wv", "b_w_gates", "b_b_gates", "b_out_g", "b_skip", "c_ln_g", "c_ln_b", "c_ws", "c_bs"]


def kernel(**inputs):
    import numpy as _np
    import concourse.bacc as _bacc
    from concourse import mybir as _mybir
    from concourse.bass_utils import run_bass_kernel_spmd as _run

    nc = _bacc.Bacc("TRN2", target_bir_lowering=False, num_devices=1)
    arrays, args = {}, []
    for name in _INS:
        a = _np.ascontiguousarray(inputs[name])
        arrays[f"in_{name}_dram"] = a
        args.append(nc.dram_tensor(f"in_{name}_dram", a.shape, _mybir.dt.from_np(a.dtype), kind="ExternalInput").ap())
    args.append(nc.dram_tensor("out_0_dram", (1, T, D), _mybir.dt.float32, kind="ExternalOutput").ap())
    build(nc, *args)
    r = _run(nc, [arrays], core_ids=[0])
    return r.results[0]["out_0_dram"]
```

```python
from contextlib import ExitStack

import concourse.bass as bass
from concourse import mybir

F32 = mybir.dt.float32
F32R = mybir.dt.float32r
BF16 = mybir.dt.bfloat16
ALU = mybir.AluOpType
ACT = mybir.ActivationFunctionType
AX_X = mybir.AxisListType.X

P = 128
D = 1024
T = 512
KT = D // P
NT = T // P
CH = 512
KH = 4
AH = 8
DA = 64
MH = 4
VP = 130
NEG = -1e30
RAW = 3
SPLIT = 2
L1 = 16
PARTS = 2
LNEXP = "natural_log_exp_and_others"

CHUNKS = [
    ("in", 0, 4, (0, 1), "feature", "bx"), ("in", 0, 5, (0, 1), "feature", "bz"),
    ("in", 0, 0, (0, 1), "token", "aq"), ("in", 0, 1, (0, 1), "token", "ak"),
    ("in", 0, 2, (0, 1), "token", "av"), ("in", 0, 3, (1, 0), "feature", "az"),
    ("out", 0, 0, (1, 0), "token", "y0"), ("out", 0, 1, (1, 0), "token", "y0"),
    ("in", 1, 2, (0, 1), "token", "cv"), ("in", 1, 3, (0, 1), "token", "cv"),
    ("in", 1, 0, (0, 1), "feature", "cu"), ("in", 1, 1, (0, 1), "feature", "cu"),
    ("in", 1, 4, (0, 1), "feature", "cz"), ("in", 1, 5, (0, 1), "feature", "cz"),
    ("out", 1, 0, (0, 1), "token", "y1"), ("out", 1, 1, (0, 1), "token", "y1"),
]
BX, BZ, AQ, AK, AV, AZ, Y0, CV, CU, CZ = 0, 1, 2, 3, 4, 5, 6, 8, 10, 12
HALVES = [(c, kh) for c in range(len(CHUNKS)) for kh in CHUNKS[c][3]]
NHALF = len(HALVES)
ADA_FIRST = [(0, 2), (0, 3), (0, 0), (0, 1)]
ADA_LATER = [(0, 4), (0, 5), (1, 2), (1, 3), (1, 0), (1, 1), (1, 4), (1, 5)]
ADA = ADA_FIRST + ADA_LATER
GATE_ITEMS = [n for n, (_, cc) in enumerate(ADA) if cc >= 4]
MOD_ITEMS = [n for n, (_, cc) in enumerate(ADA) if cc < 4]
ADA_LANDS = {4: 2, 5: 3, 6: 4, 7: 6, 8: 10, 9: 11, 10: 14, 11: 16}
ADA_MUL_SLOT = {4: ((1, 0), (1, 1)), 5: ((2, 0), (2, 1)), 6: ((3, 0), (3, 1)), 7: ((5, 0), (5, 1)),
                8: ((9, 0), (9, 1)), 9: ((10, 0), (10, 1)), 10: ((13, 0), (13, 1)), 11: ((15, 0), (15, 1))}
ADA_USE_SLOT = {4: (2, 2), 5: (4, 2), 6: (5, 3), 7: (7, 1), 8: (13, 0), 9: (13, 1), 10: (17, 1), 11: (19, 0)}

PLACES = {
    "spatial weights": (0, 0), "ln_b sums": (0, 2), "wv transposes": (0, 3), "gate fold": (1, 0),
    "mLSTM values": ((2, 0), (2, 1), (2, 2), (2, 3)),
    "mLSTM q, k": ((3, 0), (3, 0), (3, 1), (3, 2), (3, 2), (3, 2), (3, 3), (3, 3)),
    "skip": (3, 3), "gates": (4, 0), "gate columns": (4, 1), "gate logs": (4, 1), "running sums": (4, 2),
    "running max": (5, 0), "max columns": (5, 3),
    "q, k norms": (7, 3), "mLSTM norms": (8, 3), "mLSTM normalised": (9, 0),
    "q, k transposes": ((8, 3), (8, 3), (8, 3), (8, 3), (9, 0), (9, 0), (9, 0), (9, 0)),
    "mLSTM outputs": ((9, 3), (9, 3), (9, 3), (10, 0)),
    "spatial": ((21, 3), (22, 1), (22, 1), (22, 2), (23, 2), (23, 3), (24, 1), (24, 2)),
}


def plan_stream():
    stream = [("ada", n) for n in range(2 * len(ADA_FIRST))]
    stream.insert(4, ("w", 0))
    for w in range(1, NHALF):
        stream.append(("w", w))
        for n, after in ADA_LANDS.items():
            if after == w:
                stream += [("ada", 2 * n), ("ada", 2 * n + 1)]
    return stream


STREAM = plan_stream()
PLACE = {item: n for n, item in enumerate(STREAM)}

ROWS = {}
for _name, _rows in (("ada_b", 48), ("ln_g", 16), ("conv_w", 16), ("conv_b", 4), ("out_g", 4),
                     ("skip", 4), ("c_ln_g", 8), ("q_g", 1), ("k_g", 1)):
    ROWS[_name] = (sum(r for _, r in ROWS.values()), _rows)
NROWS = sum(r for _, r in ROWS.values())

UNITS = [(2 * p + e, i, e) for p in range(AH // 2) for i in range(NT) for e in range(2)]
NU = len(UNITS)
S_ORDER = (0, 1, 3, 2)
PAD = 256


def PT_ON_ACT(u):
    return UNITS[u][1] == 3


LAG = 2
ATT_SLOTS = {}
_u = 0
for _slot, _n in zip([(9, 1), (9, 2), (9, 3)] + [(w, g) for w in (10, 11, 12) for g in range(4)][:11],
                     (2, 2, 2, 3, 3, 2, 3, 2, 2, 2, 3, 3, 3, 3)):
    ATT_SLOTS[_slot] = list(range(_u, _u + _n))
    _u += _n
assert _u == NU + LAG + 1
O_FIRST = 2
HEAD_SLOT = 24
YA_SPLIT = {8 * p + 9 + LAG: p for p in range(2, 3)} | {NU + LAG: 3}
Y_ORDER = (4, 5, 6, 7, 0, 1, 2, 3)


def build(nc, x, c, ln_g, ada_w, ada_b, w_in, w_out, a_q_g, a_k_g, b_conv_w, b_conv_b, b_wq, b_wk, b_wv,
          b_w_gates, b_b_gates, b_out_g, b_skip, c_ln_g, c_ln_b, c_ws, c_bs, out):
    with ExitStack() as ctx:
        def sb(name, shape, dt=F32):
            return ctx.enter_context(nc.sbuf_tensor(name, shape, dt))

        def sem(name):
            return ctx.enter_context(nc.semaphore(name))

        acc = [ctx.enter_context(nc.psum_tensor(f"acc{g}", [P, 512], F32)) for g in range(4)]
        work = [ctx.enter_context(nc.psum_tensor(f"work{g}", [P, 512], F32)) for g in range(4)]

        raw = sb("raw", [P, RAW, KH, CH])
        w_hi = sb("w_hi", [P, SPLIT, KH, CH], F32R)
        w_lo = sb("w_lo", [P, SPLIT, KH, CH], F32R)
        act_hi = sb("act_hi", [P, KT, T], F32R)
        act_lo = sb("act_lo", [P, KT, T], F32R)
        act = sb("act", [P, KT, T])
        xres = sb("xres", [P, NT, D])
        xc = sb("xc", [P, MH, T])
        conv = sb("conv", [P, MH, T])
        late = sb("late", [P, 2 * NT * MH * VP])
        wts = sb("wts", [P, 1280])
        probs = sb("probs", [P, 3, T])
        gate_bc = sb("gate_bc", [P, D])
        ada_row = sb("ada_row", [P, 2, CH])
        ident = sb("ident", [P, P])
        ident_bf = sb("ident_bf", [P, P], BF16)
        causal_bf = sb("causal_bf", [P, P], BF16)
        upper = sb("upper", [P, P])
        ones = sb("ones", [P, P])
        head_sel = sb("head_sel", [P, MH, P])
        gate_sel = sb("gate_sel", [P, 8])
        cols = sb("cols", [P, NROWS])
        c_pad = sb("c_pad", [P, KT, 32])
        mod = sb("mod", [P, 2, 16])
        gain = sb("gain", [P, 2, 8])
        bg_bc = sb("bg_bc", [P, 8])
        wm = sb("wm", [P, 8, P])
        sg_add = sb("sg_add", [P, 8, P])
        neg_m = sb("neg_m", [P, T])
        rms = sb("rms", [P, 4, 8])
        gt = sb("gt", [P, 12, 16])
        pre = sb("pre", [P, NT, 4])
        st6 = sb("st6", [P, 16, 6])
        mv2 = sb("mv2", [P, 16, 2])
        qs = sb("qs", [P, 5, 64])
        mx = sb("mx", [P, 2, NU])
        rs = sb("rs", [P, 2, NU])
        with nc.sbuf_tensor("mid", [P, 4160], F32) as mid:
            pass
        third = sb("third", [P, 2, KH, CH], F32R)
        vals = late[:, 0:NT * MH * VP]
        num = late[:, NT * MH * VP:].rearrange("p (n v) -> p n v", v=VP)
        vg = late[:, 0:4096].rearrange("p (t n) -> p t n", t=NT)
        wbd = mid[:, 2064:2064 + 1536].rearrange("p (m h c) -> p m h c", m=3, h=4)
        bx = mid[:, 0:4 * 515].rearrange("p (h t) -> p h t", h=4)
        k_raw = mid[:, 0:2048].rearrange("p (t n) -> p t n", t=NT)
        q_raw = mid[:, 2064:2064 + 2048].rearrange("p (t n) -> p t n", t=NT)
        probs_t = mid[:, 0:4096].rearrange("p (e j q) -> p e j q", e=2, j=NT)
        mq = xres[:, 0:2, :].rearrange("p a (b t) -> p (a b) t", b=2)
        mk = xres[:, 2:4, :].rearrange("p a (b t) -> p (a b) t", b=2)
        qt = xres[:, :, :].rearrange("p a (b t) -> p (a b) t", b=2)
        kt = conv
        mvals = vals[:, :].rearrange("p (t h v) -> p t h v", t=NT, h=MH)
        avals = vals[:, 0:2048].rearrange("p (t n) -> p t n", t=NT)
        wvt = wts[:, 0:512].rearrange("p (h c) -> p h c", h=4)
        ws_raw = num[:, 0:8, 0:P]
        lnb_bc = vals[:, 0:1024]
        bs_bc = gate_bc[:, :].rearrange("p (g t) -> p g t", g=8)
        expw = probs[:, :, :].rearrange("p a b -> p (a b)")
        xn = xc[:, :, :].rearrange("p (a b) t -> p a (b t)", a=2)
        gates_t = conv[:, 3, :]
        run = probs[0:4, :, :].rearrange("p a t -> p (a t)").rearrange("p (b n) -> p b n", b=2)
        rows = probs[:, 2, 0:P]
        c_row = conv[0:KT, 0, 0:P]
        block_diag = wts[:, 512:640].rearrange("p (b o) -> p b o", o=4)
        wqkv = wts[:, 640:688].rearrange("p (m h o) -> p m h o", m=3, h=4)
        wg_pad = num[:, :, :].rearrange("p a b -> p (a b)")[:, 1040:1424].rearrange("p (b r) -> p b r", r=32)
        tmp = conv
        OFF = [0, 512, 896, 1152]

        def col(name, n, k=1):
            r = ROWS[name][0] + n
            return cols[:, r:r + k]

        raw_in = [sem(f"raw_in{s}") for s in range(RAW)]
        ada_mult, ada_used = sem("ada_mult"), sem("ada_used")
        w_hi_ready, w_lo_ready = sem("w_hi_ready"), sem("w_lo_ready")
        even_half_done, acc_ready = sem("even_half_done"), sem("acc_ready")
        acc_freed_act, acc_freed_dve = sem("acc_freed_act"), sem("acc_freed_dve")
        rows_in, x_in, small_in, ws_in, wg_in = (sem("rows_in"), [sem(f"x_in{t}") for t in range(NT)],
                                                 sem("small_in"), sem("ws_in"), sem("wg_in"))
        consts, pool_step, dve_step, act_step = sem("consts"), sem("pool_step"), sem("dve_step"), sem("act_step")
        pool_prep = sem("pool_prep")
        rows_in_pool = sem("rows_in_pool")
        rows_t, cols_ready = sem("rows_t"), sem("cols_ready")
        c_in, c_psum, c_ready = sem("c_in"), sem("c_psum"), sem("c_ready")
        ss_ready, ln_ready, xn_ready = sem("ss_ready"), sem("ln_ready"), sem("xn_ready")
        var_ready = sem("var_ready")
        xt_psum, xt_evac = sem("xt_psum"), sem("xt_evac")
        wm_psum, wm_evac, sg_psum0, sg_ready = sem("wm_psum"), sem("wm_evac"), sem("sg_psum0"), sem("sg_ready")
        ada_evac, modc_psum, mod_ready = sem("ada_evac"), sem("modc_psum"), sem("mod_ready")
        gate_b_in, gate_psum, gate_ready = sem("gate_b_in"), sem("gate_psum"), sem("gate_ready")
        h_exact, h_hi, h_ready = sem("h_exact"), sem("h_hi"), sem("h_ready")
        conv_step, xc_ready = sem("conv_step"), sem("xc_ready")
        wvt_psum, wvt_ready, eff_psum, eff_ready = (sem("wvt_psum"), sem("wvt_ready"), sem("eff_psum"),
                                                    sem("eff_ready"))
        mv_psum, mv_evac, mqk_psum, mqk_evac = sem("mv_psum"), sem("mv_evac"), sem("mqk_psum"), sem("mqk_evac")
        skip_done = sem("skip_done")
        g_psum, g_evac, gt_psum, gt_abs, gt_ln, lf_ready = (sem("g_psum"), sem("g_evac"), sem("gt_psum"),
                                                            sem("gt_abs"), sem("gt_ln"), sem("lf_ready"))
        cum_psum, a_ready, at_psum, m_rows, mc_psum, mc_ready, guard_ready = (
            sem("cum_psum"), sem("a_ready"), sem("at_psum"), sem("m_rows"), sem("mc_psum"), sem("mc_ready"),
            sem("guard_ready"))
        mb_psum, mexp, st_psum, wt_mult, wt_ready, pv_psum, num_evac = (
            sem("mb_psum"), sem("mexp"), sem("st_psum"), sem("wt_mult"), sem("wt_ready"), sem("pv_psum"),
            sem("num_evac"))
        hb_ready, hbt_psum, yb_part = sem("hb_ready"), sem("hbt_psum"), sem("yb_part")
        q_evac, k_evac, qk_ss, qk_ln, k_norm = (sem("q_evac"), sem("k_evac"), sem("qk_ss"),
                                                sem("qk_ln"), sem("k_norm"))
        sq_used = sem("sq_used")
        qt_zero, qt_psum, kt_psum, qt_ready, kt_ready = (sem("qt_zero"), sem("qt_psum"), sem("kt_psum"),
                                                         sem("qt_ready"), sem("kt_ready"))
        s_psum, bias_ready, exp_ready, p_ready, pt_psum, pt_dve, pt_act, o_psum = (
            sem("s_psum"), sem("bias_ready"), sem("exp_ready"), sem("p_ready"), sem("pt_psum"), sem("pt_dve"),
            sem("pt_act"), sem("o_psum"))
        mvar_ready, mln_ready = sem("mvar_ready"), sem("mln_ready")
        az_exp, az_den, az_rec, o_evac = sem("az_exp"), sem("az_den"), sem("az_rec"), sem("o_evac")
        y_exact, y_hi, y_ready = sem("y_exact"), sem("y_hi"), sem("y_ready")
        h1_exact_act = sem("h1_exact_act")
        x1_ready, h1_psum, h1_exact, h1_hi, h1_ready = (sem("x1_ready"), sem("h1_psum"), sem("h1_exact"),
                                                        sem("h1_hi"), sem("h1_ready"))
        ss1_ready, var1_ready, ln1_ready, xn1_ready = (sem("ss1_ready"), sem("var1_ready"), sem("ln1_ready"),
                                                       sem("xn1_ready"))
        cvar_ready, cln_ready, vn_ready = sem("cvar_ready"), sem("cln_ready"), sem("vn_ready")
        sg_psum, us_ready = sem("sg_psum"), sem("us_ready")
        z1_exact, z1_hi, z1_ready = sem("z1_exact"), sem("z1_hi"), sem("z1_ready")
        out_ready, stored = sem("out_ready"), sem("stored")

        w_views = {"in": [w_in[l].rearrange("(k p) n -> p k n", p=P) for l in range(2)],
                   "out": [w_out[l].rearrange("(k p) n -> p k n", p=P) for l in range(2)]}
        ada_views = [ada_w[l].rearrange("(k p) n -> p k n", p=P) for l in range(2)]
        x_view = x[0].rearrange("(t p) d -> p t d", p=P)
        out_view = out[0].rearrange("(t p) d -> p t d", p=P)

        def landed(eng, item):
            n = PLACE[item]
            eng.wait_ge(raw_in[n % RAW], 16 * (n // RAW + 1))
            return n % RAW

        def half_done(eng, w):
            if w % 2:
                eng.wait_ge(acc_ready, 4 * (w // 2) + 4)
            else:
                eng.wait_ge(even_half_done, w // 2 + 1)

        def split_slot(w):
            s = w % SPLIT if w < L1 else (w + 1) % (SPLIT + 1)
            if s == SPLIT:
                return third[:, 0, :, :], third[:, 1, :, :]
            return w_hi[:, s, :, :], w_lo[:, s, :, :]

        def split_free(eng, w):
            if w == L1:
                eng.wait_ge(o_psum, 4)
            elif w >= SPLIT:
                half_done(eng, w - (SPLIT if w < L1 else SPLIT + 1))

        DVE_CHUNKS = [n for n, ch in enumerate(CHUNKS) if ch[5] in ("az", "y0", "y1")]

        def acc_free(eng, chunk, g):
            before = sum(n < chunk for n in DVE_CHUNKS)
            if chunk in DVE_CHUNKS:
                eng.wait_ge(acc_freed_dve, 4 * before + g + 1)
            else:
                eng.wait_ge(acc_freed_act, 4 * (chunk - before) + g + 1)

        def what(w):
            return CHUNKS[HALVES[w][0]][5]

        block = ctx.enter_context(nc.Block())

        @block.sync
        def _(sp):
            for t in range(NT):
                sp.dma_start(xres[:, t, :], x_view[:, t, :]).then_inc(x_in[t], 16)
            for n, (kind, m) in enumerate(STREAM):
                if n >= RAW:
                    before = STREAM[n - RAW]
                    if before[0] == "ada":
                        sp.wait_ge(ada_used, before[1] + 1)
                    else:
                        sp.wait_ge(w_lo_ready, PARTS * (before[1] + 1))
                if kind == "ada":
                    layer, cc = ADA[m // 2]
                    src = ada_views[layer][:, KH * (m % 2):KH * (m % 2) + KH, CH * cc:CH * cc + CH]
                else:
                    chunk, kh = HALVES[m]
                    mat, layer, cc = CHUNKS[chunk][:3]
                    src = w_views[mat][layer][:, KH * kh:KH * kh + KH, CH * cc:CH * cc + CH]
                sp.dma_start(raw[:, n % RAW, :, :], src).then_inc(raw_in[n % RAW], 16)
            for cc in range(2):
                for t in range(NT):
                    sp.wait_ge(out_ready, 4 * cc + t + 1)
                    sp.dma_start(out_view[:, t, CH * cc:CH * cc + CH],
                                 xres[:, t, CH * cc:CH * cc + CH]).then_inc(stored, 16)
            sp.wait_ge(stored, 16 * 8)

        @block.gpsimd
        def _(pool):
            count = [0]

            def link(ins):
                count[0] += 1
                ins.then_inc(pool_step, 1)
                pool.wait_ge(pool_step, count[0])

            link(pool.memset(ident[:], 0.0))
            pool.affine_select(out=ident[:], in_=ident[:], compare_op=ALU.not_equal, fill=1.0, base=0,
                               pattern=[[-1, P]], channel_multiplier=1).then_inc(consts, 1)
            link(pool.memset(c_pad[:], 0.0))
            pool.memset(ones[:], 1.0).then_inc(consts, 1)
            for name, a in (("conv_w", b_conv_w[0]), ("conv_b", b_conv_b), ("out_g", b_out_g), ("skip", b_skip),
                            ("c_ln_g", c_ln_g)):
                r, n = ROWS[name]
                pool.dma_start(rows[r:r + n, :], a.rearrange("l (j f) -> (l j) f", f=P)).then_inc(rows_in_pool, 16)
            for name, a in (("q_g", a_q_g), ("k_g", a_k_g)):
                r = ROWS[name][0]
                for e in range(2):
                    pool.dma_start(rows[r:r + 1, DA * e:DA * e + DA], a).then_inc(rows_in_pool, 16)
            link(pool.memset(ident_bf[:], 0.0))
            pool.affine_select(out=ident_bf[:], in_=ident_bf[:], compare_op=ALU.not_equal, fill=1.0, base=0,
                               pattern=[[-1, P]], channel_multiplier=1).then_inc(consts, 1)
            link(pool.memset(causal_bf[:], 0.0))
            pool.affine_select(out=causal_bf[:], in_=causal_bf[:], compare_op=ALU.is_ge, fill=NEG, base=0,
                               pattern=[[-1, P]], channel_multiplier=1).then_inc(consts, 1)
            link(pool.memset(upper[:], 1.0))
            pool.affine_select(out=upper[:], in_=upper[:], compare_op=ALU.is_ge, fill=0.0, base=0,
                               pattern=[[1, P]], channel_multiplier=-1).then_inc(consts, 1)
            link(pool.memset(wg_pad, 0.0))
            landed(pool, ("ada", 2 * len(ADA_FIRST) - 2))
            pool.dma_start(wg_pad[:, :, 0:8], b_w_gates[0].rearrange("(b p) r -> p b r", p=P)).then_inc(wg_in, 16)
            pool.dma_start(ws_raw, c_ws[0].rearrange("g t s -> t g s")).then_inc(ws_in, 16)
            pool.dma_start(lnb_bc, c_ln_b[0:1, :].to_broadcast((P, D))).then_inc(small_in, 16)
            pool.dma_start(gate_bc[:, :],
                           c_bs[0:1].rearrange("a g t -> a (g t)").to_broadcast((P, D))).then_inc(small_in, 16)
            pool.dma_start(bg_bc[:, :], b_b_gates[0:1, :].to_broadcast((P, 8))).then_inc(small_in, 16)
            for m, w in enumerate((b_wq, b_wk, b_wv)):
                pool.dma_start(wqkv[:, m, :, :],
                               w[0].rearrange("(h b) i o -> (b i) h o", h=4)).then_inc(small_in, 16)
            pool.wait_ge(ws_in, 16)
            pool.affine_select(out=ws_raw, in_=ws_raw, compare_op=ALU.is_ge, fill=0.0, base=0,
                               pattern=[[0, 8], [-1, P]], channel_multiplier=1).then_inc(pool_prep, 1)
            link(pool.memset(block_diag, 1.0))
            link(pool.affine_select(out=block_diag, in_=block_diag, compare_op=ALU.is_ge, fill=0.0, base=0,
                                    pattern=[[-4, 32], [0, 4]], channel_multiplier=1))
            link(pool.affine_select(out=block_diag, in_=block_diag, compare_op=ALU.is_ge, fill=0.0, base=3,
                                    pattern=[[4, 32], [0, 4]], channel_multiplier=-1))
            pool.wait_ge(small_in, 16 * 6)
            for m in (2, 0, 1):
                for h in range(4):
                    last = pool.tensor_tensor(
                        wbd[:, m, h, :].rearrange("p (b o) -> p b o", o=4),
                        wqkv[:, m, h:h + 1, :].to_broadcast((P, 32, 4)), block_diag, ALU.mult)
                last.then_inc(pool_prep, 1)
            for h in range(MH):
                last = pool.memset(bx[:, h, 0:3], 0.0)
            last.then_inc(pool_prep, 1)
            link(pool.memset(head_sel[:], 0.0))
            pool.affine_select(out=head_sel[:], in_=head_sel[:], compare_op=ALU.not_equal, fill=1.0, base=0,
                               pattern=[[-1, MH], [0, P]], channel_multiplier=1).then_inc(pool_prep, 1)
            link(pool.memset(gate_sel[:], 0.0))
            for g in range(4):
                link(pool.affine_select(out=gate_sel[:], in_=gate_sel[:], compare_op=ALU.not_equal, fill=1.0,
                                        base=-32 * g, pattern=[[-1, 8]], channel_multiplier=1))
            pool.wait_ge(sg_psum0, 8)
            pool.memset(mvals[:, :, :, P:P + 1], 1.0).then_inc(pool_prep, 1)
            pool.memset(neg_m[:], 0.0).then_inc(pool_prep, 1)
            pool.wait_ge(cols_ready, 1)
            pool.memset(run[:, :, 0:PAD], 0.0).then_inc(pool_prep, 1)

            def gate_bias(layer):
                pool.dma_start(gate_bc[:, :],
                               ada_b[layer:layer + 1, 2 * D:3 * D].to_broadcast((P, D))).then_inc(gate_b_in, 16)

            def ada_sum(n):
                row = ada_row[:, n % 2, :]
                m = n - 2
                if m in GATE_ITEMS:
                    pool.wait_ge(gate_psum, GATE_ITEMS.index(m) + 1)
                else:
                    pool.wait_ge(modc_psum, MOD_ITEMS.index(m) + 1)
                for kh in range(2):
                    s = landed(pool, ("ada", 2 * n + kh))
                    pool.wait_ge(ada_mult, 2 * (n - len(ADA_FIRST)) + kh + 1)
                    link(pool.tensor_tensor(raw[:, s, 0:2, :], raw[:, s, 0:2, :], raw[:, s, 2:4, :], ALU.add))
                    if kh:
                        link(pool.tensor_tensor(row, row, raw[:, s, 0, :], ALU.add))
                        pool.tensor_tensor(row, row, raw[:, s, 1, :], ALU.add).then_inc(ada_used, 1)
                    else:
                        pool.tensor_tensor(row, raw[:, s, 0, :], raw[:, s, 1, :], ALU.add).then_inc(ada_used, 1)
                        pool.wait_ge(ada_used, 2 * n + 1)

            pool.wait_ge(sg_ready, 2)
            gate_bias(0)
            ada_sum(4)
            ada_sum(5)
            ada_sum(6)
            ada_sum(7)

            for h in range(MH):
                for n, s in enumerate(S_ORDER):
                    pool.wait_ge(wt_mult, NT * h + n + 1)
                    blk = wts[:, OFF[s]:OFF[s] + P]
                    pool.affine_select(out=blk, in_=blk, compare_op=ALU.is_ge, fill=0.0, base=0,
                                       pattern=[[1, P]], channel_multiplier=-1).then_inc(wt_ready, 1)
            pool.wait_ge(st_psum, 4 * MH)
            pool.wait_ge(wt_ready, NT * MH)
            for e in range(2):
                if e:
                    pool.wait_ge(qt_zero, 1)
                pool.memset(xres[64 - 64 * e:P - 64 * e, :, CH * e:CH * e + CH], 0.0).then_inc(qt_zero, 1)
            ada_sum(8)
            ada_sum(9)
            ada_sum(10)
            acc_free(pool, Y0 + 1, 3)
            gate_bias(1)
            ada_sum(11)

        @block.tensor
        def _(pe):
            def group(w, g):
                chunk, kh = HALVES[w]
                layout, name = CHUNKS[chunk][4:6]
                first = kh == CHUNKS[chunk][3][0]
                if first and chunk:
                    acc_free(pe, chunk - 1, g)
                hi, lo = split_slot(w)
                for i in range(KH):
                    k = KH * kh + i
                    if g == 0 and i % 2 == 0:
                        pe.wait_ge(w_lo_ready, PARTS * w + i // 2 + 1)
                    if name in ("bx",) and g == 0:
                        pe.wait_ge(h_ready, k + 1)
                    if name == "y0" and chunk == 6 and g == 0:
                        pe.wait_ge(y_ready, (k - KH if kh else k + KH) + 1)
                    if name == "cv" and chunk == 8 and i == 0 and kh == 0:
                        pe.wait_ge(h1_ready, g + 1)
                    if name == "y1" and chunk == 14 and g == 0:
                        pe.wait_ge(z1_ready, k + 1)
                    parts = [(hi, act_hi), (hi, act_lo), (lo, act_hi)]
                    if layout == "token":
                        parts = [(hi, act_hi), (lo, act_hi), (hi, act_lo)]
                    for n, (wp, ap) in enumerate(parts):
                        if layout == "feature":
                            lhsT, rhs = wp[:, i, P * g:P * g + P], ap[:, k, :]
                        else:
                            lhsT, rhs = ap[:, k, P * g:P * g + P], wp[:, i, :]
                        last = pe.matmul(acc[g][:, :], lhsT, rhs, start=first and i == 0 and n == 0,
                                         stop=not first and i == KH - 1 and n == 2)
                if not first:
                    last.then_inc(acc_ready, 1)
                elif g == 3:
                    last.then_inc(even_half_done, 1)

            def ada_pair(n, bank):
                for kh in range(2):
                    s = landed(pe, ("ada", 2 * n + kh))
                    for j in range(4):
                        last = pe.matmul(bank[32 * j:32 * j + 32, :], c_pad[:, KH * kh + j, :], raw[:, s, j, :],
                                         start=kh == 0, stop=kh == 1, tile_position=(0, 32 * j))
                        if j == 3 and kh == 0:
                            last.then_inc(ada_used, 1)
                last.then_inc(ada_used, 1)

            def mod_cols(n, bank):
                pe.wait_ge(*((ada_evac, n + 1) if n < 4 else (ada_used, 2 * n + 2)))
                for q in range(4):
                    last = pe.matmul(bank[:, q:q + 1], ada_row[:, n % 2, P * q:P * q + P], ones[:, 0:1],
                                     start=True, stop=True)
                last.then_inc(modc_psum, 1)

            def gate_row(n, bank):
                pe.wait_ge(*((ada_evac, n + 1) if n < 4 else (ada_used, 2 * n + 2)))
                pe.matmul(bank[:, :], ones[:, :], ada_row[:, n % 2, :], start=True, stop=True).then_inc(gate_psum, 1)

            pe.wait_ge(consts, 2)
            pe.wait_ge(c_in, 16)
            pe.transpose(work[2][:, 0:KT], c_row, ident[0:KT, 0:KT]).then_inc(c_psum, 1)
            pe.wait_ge(c_ready, 1)
            ada_pair(0, work[2])
            for t in range(NT):
                if t == NT - 1:
                    ada_pair(1, work[3])
                pe.wait_ge(xn_ready, t + 1)
                for hf in range(2):
                    n = 2 * t + hf
                    if n >= 4:
                        pe.wait_ge(xt_evac, n - 3)
                    for q in range(4):
                        k = 4 * hf + q
                        last = pe.transpose(acc[n % 4][:, P * q:P * q + P], xres[:, t, P * k:P * k + P], ident[:, :])
                    last.then_inc(xt_psum, 1)
            pe.wait_ge(rows_in, 16 * 2)
            pe.wait_ge(rows_in_pool, 16 * 9)
            pe.transpose(work[0][:, 0:NROWS], rows[0:NROWS, :], ident[0:NROWS, 0:NROWS]).then_inc(rows_t, 1)
            for n in range(4):
                if n >= 2:
                    pe.wait_ge(mod_ready, n - 1)
                    ada_pair(n, work[2 + n % 2])
                mod_cols(n, work[2 + n % 2])

            def wm_transposes():
                pe.wait_ge(pool_prep, 1)
                pe.wait_ge(cols_ready, 1)
                for hf in range(2):
                    for q in range(4):
                        last = pe.transpose(work[hf][:, P * q:P * q + P], ws_raw[:, 4 * hf + q, :], ident[:, :])
                    last.then_inc(wm_psum, 1)

            def ln_b_sums():
                pe.wait_ge(small_in, 16 * 6)
                for g in range(8):
                    pe.wait_ge(wm_evac, g // 4 + 1)
                    pe.matmul(work[g // 4][:, P * (g % 4):P * (g % 4) + P], lnb_bc[:, P * g:P * g + P], wm[:, g, :],
                              start=True, stop=True).then_inc(sg_psum0, 1)

            def wv_transposes():
                pe.wait_ge(consts, 5)
                pe.wait_ge(pool_prep, 2)
                pe.wait_ge(sg_ready, 2)
                for h in range(4):
                    last = pe.transpose(work[0][:, P * h:P * h + P], wbd[:, 2, h, :], ident[:, :])
                last.then_inc(wvt_psum, 1)

            def gate_eff():
                pe.wait_ge(wvt_ready, 1)
                pe.wait_ge(wg_in, 16)
                for h in range(4):
                    last = pe.matmul(work[1][:, 8 * h:8 * h + 8], wvt[:, h, :], wg_pad[:, 8 + h, 0:8],
                                     start=True, stop=True)
                last.then_inc(eff_psum, 1)

            def m_values(t):
                if t == 0:
                    acc_free(pe, BX, 3)
                    pe.wait_ge(eff_ready, 1)
                if t == 3:
                    pe.wait_ge(mv_evac, 1)
                for h in range(MH):
                    last = pe.matmul(work[t % 3][:, P * h:P * h + P], bx[:, h, 3 + P * t:3 + P * t + P],
                                     wbd[:, 2, h, :], start=True, stop=True)
                last.then_inc(mv_psum, 1)

            def m_qk(n):
                pe.wait_ge(mv_evac, 4)
                pe.wait_ge(xc_ready, n % 4 + 1)
                pe.wait_ge(pool_prep, 4)
                if n >= 3:
                    pe.wait_ge(mqk_evac, n - 2)
                pe.matmul(work[n % 3][:, :], wbd[:, n // 4, n % 4, :], xc[:, n % 4, :],
                          start=True, stop=True).then_inc(mqk_psum, 1)

            def gates():
                pe.wait_ge(mqk_evac, 8)
                for part in range(3):
                    for h in range(MH):
                        rhs = (mq[:, h, :], mk[:, h, :], bx[:, h, 3:3 + T])[part]
                        last = pe.matmul(work[0][32 * h:32 * h + 32, :], wg_pad[:, 4 * part + h, :], rhs,
                                         start=part == 0, stop=part == 2, tile_position=(0, 32 * h))
                last.then_inc(g_psum, 1)

            def gates_tokens():
                pe.wait_ge(g_evac, 1)
                pe.wait_ge(pool_prep, 8)
                for t in range(NT):
                    last = pe.matmul(work[1][:, 8 * t:8 * t + 8], gates_t[:, P * t:P * t + P], gate_sel[:, :],
                                     start=True, stop=True)
                last.then_inc(gt_psum, 1)

            def cumulate():
                pe.wait_ge(lf_ready, 1)
                pe.matmul(work[2][:, 0:16], upper[:, :], gt[:, 4, :], start=True, stop=False)
                pe.matmul(work[2][:, 0:16], ones[:, :], pre[:, :, :].rearrange("p t h -> p (t h)"), start=False,
                          stop=True).then_inc(cum_psum, 1)

            def a_rows():
                pe.wait_ge(a_ready, 1)
                for t in range(NT):
                    last = pe.transpose(work[0][0:4, P * t:P * t + P], gt[:, 6, 4 * t:4 * t + 4], ident[:, :])
                last.then_inc(at_psum, 1)

            def m_cols():
                pe.wait_ge(m_rows, 1)
                for t in range(NT):
                    last = pe.transpose(work[1][:, 4 * t:4 * t + 4], neg_m[0:4, P * t:P * t + P], ident[0:4, 0:4])
                last.then_inc(mc_psum, 1)

            def m_scores(h):
                if h == 0:
                    pe.wait_ge(mc_ready, 1)
                else:
                    pe.wait_ge(wt_mult, NT * h)
                    pe.wait_ge(num_evac, 2 * h)
                pe.matmul(work[0][:, :], head_sel[:, h, :], neg_m[:, :], start=True, stop=True).then_inc(mb_psum, 1)
                for s, bank, at in ((0, 1, 0), (1, 2, 0), (3, 2, 384)):
                    n = T - P * s
                    pe.matmul(work[bank][:, at:at + n], mk[:, h, P * s:P * s + P], mq[:, h, P * s:T],
                              start=True, stop=True).then_inc(st_psum, 1)

            def m_scores2(h):
                pe.wait_ge(mexp, NT * (h + 1))
                pe.matmul(work[0][:, 0:256], mk[:, h, 256:384], mq[:, h, 256:T], start=True,
                          stop=True).then_inc(st_psum, 1)

            def m_values_out(h):
                pe.wait_ge(wt_ready, NT * (h + 1))
                for t in range(NT):
                    bank = work[1 + t // 2]
                    at = 256 * (t % 2)
                    for s in range(t + 1):
                        o = OFF[s] + P * (t - s)
                        last = pe.matmul(bank[:, at:at + P + 1], wts[:, o:o + P], mvals[:, s, h, 0:P + 1],
                                         start=s == 0, stop=s == t)
                    if t % 2:
                        last.then_inc(pv_psum, 1)

            def hb_transposes(h):
                if h == 0:
                    pe.wait_ge(hb_ready, 1)
                    pe.wait_ge(mod_ready, 6)
                else:
                    pe.wait_ge(yb_part, h)
                for t in range(NT):
                    last = pe.transpose(work[3][:, P * t:P * t + P], num[:, 4 * t + h, 0:P], ident[:, :])
                last.then_inc(hbt_psum, 1)

            def qk_transposes(n):
                if n == 0:
                    pe.wait_ge(q_evac, 4)
                    pe.wait_ge(num_evac, 2 * MH)
                if n == 4:
                    pe.wait_ge(k_norm, 4)
                if 2 <= n < 6:
                    pe.wait_ge(qt_ready, n - 1)
                if n >= 6:
                    pe.wait_ge(kt_ready, n - 5)
                src = q_raw if n < 4 else k_raw
                p = n % 4
                for t in range(NT):
                    last = pe.transpose(work[n % 2][:, P * t:P * t + P], src[:, t, P * p:P * p + P], ident[:, :])
                last.then_inc(qt_psum if n < 4 else kt_psum, 1)

            def a_scores(u):
                h, i, e = UNITS[u]
                if u < 2:
                    pe.wait_ge(qt_ready, 4)
                    pe.wait_ge(kt_ready, 4)
                    pe.wait_ge(qt_zero, 2)
                else:
                    pe.wait_ge(exp_ready, u - 1)
                n = P * (i + 1)
                bank = work[u % 2]
                pe.matmul(bank[:, 0:n], qt[:, h, P * i:P * i + P], kt[:, h // 2, 0:n], start=True, stop=False)
                pe.matmul(bank[:, n - P:n], ident_bf[:, :], causal_bf[:, :], start=False,
                          stop=True).then_inc(s_psum, 1)

            def p_transposes(u):
                h, i, e = UNITS[u]
                pe.wait_ge(p_ready, u + 1)
                if u:
                    pt_done(pe, u - 1)
                for j in range(i + 1):
                    last = pe.transpose(work[2][:, P * j:P * j + P], probs[:, u % 3, P * j:P * j + P], ident[:, :])
                last.then_inc(pt_psum, 1)

            def a_values(p):
                pt_done(pe, 8 * p + 7)
                pt_done(pe, 8 * p + 6)
                if p == 0:
                    acc_free(pe, AV, 3)
                    pe.wait_ge(yb_part, 4)
                else:
                    pe.wait_ge(o_evac, p)
                for j in range(NT):
                    for e in range(2):
                        h = 2 * p + e
                        last = pe.matmul(work[3][64 * e:64 * e + 64, P * j:T], avals[:, j, DA * h:DA * h + DA],
                                         probs_t[:, e, j, P * j:T], start=j == 0, stop=j == NT - 1)
                last.then_inc(o_psum, 1)

            def pt_done(eng, u):
                n = sum(PT_ON_ACT(v) for v in range(u + 1))
                if PT_ON_ACT(u):
                    eng.wait_ge(pt_act, n)
                else:
                    eng.wait_ge(pt_dve, u + 1 - n)

            def attention(u):
                if u < NU:
                    a_scores(u)
                if u >= LAG and (u - LAG) % 8 == 0 and u - LAG > 0:
                    a_values((u - LAG) // 8 - 1)
                if LAG <= u < NU + LAG:
                    p_transposes(u - LAG)

            def h1_transposes(t):
                pe.wait_ge(xn1_ready, t + 1)
                if t:
                    pe.wait_ge(h1_exact, 4 * t)
                    pe.wait_ge(h1_exact_act, 4 * t)
                for k in range(KT):
                    last = pe.transpose(work[k // 4][:, P * (k % 4):P * (k % 4) + P], xn[:, t % 2, P * k:P * k + P],
                                        ident[:, :])
                last.then_inc(h1_psum, 1)

            def spatial(g):
                pe.wait_ge(vn_ready, 4)
                if g >= 3:
                    pe.wait_ge(us_ready, g - 2)
                for t in range(NT):
                    last = pe.matmul(work[g % 3][:, P * t:P * t + P], vg[:, t, P * g:P * g + P], wm[:, g, :],
                                     start=True, stop=True)
                last.then_inc(sg_psum, 1)

            def small_jobs(here):
                if here == PLACES["spatial weights"]:
                    wm_transposes()
                if here == PLACES["ln_b sums"]:
                    ln_b_sums()
                if here == PLACES["wv transposes"]:
                    wv_transposes()
                if here == PLACES["gate fold"]:
                    gate_eff()
                for t in range(NT):
                    if here == PLACES["mLSTM values"][t]:
                        m_values(t)
                for n in range(8):
                    if here == PLACES["mLSTM q, k"][n]:
                        m_qk(n)
                if here == PLACES["gates"]:
                    gates()
                if here == PLACES["gate columns"]:
                    gates_tokens()
                if here == PLACES["running sums"]:
                    cumulate()
                if here == PLACES["running max"]:
                    a_rows()
                if here == PLACES["max columns"]:
                    m_cols()
                for h in range(MH):
                    for n, job in enumerate((m_scores, m_scores2, m_values_out)):
                        slot = HEAD_SLOT + 3 * h + n
                        if here == (slot // 4, slot % 4):
                            job(h)
                for n in range(8):
                    if here == PLACES["q, k transposes"][n]:
                        qk_transposes(n)
                for p, slot in enumerate(PLACES["mLSTM outputs"]):
                    if here == slot:
                        hb_transposes(p)
                for u in ATT_SLOTS.get(here, ()):
                    attention(u)
                for t, slot in enumerate(((15, 1), (15, 2), (15, 3), (16, 1))):
                    if here == slot:
                        h1_transposes(t)
                for g in range(8):
                    if here == PLACES["spatial"][g]:
                        spatial(g)
                bank3_free = {4: (mod_ready, 4), 5: (gate_ready, 1), 6: (gate_ready, 2), 7: (mod_ready, 5),
                              8: (o_evac, 4), 9: (mod_ready, 7), 10: (mod_ready, 8), 11: (gate_ready, 3)}

                def ada_use(n):
                    pe.wait_ge(*bank3_free[n])
                    (mod_cols if n in MOD_ITEMS else gate_row)(n, work[3])

                for n in range(4, 12):
                    if here == ADA_USE_SLOT[n]:
                        ada_use(n)

            for w in range(NHALF):
                if w == L1 - 2:
                    continue
                for g in range(4):
                    if w == L1 - 1:
                        group(w - 1, g)
                        small_jobs((w - 1, g))
                    group(w, g)
                    small_jobs((w, g))

        @block.scalar
        def _(act_e):
            count = [0]

            def link(ins):
                count[0] += 1
                ins.then_inc(act_step, 1)
                act_e.wait_ge(act_step, count[0])

            def copy(dst, src):
                return nc.scalar.activation(dst, src, ACT.Copy)

            def rsqrt(y, v, ready, n, done):
                act_e.wait_ge(ready, n)
                link(nc.scalar.activation(y, v, ACT.Ln))
                nc.scalar.activation(y, y, ACT.Exp, scale=-0.5).then_inc(done, 1)

            def split_hi(w):
                s = landed(act_e, ("w", w))
                split_free(act_e, w)
                for a in range(PARTS):
                    copy(split_slot(w)[0][:, 2 * a:2 * a + 2, :], raw[:, s, 2 * a:2 * a + 2, :]).then_inc(w_hi_ready, 1)

            def ada_out(n):
                act_e.wait_ge(ada_used, 2 * n + 2)
                copy(ada_row[:, n % 2, :], work[2 + n % 2][:, :]).then_inc(ada_evac, 1)

            def ada_mul(n, kh):
                s = landed(act_e, ("ada", 2 * n + kh))
                for j in range(KH):
                    k = KH * kh + j
                    ins = nc.scalar.activation(raw[:, s, j, :], raw[:, s, j, :], ACT.Copy, scale=c_pad[:, k, 0:1])
                ins.then_inc(ada_mult, 1)

            act_e.dma_start(c_row, c.rearrange("l (j f) -> (l j) f", f=P)).then_inc(c_in, 16)
            flat = [("ada_b", ada_b), ("ln_g", ln_g)]
            for name, a in flat:
                r, n = ROWS[name]
                act_e.dma_start(rows[r:r + n, :], a.rearrange("l (j f) -> (l j) f", f=P)).then_inc(rows_in, 16)
            nc.scalar.preload_act_table_set("silu_and_others")
            act_e.wait_ge(c_psum, 1)
            nc.scalar.activation(c_pad[:, :, 0], work[2][:, 0:KT], ACT.Silu).then_inc(c_ready, 1)
            for t in range(NT):
                act_e.wait_ge(x_in[t], 16)
                nc.scalar.activation(act[:, 2 * t:2 * t + 2, :].rearrange("p a b -> p (a b)"), xres[:, t, :],
                                     ACT.Square, accum_out=rms[:, 0, t:t + 1]).then_inc(ss_ready, 1)
            nc.scalar.preload_act_table_set(LNEXP)
            rsqrt(rms[:, 2, 0:4], rms[:, 1, 0:4], var_ready, 1, ln_ready)
            ada_out(0)
            for n in range(8):
                act_e.wait_ge(xt_psum, n + 1)
                t, hf = n // 2, n % 2
                copy(act[:, 4 * hf:4 * hf + 4, P * t:P * t + P],
                     acc[n % 4][:, :].rearrange("p (k q) -> p k q", k=4)).then_inc(xt_evac, 1)
            ada_out(1)
            split_hi(0)
            ada_out(2)
            ada_out(3)
            for k in range(KT):
                act_e.wait_ge(h_exact, k + 1)
                copy(act_hi[:, k, :], act[:, k, :]).then_inc(h_hi, 1)

            def acc_wait(w, g):
                act_e.wait_ge(acc_ready, 4 * (w // 2) + g + 1)

            def wm_out():
                for hf in range(2):
                    act_e.wait_ge(wm_psum, hf + 1)
                    copy(wm[:, 4 * hf:4 * hf + 4, :],
                         work[hf][:, :].rearrange("p (k q) -> p k q", k=4)).then_inc(wm_evac, 1)

            def bx_out(g):
                acc_wait(1, g)
                copy(bx[:, g, 3:3 + T], acc[g][:, :]).then_inc(acc_freed_act, 1)

            def gate_act(w, g, k):
                acc_wait(w, g)
                nc.scalar.activation(act[:, k, :], acc[g][:, :], ACT.Silu).then_inc(acc_freed_act, 1)

            def mv_out(t):
                act_e.wait_ge(mv_psum, t + 1)
                if t == 0:
                    act_e.wait_ge(pool_prep, 7)
                copy(mvals[:, t, :, 0:P], work[t % 3][:, :].rearrange("p (h v) -> p h v", h=MH)).then_inc(mv_evac, 1)

            def xc_out(h):
                act_e.wait_ge(conv_step, 4 * h + 4)
                nc.scalar.activation(xc[:, h, :], conv[:, h, :], ACT.Silu).then_inc(xc_ready, 1)

            def mqk_out(n):
                act_e.wait_ge(mqk_psum, n + 1)
                copy((mq if n < 4 else mk)[:, n % 4, :], work[n % 3][:, :]).then_inc(mqk_evac, 1)

            def gates_out():
                act_e.wait_ge(g_psum, 1)
                copy(gates_t[:, :], work[0][:, :]).then_inc(g_evac, 1)

            def gates_log():
                nc.scalar.preload_act_table_set(LNEXP)
                act_e.wait_ge(gt_abs, 1)
                link(nc.scalar.activation(gt[:, 3, :], gt[:, 2, :], ACT.Exp, scale=-1.0))
                nc.scalar.activation(gt[:, 3, :], gt[:, 3, :], ACT.Ln, bias=1.0).then_inc(gt_ln, 1)

            def guard():
                act_e.wait_ge(mc_ready, 1)
                nc.scalar.activation(gt[:, 9, :], gt[:, 7, :], ACT.Exp).then_inc(guard_ready, 1)

            def m_exps(h):
                act_e.wait_ge(mb_psum, h + 1)
                for s in S_ORDER:
                    n = T - P * s
                    nc.scalar.activation(expw[:, OFF[s]:OFF[s] + n], work[0][:, P * s:T], ACT.Exp,
                                         bias=gt[:, 6, 4 * s + h:4 * s + h + 1]).then_inc(mexp, 1)

            def num_out(h):
                for a in range(2):
                    act_e.wait_ge(pv_psum, 2 * h + a + 1)
                    dst = num[:, :, :].rearrange("p (t h) v -> p t h v", t=NT)[:, 2 * a:2 * a + 2, h, 0:P + 1]
                    src = work[1 + a][:, :].rearrange("p (t v) -> p t v", t=2)[:, :, 0:P + 1]
                    copy(dst, src).then_inc(num_evac, 1)

            def qk_out(w, g, dst, evac):
                n = g + (4 if dst is k_raw else 0)
                acc_wait(w, g)
                copy(dst[:, g, :], acc[g][:, :]).then_inc(evac, 1)
                if n >= 2:
                    act_e.wait_ge(sq_used, n - 1)
                nc.scalar.activation(conv[:, n % 2, :], acc[g][:, :], ACT.Square).then_inc(acc_freed_act, 1)

            def v_out(g):
                acc_wait(9, g)
                copy(avals[:, g, :], acc[g][:, :]).then_inc(acc_freed_act, 1)

            def az_exp_out(g):
                acc_wait(11, g)
                if g >= 2:
                    acc_free(act_e, AZ, g - 2)
                nc.scalar.activation(wts[:, 512 * (g % 2):512 * (g % 2) + 512], acc[g][:, :], ACT.Exp,
                                     scale=-1.0).then_inc(az_exp, 1)

            def az_rec_out(g):
                act_e.wait_ge(az_den, g + 1)
                e = wts[:, 512 * (g % 2):512 * (g % 2) + 512]
                link(nc.scalar.activation(e, e, ACT.Ln))
                nc.scalar.activation(e, e, ACT.Exp, scale=-1.0).then_inc(az_rec, 1)

            def x_again():
                act_e.wait_ge(s_psum, NU)
                for t in range(NT):
                    act_e.dma_start(xres[:, t, :], x_view[:, t, :]).then_inc(x_in[t], 16)

            def qt_out(p):
                act_e.wait_ge(qt_psum, p + 1)
                for e in range(2):
                    r = slice(64 * e, 64 * e + 64)
                    last = nc.scalar.activation(qt[r, 2 * p + e, :], work[p % 2][r, :], ACT.Copy,
                                                scale=col("q_g", 0)[r])
                last.then_inc(qt_ready, 1)

            def attention(u):
                if u < NU:
                    h, i, e = UNITS[u]
                    n = P * (i + 1)
                    act_e.wait_ge(bias_ready, u + 1)
                    if u >= 3:
                        act_e.wait_ge(pt_psum, u - 2)
                    q = 8 * i + h
                    nc.scalar.activation(probs[:, u % 3, 0:n], work[u % 2][:, 0:n], ACT.Exp, bias=mx[:, 1, u:u + 1],
                                         scale=qs[:, 4, q:q + 1], accum_out=rs[:, 0, u:u + 1]).then_inc(exp_ready, 1)
                v = u - LAG
                if 0 <= v < NU and PT_ON_ACT(v):
                    h, i, e = UNITS[v]
                    act_e.wait_ge(pt_psum, v + 1)
                    copy(probs_t[:, e, 0:i + 1, P * i:P * i + P],
                         work[2][:, 0:P * (i + 1)].rearrange("p (j q) -> p j q", j=i + 1)).then_inc(pt_act, 1)
                if u in YA_SPLIT:
                    y_hi_part(4 + YA_SPLIT[u])

            def y_hi_part(n):
                k = Y_ORDER[n]
                half_done(act_e, 10 if k >= KH else 11)
                if n < 4:
                    act_e.wait_ge(y_exact, n + 1)
                elif n - 4 < O_FIRST:
                    acc_free(act_e, AZ, n - 4)
                else:
                    act_e.wait_ge(o_evac, n - 3)
                copy(act_hi[:, k, :], act[:, k, :]).then_inc(y_hi, 1)

            def x1_square(t):
                act_e.wait_ge(x1_ready, t + 1)
                nc.scalar.activation(probs[:, :, :].rearrange("p a b -> p (a b)")[:, 0:D], xres[:, t, :], ACT.Square,
                                     accum_out=rms[:, 0, 4 + t:5 + t]).then_inc(ss1_ready, 1)
                rsqrt(rms[:, 2, 4 + t:5 + t], rms[:, 1, 4 + t:5 + t], var1_ready, t + 1, ln1_ready)

            def h1_act_part(t):
                act_e.wait_ge(h1_psum, t + 1)
                act_e.wait_ge(mod_ready, 8)
                for k in range(KH, KT):
                    nc.scalar.activation(act[:, k, P * t:P * t + P], work[1][:, P * (k - KH):P * (k - KH) + P],
                                         ACT.Identity, bias=mod[:, 1, k:k + 1],
                                         scale=gain[:, 1, k:k + 1]).then_inc(h1_exact_act, 1)

            def h1_hi_part(t):
                act_e.wait_ge(h1_exact, 4 * (t + 1))
                act_e.wait_ge(h1_exact_act, 4 * (t + 1))
                copy(act_hi[:, :, P * t:P * t + P], act[:, :, P * t:P * t + P]).then_inc(h1_hi, 1)

            def gelu_v(w, g):
                cc = (w - 17) // 2
                acc_wait(w, g)
                nc.scalar.activation(vg[:, g, CH * cc:CH * cc + CH], acc[g][:, :],
                                     ACT.Gelu_apprx_tanh).then_inc(acc_freed_act, 1)

            def cv_rsqrt():
                nc.scalar.preload_act_table_set(LNEXP)
                rsqrt(rms[:, 2, 0:4], rms[:, 1, 0:4], cvar_ready, 1, cln_ready)
                nc.scalar.preload_act_table_set("gelu_apprx_tanh_and_others")

            def gelu_u(w, g):
                acc_wait(w, g)
                k = g + 4 * ((w - 21) // 2)
                nc.scalar.activation(act[:, k, :], acc[g][:, :], ACT.Gelu_apprx_tanh).then_inc(acc_freed_act, 1)

            def silu_z(w, g):
                n = g + 4 * ((w - 25) // 2)
                acc_wait(w, g)
                if n >= 4:
                    act_e.wait_ge(z1_exact, n - 3)
                nc.scalar.activation(tmp[:, n % 4, :], acc[g][:, :], ACT.Silu).then_inc(acc_freed_act, 1)

            def z1_hi_part(k):
                half_done(act_e, 26 if k < KH else 27)
                act_e.wait_ge(z1_exact, k + 1)
                copy(act_hi[:, k, :], act[:, k, :]).then_inc(z1_hi, 1)

            def small_jobs(here):
                if here == PLACES["spatial weights"]:
                    wm_out()
                for g in range(4):
                    if here == (1, g):
                        bx_out(g)
                    if here == PLACES["mLSTM values"][g]:
                        mv_out(g)
                    if here == (3, g):
                        gate_act(3, g, 4 + g)
                    if here == (5, g):
                        qk_out(5, g, q_raw, q_evac)
                    if here == (7, g):
                        qk_out(7, g, k_raw, k_evac)
                    if here == (9, g):
                        v_out(g)
                    if here == (17, g):
                        gelu_v(17, g)
                    if here == (19, g):
                        gelu_v(19, g)
                    if here == (21, g):
                        gelu_u(21, g)
                    if here == (23, g):
                        gelu_u(23, g)
                    if here == (25, g):
                        silu_z(25, g)
                    if here == (27, g):
                        silu_z(27, g)
                if here == (1, 3):
                    nc.scalar.preload_act_table_set("silu_and_others")
                for h in range(MH):
                    if here == (2, 0):
                        xc_out(h)
                for n in range(8):
                    if here == PLACES["mLSTM q, k"][n]:
                        mqk_out(n)
                if here == PLACES["gates"]:
                    gates_out()
                if here == PLACES["gate logs"]:
                    gates_log()
                if here == PLACES["max columns"]:
                    guard()
                for h in range(MH):
                    s0, s2 = HEAD_SLOT + 3 * h, HEAD_SLOT + 3 * h + 2
                    if here == (s0 // 4, s0 % 4):
                        m_exps(h)
                    if here == (s2 // 4, s2 % 4):
                        num_out(h)
                if here == PLACES["q, k norms"]:
                    rsqrt(qs[:, 2, :], qs[:, 1, :], qk_ss, 1, qk_ln)
                for p in range(4):
                    if here == PLACES["q, k transposes"][p]:
                        qt_out(p)
                if here == PLACES["mLSTM normalised"]:
                    rsqrt(gt[:, 9, :], gt[:, 8, :], mvar_ready, 1, mln_ready)
                for g in range(4):
                    if here == (11, g):
                        az_exp_out(g)
                for u in ATT_SLOTS.get(here, ()):
                    attention(u)
                for g in range(4):
                    if here == (11, g):
                        az_rec_out(g)
                for n in range(4 + O_FIRST):
                    if here == ((11, n // 2) if n < 4 else (11, 3)):
                        y_hi_part(n)
                if here == (12, 2):
                    x_again()
                if here in [(15, t) for t in range(NT)]:
                    t = here[1]
                    if t:
                        h1_act_part(t - 1)
                    x1_square(t)
                    if t:
                        h1_hi_part(t - 1)
                if here == (15, 3):
                    h1_act_part(3)
                    h1_hi_part(3)
                    split_hi(L1 + 1)
                if here == (16, 1):
                    nc.scalar.preload_act_table_set("gelu_apprx_tanh_and_others")
                if here == (20, 0):
                    cv_rsqrt()
                if here == (24, 0):
                    nc.scalar.preload_act_table_set("silu_and_others")
                for k in range(KT):
                    if here == ((27, -1) if k < KH else (27, 3)):
                        z1_hi_part(k)
                for n in ADA_LANDS:
                    for kh in range(2):
                        if here == ADA_MUL_SLOT[n][kh]:
                            ada_mul(n, kh)

            for w in range(NHALF):
                for g in range(-1, 4):
                    if g == -1 and w + 1 < NHALF and w != L1:
                        split_hi(w + 1)
                    small_jobs((w, g))

        @block.vector
        def _(dve):
            v_e = nc.vector
            count = [0]

            def link(ins):
                count[0] += 1
                ins.then_inc(dve_step, 1)
                dve.wait_ge(dve_step, count[0])

            def refine(y, v, t):
                link(v_e.tensor_tensor(t, y, y, ALU.mult))
                link(v_e.tensor_tensor(t, t, v, ALU.mult))
                link(v_e.tensor_scalar(t, t, -0.5, 1.5, ALU.mult, ALU.add))
                link(v_e.tensor_tensor(y, y, t, ALU.mult))

            def minus(dst, whole, hi):
                return v_e.tensor_tensor(dst, whole, hi.bitcast(F32), ALU.subtract)

            def split_lo(w):
                s = landed(dve, ("w", w))
                for a in range(PARTS):
                    dve.wait_ge(w_hi_ready, PARTS * w + a + 1)
                    ks = slice(2 * a, 2 * a + 2)
                    hi, lo = split_slot(w)
                    minus(lo[:, ks, :], raw[:, s, ks, :], hi[:, ks, :]).then_inc(w_lo_ready, 1)

            def mod_out(n):
                layer, cc = ADA[n]
                dve.wait_ge(modc_psum, MOD_ITEMS.index(n) + 1)
                dst = mod[:, layer, 4 * cc:4 * cc + 4]
                ins = v_e.tensor_tensor(dst, work[2 + n % 2 if n < 4 else 3][:, 0:4],
                                        col("ada_b", 24 * layer + 4 * cc, 4), ALU.add)
                if cc >= 2:
                    link(ins)
                    ins = v_e.scalar_tensor_tensor(out=gain[:, layer, 4 * cc - 8:4 * cc - 4], in0=dst, scalar=1.0,
                                                   in1=col("ln_g", 8 * layer + 4 * cc - 8, 4), op0=ALU.add,
                                                   op1=ALU.mult)
                ins.then_inc(mod_ready, 1)

            def gate_out(n):
                cc = ADA[n][1]
                dve.wait_ge(gate_psum, GATE_ITEMS.index(n) + 1)
                dve.wait_ge(gate_b_in, 16 * (ADA[n][0] + 1))
                dst = gate_bc[:, CH * (cc - 4):CH * (cc - 3)]
                v_e.tensor_tensor(dst, work[3][:, :], dst, ALU.add).then_inc(gate_ready, 1)

            dve.wait_ge(ss_ready, NT)
            v_e.tensor_scalar(rms[:, 1, 0:4], rms[:, 0, 0:4], 1.0 / D, 1e-6, ALU.mult, ALU.add).then_inc(var_ready, 1)
            dve.wait_ge(ln_ready, 1)
            refine(rms[:, 2, 0:4], rms[:, 1, 0:4], rms[:, 3, 0:4])
            for t in range(NT):
                v_e.tensor_scalar(xres[:, t, :], xres[:, t, :], rms[:, 2, t:t + 1], None,
                                  ALU.mult).then_inc(xn_ready, 1)
            dve.wait_ge(rows_t, 1)
            v_e.tensor_copy(cols[:, :], work[0][:, 0:NROWS]).then_inc(cols_ready, 1)
            dve.wait_ge(cols_ready, 1)
            mod_out(0)
            for n in range(1, 4):
                if n == 2:
                    split_lo(0)
                mod_out(n)
            dve.wait_ge(mod_ready, 4)
            dve.wait_ge(xt_evac, 8)

            def h_part(k):
                v_e.tensor_scalar(act[:, k, :], act[:, k, :], gain[:, 0, k:k + 1], mod[:, 0, k:k + 1], ALU.mult,
                                  ALU.add).then_inc(h_exact, 1)

            def h_lo_part(k):
                dve.wait_ge(h_hi, k + 1)
                minus(act_lo[:, k, :], act[:, k, :], act_hi[:, k, :]).then_inc(h_ready, 1)

            h_part(0)
            h_part(1)
            for k in range(KT):
                if k + 2 < KT:
                    h_part(k + 2)
                h_lo_part(k)

            def wvt_out():
                dve.wait_ge(wvt_psum, 1)
                v_e.tensor_copy(wvt, work[0][:, :].rearrange("p (h c) -> p h c", h=4)).then_inc(wvt_ready, 1)

            def sg_out():
                dve.wait_ge(small_in, 16 * 6)
                for a in range(2):
                    dve.wait_ge(sg_psum0, 4 * a + 4)
                    v_e.tensor_tensor(sg_add[:, 4 * a:4 * a + 4, :], work[a][:, :].rearrange("p (g t) -> p g t", g=4),
                                      bs_bc[:, 4 * a:4 * a + 4, :], ALU.add).then_inc(sg_ready, 1)

            def eff_out():
                dve.wait_ge(eff_psum, 1)
                v_e.tensor_copy(wg_pad[:, 8:12, 0:8],
                                work[1][:, 0:32].rearrange("p (h r) -> p h r", h=4)).then_inc(eff_ready, 1)

            def conv_tap(j, h):
                w = col("conv_w", 4 * j + h)
                if j == 0:
                    acc_free(dve, BX, h)
                    dve.wait_ge(pool_prep, 5)
                    ins = v_e.tensor_scalar(conv[:, h, :], bx[:, h, 0:T], w, col("conv_b", h), ALU.mult, ALU.add)
                else:
                    dve.wait_ge(conv_step, 4 * h + j)
                    ins = v_e.scalar_tensor_tensor(out=conv[:, h, :], in0=bx[:, h, j:j + T], scalar=w,
                                                   in1=conv[:, h, :], op0=ALU.mult, op1=ALU.add)
                ins.then_inc(conv_step, 1)

            def skip_part():
                dve.wait_ge(mqk_psum, 8)
                for h in range(MH):
                    last = v_e.tensor_scalar(xc[:, h, :], xc[:, h, :], col("skip", h), None, ALU.mult)
                last.then_inc(skip_done, 1)

            def gates_add():
                dve.wait_ge(gt_psum, 1)
                for m in range(2):
                    ins = v_e.tensor_tensor(
                        gt[:, m, :].rearrange("p (t h) -> p t h", t=NT),
                        work[1][:, 0:32].rearrange("p (t r) -> p t r", t=NT)[:, :, 4 * m:4 * m + 4],
                        bg_bc[:, 4 * m:4 * m + 4].unsqueeze(1).to_broadcast((P, NT, 4)), ALU.add)
                link(ins)
                v_e.scalar_tensor_tensor(out=gt[:, 2, :], in0=gt[:, 1, :], scalar=-1.0, in1=gt[:, 1, :],
                                         op0=ALU.mult, op1=ALU.max).then_inc(gt_abs, 1)

            def log_forget():
                dve.wait_ge(gt_ln, 1)
                link(v_e.scalar_tensor_tensor(out=gt[:, 4, :], in0=gt[:, 1, :], scalar=0.0, in1=gt[:, 3, :],
                                              op0=ALU.min, op1=ALU.subtract))
                v_e.memset(pre[:, 0, :], 0.0)
                link(v_e.tensor_copy(pre[:, 1, :], gt[:, 4, 0:4]))
                link(v_e.tensor_tensor(pre[:, 2, :], pre[:, 1, :], gt[:, 4, 4:8], ALU.add))
                v_e.tensor_tensor(pre[:, 3, :], pre[:, 2, :], gt[:, 4, 8:12], ALU.add).then_inc(lf_ready, 1)

            def a_cols():
                dve.wait_ge(cum_psum, 1)
                v_e.tensor_copy(gt[:, 5, :], work[2][:, 0:16])
                v_e.tensor_tensor(gt[:, 6, :], gt[:, 0, :], work[2][:, 0:16], ALU.subtract).then_inc(a_ready, 1)

            def running_max():
                dve.wait_ge(at_psum, 1)
                dve.wait_ge(pool_prep, 9)
                link(v_e.tensor_scalar(run[:, 0, PAD:PAD + T], work[0][0:4, :], 0.0, None, ALU.max))
                b, d = 0, 1
                while d < T:
                    link(v_e.tensor_tensor(run[:, 1 - b, PAD:PAD + T], run[:, b, PAD:PAD + T],
                                           run[:, b, PAD - d:PAD + T - d], ALU.max))
                    b, d = 1 - b, 2 * d
                v_e.tensor_scalar(neg_m[0:4, :], run[:, b, PAD:PAD + T], -1.0, None, ALU.mult).then_inc(m_rows, 1)

            def m_exponent():
                dve.wait_ge(mc_psum, 1)
                v_e.tensor_tensor(gt[:, 7, :], work[1][:, 0:16], gt[:, 5, :], ALU.subtract).then_inc(mc_ready, 1)

            def weights(h, part):
                if part == 0 and h:
                    dve.wait_ge(pv_psum, 2 * h)
                for n, s in enumerate(S_ORDER):
                    if (n == 3) != (part == 1):
                        continue
                    dve.wait_ge(st_psum, NT * h + (1, 3, 3, 4)[n])
                    dve.wait_ge(mexp, NT * h + n + 1)
                    bank, at_ = {0: (1, 0), 1: (2, 0), 3: (2, 384), 2: (0, 0)}[s]
                    m = T - P * s
                    v_e.scalar_tensor_tensor(out=wts[:, OFF[s]:OFF[s] + m], in0=work[bank][:, at_:at_ + m],
                                             scalar=float(P) ** -0.5, in1=expw[:, OFF[s]:OFF[s] + m], op0=ALU.mult,
                                             op1=ALU.mult).then_inc(wt_mult, 1)

            def head_stats(h):
                dve.wait_ge(num_evac, 2 * h + 2)
                for t in range(NT):
                    ins = v_e.bn_stats(st6[:, 4 * t + h, :], num[:, 4 * t + h, 0:P])
                link(ins)
                for t in range(NT):
                    ins = v_e.bn_aggr(mv2[:, 4 * t + h, :], st6[:, 4 * t + h, :])
                if h == MH - 1:
                    link(ins)

            def square_sums(n):
                acc_free(dve, AQ + n // 4, n % 4)
                v_e.tensor_reduce(qs[:, 0, 8 * n:8 * n + 8], conv[:, n % 2, :].rearrange("p (h d) -> p h d", h=AH),
                                  AX_X, ALU.add).then_inc(sq_used, 1)

            def m_norms():
                dve.wait_ge(guard_ready, 1)
                link(v_e.scalar_tensor_tensor(out=gt[:, 8, :], in0=num[:, :, P], scalar=-1.0, in1=num[:, :, P],
                                              op0=ALU.mult, op1=ALU.max))
                link(v_e.tensor_tensor(gt[:, 8, :], gt[:, 8, :], gt[:, 9, :], ALU.max))
                link(v_e.reciprocal(gt[:, 10, :], gt[:, 8, :]))
                link(v_e.tensor_tensor(gt[:, 11, :], gt[:, 10, :], gt[:, 10, :], ALU.mult))
                link(v_e.tensor_tensor(gt[:, 11, :], gt[:, 11, :], mv2[:, :, 1], ALU.mult))
                v_e.tensor_scalar(gt[:, 8, :], gt[:, 11, :], 1e-5, None, ALU.add).then_inc(mvar_ready, 1)

            def qk_norms():
                dve.wait_ge(sq_used, 8)
                dve.wait_ge(k_evac, 4)
                v_e.tensor_scalar(qs[:, 1, :], qs[:, 0, :], 1.0 / DA, 1e-6, ALU.mult, ALU.add).then_inc(qk_ss, 1)
                dve.wait_ge(qk_ln, 1)
                refine(qs[:, 2, :], qs[:, 1, :], qs[:, 3, :])
                link(v_e.tensor_scalar(qs[:, 4, :], qs[:, 2, :], float(DA) ** -0.5, None, ALU.mult))
                for t in range(NT):
                    v = k_raw[:, t, :].rearrange("p (h d) -> p h d", h=AH)
                    v_e.tensor_tensor(v, v, qs[:, 2, 32 + 8 * t:40 + 8 * t].unsqueeze(2).to_broadcast((P, AH, DA)),
                                      ALU.mult).then_inc(k_norm, 1)

            def hb_part():
                dve.wait_ge(mln_ready, 1)
                refine(gt[:, 9, :], gt[:, 8, :], gt[:, 11, :])
                link(v_e.tensor_tensor(gt[:, 10, :], gt[:, 10, :], gt[:, 9, :], ALU.mult))
                for n in range(16):
                    last = v_e.tensor_scalar(num[:, n, 0:P], num[:, n, 0:P], mv2[:, n, 0:1], gt[:, 10, n:n + 1],
                                             ALU.subtract, ALU.mult)
                last.then_inc(hb_ready, 1)

            def kt_out(p):
                dve.wait_ge(kt_psum, p + 1)
                v_e.tensor_scalar(kt[:, p, :], work[p % 2][:, :], col("k_g", 0), None, ALU.mult).then_inc(kt_ready, 1)

            def yb_out(h):
                dve.wait_ge(hbt_psum, h + 1)
                if h == 0:
                    dve.wait_ge(skip_done, 1)
                v_e.scalar_tensor_tensor(out=xc[:, h, :], in0=work[3][:, :], scalar=col("out_g", h), in1=xc[:, h, :],
                                         op0=ALU.mult, op1=ALU.add).then_inc(yb_part, 1)
                dve.wait_ge(yb_part, h + 1)
                acc_free(dve, BZ, 3)
                v_e.tensor_tensor(act[:, 4 + h, :], act[:, 4 + h, :], xc[:, h, :], ALU.mult).then_inc(y_exact, 1)

            def attention(u):
                if u < NU:
                    h, i, e = UNITS[u]
                    n = P * (i + 1)
                    q = 8 * i + h
                    dve.wait_ge(s_psum, u + 1)
                    link(v_e.reduce_max(mx[:, 0, u:u + 1], work[u % 2][:, 0:n], AX_X))
                    v_e.scalar_tensor_tensor(out=mx[:, 1, u:u + 1], in0=mx[:, 0, u:u + 1], scalar=-1.0,
                                             in1=qs[:, 4, q:q + 1], op0=ALU.mult, op1=ALU.mult).then_inc(bias_ready, 1)
                v = u - 1
                if 0 <= v < NU:
                    n = P * (UNITS[v][1] + 1)
                    dve.wait_ge(exp_ready, v + 1)
                    link(v_e.reciprocal(rs[:, 1, v:v + 1], rs[:, 0, v:v + 1]))
                    v_e.tensor_scalar(probs[:, v % 3, 0:n], probs[:, v % 3, 0:n], rs[:, 1, v:v + 1], None,
                                      ALU.mult).then_inc(p_ready, 1)
                v = u - LAG
                if v >= 8 and v % 8 == 0:
                    ya_out(v // 8 - 1)
                if 0 <= v < NU and not PT_ON_ACT(v):
                    h, i, e = UNITS[v]
                    dve.wait_ge(pt_psum, v + 1)
                    v_e.tensor_copy(probs_t[:, e, 0:i + 1, P * i:P * i + P],
                                    work[2][:, 0:P * (i + 1)].rearrange("p (j q) -> p j q",
                                                                        j=i + 1)).then_inc(pt_dve, 1)
                if u in YA_SPLIT:
                    y_lo_part(4 + YA_SPLIT[u])

            def ya_out(p):
                dve.wait_ge(o_psum, p + 1)
                if p < O_FIRST:
                    v_e.tensor_copy(act[:, p, :], work[3][:, :]).then_inc(o_evac, 1)
                else:
                    acc_free(dve, AZ, p)
                    v_e.tensor_tensor(act[:, p, :], work[3][:, :], act[:, p, :], ALU.mult).then_inc(o_evac, 1)

            def az_add(p):
                dve.wait_ge(az_exp, p + 1)
                e = wts[:, 512 * (p % 2):512 * (p % 2) + 512]
                v_e.tensor_scalar(e, e, 3e38, 1.0, ALU.min, ALU.add).then_inc(az_den, 1)

            def az_out(p):
                dve.wait_ge(az_rec, p + 1)
                e = wts[:, 512 * (p % 2):512 * (p % 2) + 512]
                if p < O_FIRST:
                    dve.wait_ge(o_evac, p + 1)
                    link(v_e.tensor_tensor(act[:, p, :], act[:, p, :], e, ALU.mult))
                    e = act[:, p, :]
                v_e.tensor_tensor(act[:, p, :], acc[p][:, :], e, ALU.mult).then_inc(acc_freed_dve, 1)

            def y_lo_part(n):
                k = Y_ORDER[n]
                dve.wait_ge(y_hi, n + 1)
                minus(act_lo[:, k, :], act[:, k, :], act_hi[:, k, :]).then_inc(y_ready, 1)

            def residual(w, g, done):
                cc = CHUNKS[HALVES[w][0]][2]
                dve.wait_ge(acc_ready, 4 * (w // 2) + g + 1)
                v_e.tensor_tensor(tmp[:, g, :], acc[g][:, :], gate_bc[:, CH * cc:CH * cc + CH],
                                  ALU.mult).then_inc(acc_freed_dve, 1)
                dve.wait_ge(acc_freed_dve, 4 * sum(n < HALVES[w][0] for n in DVE_CHUNKS) + g + 1)
                if w == 13:
                    dve.wait_ge(x_in[g], 32)
                ins = v_e.tensor_tensor(xres[:, g, CH * cc:CH * cc + CH], xres[:, g, CH * cc:CH * cc + CH],
                                        tmp[:, g, :], ALU.add)
                if done is not None:
                    ins.then_inc(done, 1)

            def x1_norm(t):
                c4 = slice(4 + t, 5 + t)
                dve.wait_ge(ss1_ready, t + 1)
                v_e.tensor_scalar(rms[:, 1, c4], rms[:, 0, c4], 1.0 / D, 1e-6, ALU.mult,
                                  ALU.add).then_inc(var1_ready, 1)
                dve.wait_ge(ln1_ready, t + 1)
                refine(rms[:, 2, c4], rms[:, 1, c4], rms[:, 3, c4])
                if t >= 2:
                    dve.wait_ge(h1_psum, t - 1)
                v_e.tensor_scalar(xn[:, t % 2, :], xres[:, t, :], rms[:, 2, c4], None, ALU.mult).then_inc(xn1_ready, 1)

            def h1_part(t):
                dve.wait_ge(h1_psum, t + 1)
                dve.wait_ge(mod_ready, 8)
                for k in range(KH):
                    v_e.tensor_scalar(act[:, k, P * t:P * t + P], work[k // 4][:, P * (k % 4):P * (k % 4) + P],
                                      gain[:, 1, k:k + 1], mod[:, 1, k:k + 1], ALU.mult, ALU.add).then_inc(h1_exact, 1)

            def h1_lo_part(t):
                dve.wait_ge(h1_hi, t + 1)
                cs = slice(P * t, P * t + P)
                minus(act_lo[:, :, cs], act[:, :, cs], act_hi[:, :, cs]).then_inc(h1_ready, 1)

            def cv_stats(w, g):
                cc = (w - 17) // 2
                acc_free(dve, CV + cc, g)
                ins = v_e.bn_stats(st6[:, 2 * g + cc, :], vg[:, g, CH * cc:CH * cc + CH])
                if cc:
                    link(ins)
                    ins = v_e.bn_aggr(mv2[:, g, :], st6[:, 2 * g:2 * g + 2, :].rearrange("p a b -> p (a b)"))
                    link(ins)

            def cv_norm():
                v_e.tensor_scalar(rms[:, 1, 0:4], mv2[:, 0:4, 1], 1e-5, None, ALU.add).then_inc(cvar_ready, 1)
                dve.wait_ge(cln_ready, 1)
                refine(rms[:, 2, 0:4], rms[:, 1, 0:4], rms[:, 3, 0:4])
                for t in range(NT):
                    v_e.tensor_scalar(vg[:, t, :], vg[:, t, :], mv2[:, t, 0:1], rms[:, 2, t:t + 1], ALU.subtract,
                                      ALU.mult).then_inc(vn_ready, 1)

            def spatial_out(g):
                dve.wait_ge(sg_psum, g + 1)
                t3 = probs[:, g % 3, :].rearrange("p (t q) -> p t q", t=NT)
                link(v_e.scalar_tensor_tensor(out=t3, in0=work[g % 3][:, :].rearrange("p (t q) -> p t q", t=NT),
                                              scalar=col("c_ln_g", g),
                                              in1=sg_add[:, g:g + 1, :].to_broadcast((P, NT, P)), op0=ALU.mult,
                                              op1=ALU.add))
                acc_free(dve, CU + g // 4, g % 4)
                v_e.tensor_tensor(act[:, g, :], act[:, g, :], probs[:, g % 3, :], ALU.mult).then_inc(us_ready, 1)

            def z_out(n):
                acc_free(dve, CZ + n // 4, n % 4)
                dve.wait_ge(us_ready, n + 1)
                v_e.tensor_tensor(act[:, n, :], act[:, n, :], tmp[:, n % 4, :], ALU.mult).then_inc(z1_exact, 1)

            def z1_lo_part(k):
                dve.wait_ge(z1_hi, k + 1)
                minus(act_lo[:, k, :], act[:, k, :], act_hi[:, k, :]).then_inc(z1_ready, 1)

            def small_jobs(here):
                if here == PLACES["ln_b sums"]:
                    sg_out()
                if here == PLACES["wv transposes"]:
                    wvt_out()
                if here == PLACES["gate fold"]:
                    eff_out()
                for g in range(4):
                    for j in range(4):
                        if here == (1, g):
                            conv_tap(j, g)
                    if here == (5, g):
                        square_sums(g)
                    if here == (7, g):
                        square_sums(4 + g)
                    if here == (13, g):
                        residual(13, g, None)
                    if here == (17, g):
                        cv_stats(17, g)
                    if here == (19, g):
                        cv_stats(19, g)
                    if here == (25, g):
                        z_out(g)
                    if here == (27, g):
                        z_out(4 + g)
                    if here == (29, g):
                        residual(29, g, out_ready)
                    if here == (31, g):
                        residual(31, g, out_ready)
                for p, slot in enumerate(PLACES["mLSTM outputs"]):
                    if here == slot:
                        yb_out(p)
                for g in range(8):
                    if here == PLACES["spatial"][g]:
                        spatial_out(g)
                if here == PLACES["skip"]:
                    skip_part()
                if here == PLACES["gate columns"]:
                    gates_add()
                if here == PLACES["gate logs"]:
                    log_forget()
                if here == PLACES["running sums"]:
                    a_cols()
                if here == PLACES["running max"]:
                    running_max()
                if here == PLACES["max columns"]:
                    m_exponent()
                for h in range(MH):
                    s0 = HEAD_SLOT + 3 * h
                    if here == (s0 // 4, s0 % 4):
                        weights(h, 0)
                    if here == ((s0 + 1) // 4, (s0 + 1) % 4):
                        weights(h, 1)
                    if here == ((s0 + 2) // 4, (s0 + 2) % 4):
                        head_stats(h)
                if here == PLACES["q, k norms"]:
                    qk_norms()
                if here == PLACES["mLSTM norms"]:
                    m_norms()
                for p in range(4):
                    if here == PLACES["q, k transposes"][4 + p]:
                        kt_out(p)
                if here == PLACES["mLSTM normalised"]:
                    hb_part()
                for g in range(4):
                    if here == (11, g):
                        az_add(g)
                for u in ATT_SLOTS.get(here, ()):
                    attention(u)
                for g in range(4):
                    if here == (11, g):
                        az_out(g)
                for n in range(4 + O_FIRST):
                    if here == ((11, n // 2) if n < 4 else (11, 3)):
                        y_lo_part(n)
                if here in [(15, t) for t in range(NT)]:
                    t = here[1]
                    residual(15, t, x1_ready)
                    if t:
                        h1_part(t - 1)
                    x1_norm(t)
                    if t:
                        h1_lo_part(t - 1)
                if here == (15, 3):
                    h1_part(3)
                    h1_lo_part(3)
                    split_lo(L1 + 1)
                if here == (20, 0):
                    cv_norm()
                for n in range(4, 12):
                    if here == ADA_USE_SLOT[n]:
                        mod_out(n) if n in MOD_ITEMS else gate_out(n)
                for k in range(KT):
                    if here == ((27, -1) if k < KH else (27, 3)):
                        z1_lo_part(k)

            for w in range(NHALF):
                for g in range(-1, 4):
                    if g == -1 and w + 1 < NHALF and w != L1:
                        split_lo(w + 1)
                    small_jobs((w, g))


_INS = ["x", "c", "ln_g", "ada_w", "ada_b", "w_in", "w_out", "a_q_g", "a_k_g", "b_conv_w", "b_conv_b", "b_wq", "b_wk",
        "b_wv", "b_w_gates", "b_b_gates", "b_out_g", "b_skip", "c_ln_g", "c_ln_b", "c_ws", "c_bs"]


def kernel(**inputs):
    import numpy as _np
    import concourse.bacc as _bacc
    from concourse import mybir as _mybir
    from concourse.bass_utils import run_bass_kernel_spmd as _run

    nc = _bacc.Bacc("TRN2", target_bir_lowering=False, num_devices=1)
    arrays, args = {}, []
    for name in _INS:
        a = _np.ascontiguousarray(inputs[name])
        arrays[f"in_{name}_dram"] = a
        args.append(nc.dram_tensor(f"in_{name}_dram", a.shape, _mybir.dt.from_np(a.dtype), kind="ExternalInput").ap())
    args.append(nc.dram_tensor("out_0_dram", (1, T, D), _mybir.dt.float32, kind="ExternalOutput").ap())
    build(nc, *args)
    r = _run(nc, [arrays], core_ids=[0])
    return r.results[0]["out_0_dram"]
```
